# Optimizing a Trainium2 kernel written in Bass

```python
import math
import jax, jax.numpy as jnp
from jax import lax
import numpy as np

D_MODEL = 1024
BATCH = 1
SEQ = 512
DEPTH = 1

MEM_LEN = 256
CONV_W = 512
CONV_WIDTH = 3
ATT_HEADS = 8
ATT_DH = 64
ATT_W = ATT_HEADS * ATT_DH
MOBA_BLOCK = 256
MOBA_TOPK = 3
Q_CHUNK = 16
MEM_HEADS = 4
MEM_DH = 128
MEM_W = MEM_HEADS * MEM_DH
NUM_BUCKETS = 32
MAX_EXACT = NUM_BUCKETS // 2
MAX_DISTANCE = 1024
D_FF = 2816
FFN_CONV_WIDTH = 3
N_BRANCHES = 3
RMS_EPS = 1e-6
NEG = -1e30

IN_SPLITS = [CONV_W, CONV_W, CONV_W, ATT_W, ATT_W, ATT_W, MEM_W, D_MODEL, D_MODEL, D_MODEL]
IN_COLS = sum(IN_SPLITS)
IN_OFFSETS = list(np.cumsum(IN_SPLITS)[:-1])


def rmsnorm(x, g):
    x32 = x.astype(jnp.float32)
    y = x32 * lax.rsqrt(jnp.mean(x32 * x32, axis=-1, keepdims=True) + RMS_EPS)
    return (y * g.astype(jnp.float32)).astype(x.dtype)

def causal_dwconv(u, w, b=None):
    width, c = w.shape
    y = lax.conv_general_dilated(
        u, w.astype(u.dtype)[:, None, :], window_strides=(1,), padding=[(width - 1, 0)],
        dimension_numbers=("NWC", "WIO", "NWC"), feature_group_count=c)
    if b is not None:
        y = y + b.astype(u.dtype)
    return y

def rel_bucket(dist):
    n = jnp.maximum(dist, 0)
    is_small = n < MAX_EXACT
    n_f = jnp.maximum(n, MAX_EXACT).astype(jnp.float32)
    large = MAX_EXACT + (jnp.log(n_f / MAX_EXACT) / math.log(MAX_DISTANCE / MAX_EXACT)
                         * (NUM_BUCKETS - MAX_EXACT)).astype(jnp.int32)
    large = jnp.minimum(large, NUM_BUCKETS - 1)
    return jnp.where(is_small, n, large)

def moba_attention(q, k, v, rel_bias):
    b_, h_, s_, dh = q.shape
    nb = -(-s_ // MOBA_BLOCK)
    pad = nb * MOBA_BLOCK - s_
    k_pad = jnp.pad(k, ((0, 0), (0, 0), (0, pad), (0, 0)))
    v_pad = jnp.pad(v, ((0, 0), (0, 0), (0, pad), (0, 0)))
    kb = k_pad.reshape(b_, h_, nb, MOBA_BLOCK, dh)
    vb = v_pad.reshape(b_, h_, nb, MOBA_BLOCK, dh)
    scale = dh ** -0.5

    k_mean = jnp.mean(kb.astype(jnp.float32), axis=3)
    gate = jnp.einsum("bhsd,bhnd->bhsn", q.astype(jnp.float32), k_mean)
    q_blk = jnp.arange(s_) // MOBA_BLOCK
    past = jnp.arange(nb)[None, :] < q_blk[:, None]
    gate = jnp.where(past, gate, NEG)
    k_sel = max(1, min(MOBA_TOPK, nb - 1))
    _, sel = lax.top_k(gate, k_sel)

    bias_hb = rel_bias.astype(jnp.float32).T
    b_idx = jnp.arange(b_)[:, None, None, None]
    h_idx = jnp.arange(h_)[None, :, None, None]
    blk_off = jnp.arange(MOBA_BLOCK)

    def chunk(c):
        start = c * Q_CHUNK
        qc = lax.dynamic_slice_in_dim(q, start, Q_CHUNK, axis=2)
        selc = lax.dynamic_slice_in_dim(sel, start, Q_CHUNK, axis=2)
        t = start + jnp.arange(Q_CHUNK)
        valid = jnp.arange(k_sel)[None, :] < (t // MOBA_BLOCK)[:, None]
        kg = kb[b_idx, h_idx, selc]
        vg = vb[b_idx, h_idx, selc]
        s_sel = jnp.einsum("bhqd,bhqjkd->bhqjk", qc, kg).astype(jnp.float32) * scale
        k_pos = selc[..., None] * MOBA_BLOCK + blk_off
        bucket = rel_bucket(t[None, None, :, None, None] - k_pos)
        bias = bias_hb[h_idx[..., None], bucket]
        s_sel = jnp.where(valid[None, None, :, :, None], s_sel + bias, NEG)
        own = start // MOBA_BLOCK
        ko = lax.dynamic_slice_in_dim(k_pad, own * MOBA_BLOCK, MOBA_BLOCK, axis=2)
        vo = lax.dynamic_slice_in_dim(v_pad, own * MOBA_BLOCK, MOBA_BLOCK, axis=2)
        s_own = jnp.einsum("bhqd,bhkd->bhqk", qc, ko).astype(jnp.float32) * scale
        dist = t[:, None] - (own * MOBA_BLOCK + blk_off)[None, :]
        bias_own = bias_hb[:, rel_bucket(dist)]
        s_own = jnp.where(dist[None, None] >= 0, s_own + bias_own[None], NEG)
        logits = jnp.concatenate([s_sel.reshape(b_, h_, Q_CHUNK, k_sel * MOBA_BLOCK), s_own], axis=-1)
        p = jax.nn.softmax(logits, axis=-1).astype(v.dtype)
        p_sel = p[..., : k_sel * MOBA_BLOCK].reshape(b_, h_, Q_CHUNK, k_sel, MOBA_BLOCK)
        p_own = p[..., k_sel * MOBA_BLOCK:]
        return (jnp.einsum("bhqjk,bhqjkd->bhqd", p_sel, vg)
                + jnp.einsum("bhqk,bhkd->bhqd", p_own, vo))

    out = lax.map(chunk, jnp.arange(s_ // Q_CHUNK))
    return jnp.transpose(out, (1, 2, 0, 3, 4)).reshape(b_, h_, s_, dh)

def memory_attention(qm, mem_n, w_mem_kv):
    b_, s_, _ = qm.shape
    kv = mem_n @ w_mem_kv
    mk, mv = jnp.split(kv, 2, axis=-1)
    mk = mk.reshape(b_, -1, MEM_HEADS, MEM_DH)
    mv = mv.reshape(b_, -1, MEM_HEADS, MEM_DH)
    q4 = qm.reshape(b_, s_, MEM_HEADS, MEM_DH)
    s = jnp.einsum("bshd,bmhd->bhsm", q4, mk).astype(jnp.float32) * (MEM_DH ** -0.5)
    p = jax.nn.softmax(s, axis=-1).astype(qm.dtype)
    return jnp.einsum("bhsm,bmhd->bshd", p, mv).reshape(b_, s_, MEM_W)

def first_inputs(seed: int = 0) -> dict:
    key = jax.random.key(seed)
    ks = jax.random.split(key, 20)

    def nrm(k, shape, scale):
        return jax.random.normal(k, shape, jnp.float32) * scale

    def gain(k):
        return 1.0 + nrm(k, (DEPTH, D_MODEL), 0.05)

    return {
        "x": nrm(ks[0], (BATCH, SEQ, D_MODEL), 1.0),
        "mem": nrm(ks[1], (BATCH, MEM_LEN, D_MODEL), 1.0),
        "rel_bias": nrm(ks[2], (NUM_BUCKETS, ATT_HEADS), 0.5),
        "g_pre_mix": gain(ks[3]),
        "g_post_mix": gain(ks[4]),
        "g_pre_ffn": gain(ks[5]),
        "g_post_ffn": gain(ks[6]),
        "g_mem": gain(ks[7]),
        "w_in": nrm(ks[8], (DEPTH, D_MODEL, IN_COLS), D_MODEL ** -0.5),
        "b_gate": nrm(ks[9], (DEPTH, N_BRANCHES * D_MODEL), 0.01),
        "conv_mix_w": nrm(ks[10], (DEPTH, CONV_WIDTH, CONV_W), CONV_WIDTH ** -0.5),
        "w_conv_out": nrm(ks[11], (DEPTH, CONV_W, D_MODEL), CONV_W ** -0.5),
        "w_attn_out": nrm(ks[12], (DEPTH, ATT_W, D_MODEL), ATT_W ** -0.5),
        "w_mem_kv": nrm(ks[13], (DEPTH, D_MODEL, 2 * MEM_W), D_MODEL ** -0.5),
        "w_mem_out": nrm(ks[14], (DEPTH, MEM_W, D_MODEL), MEM_W ** -0.5),
        "w_out": nrm(ks[15], (DEPTH, D_MODEL, D_MODEL), D_MODEL ** -0.5),
        "w_up": nrm(ks[16], (DEPTH, D_MODEL, 2 * D_FF), D_MODEL ** -0.5),
        "ffn_conv_w": nrm(ks[17], (DEPTH, FFN_CONV_WIDTH, 2 * D_FF), FFN_CONV_WIDTH ** -0.5),
        "ffn_conv_b": nrm(ks[18], (DEPTH, 2 * D_FF), 0.01),
        "w_down": nrm(ks[19], (DEPTH, D_FF, D_MODEL), D_FF ** -0.5),
    }

def first_block(x, mem, rel_bias, g_pre_mix, g_post_mix, g_pre_ffn, g_post_ffn, g_mem,
              w_in, b_gate, conv_mix_w, w_conv_out, w_attn_out, w_mem_kv, w_mem_out,
              w_out, w_up, ffn_conv_w, ffn_conv_b, w_down):
    b_, s_, d_ = x.shape
    for l in range(DEPTH):
        h = rmsnorm(x, g_pre_mix[l])
        proj = h @ w_in[l]
        (cb, cc, cv, q, k, v, qm, ga, gb, gc) = jnp.split(proj, IN_OFFSETS, axis=-1)
        y_a = (cb * causal_dwconv(cc * cv, conv_mix_w[l])) @ w_conv_out[l]
        to_heads = lambda t: jnp.transpose(t.reshape(b_, s_, ATT_HEADS, ATT_DH), (0, 2, 1, 3))
        o = moba_attention(to_heads(q), to_heads(k), to_heads(v), rel_bias)
        y_b = jnp.transpose(o, (0, 2, 1, 3)).reshape(b_, s_, ATT_W) @ w_attn_out[l]
        y_c = memory_attention(qm, rmsnorm(mem, g_mem[l]), w_mem_kv[l]) @ w_mem_out[l]
        bg = b_gate[l].reshape(N_BRANCHES, d_)
        merged = (jax.nn.sigmoid(ga + bg[0]) * y_a + jax.nn.sigmoid(gb + bg[1]) * y_b
                  + jax.nn.sigmoid(gc + bg[2]) * y_c)
        x = x + rmsnorm(merged @ w_out[l], g_post_mix[l])
        h = rmsnorm(x, g_pre_ffn[l])
        u = causal_dwconv(h @ w_up[l], ffn_conv_w[l], ffn_conv_b[l])
        a, g = jnp.split(u, 2, axis=-1)
        f = (jax.nn.gelu(a) * g) @ w_down[l]
        x = x + rmsnorm(f, g_post_ffn[l])
    return x


HG_HEADS = 4
HG_DK = 128
HG_DV = 128
HG_WIDTH = HG_HEADS * HG_DV
SA_HEADS = 4
SA_DH = 64
SA_WIDTH = SA_HEADS * SA_DH
MEM_DH_2 = 64
MEM_WIDTH = MEM_HEADS * MEM_DH_2
MIX_WIDTH = HG_WIDTH + SA_WIDTH + MEM_WIDTH
IDX_HEADS = 8
IDX_DH = 64
TOPK_MAX = 256
N_MEM = 256
D_FF_2 = -(-8 * D_MODEL // (3 * 256)) * 256
CHUNK = 64
Q_BLOCK = 128
EPS = 1e-6
IN_SIZES = (HG_HEADS * HG_DK, HG_HEADS * HG_DK, HG_WIDTH, HG_WIDTH,
            SA_WIDTH, SA_WIDTH, SA_WIDTH,
            IDX_HEADS * IDX_DH, IDX_DH, IDX_HEADS,
            MEM_WIDTH)
IN_WIDTH = sum(IN_SIZES)


f32 = jnp.float32

def rmsnorm_2(x, gain):
    x32 = x.astype(f32)
    y = x32 * lax.rsqrt(jnp.mean(x32 * x32, axis=-1, keepdims=True) + EPS)
    return (y * gain.astype(f32)).astype(x.dtype)

def split_in(p):
    offs, acc = [], 0
    for s in IN_SIZES[:-1]:
        acc += s
        offs.append(acc)
    return jnp.split(p, offs, axis=-1)

def to_chunks(a, B, N):
    return a.reshape(B, N, CHUNK, a.shape[2], a.shape[3]).transpose(1, 0, 3, 2, 4)

def hgrn2_mix(q, f_logit, i, g, lb, out_gain):
    B, L = q.shape[:2]
    N = L // CHUNK
    lb = lb.reshape(HG_HEADS, HG_DK)
    z = f_logit.astype(f32)
    log_f = jnp.logaddexp(jnp.log(lb), jnp.log1p(-lb) + jax.nn.log_sigmoid(z))
    k = (1.0 - lb) * jax.nn.sigmoid(-z)
    qf = jax.nn.silu(q.astype(f32))
    xs = (to_chunks(qf, B, N), to_chunks(k, B, N),
          to_chunks(i.astype(f32), B, N), to_chunks(log_f, B, N))
    causal = jnp.tril(jnp.ones((CHUNK, CHUNK), dtype=bool))

    def step(S, inp):
        qc, kc, vc, gc = inp
        b = jnp.cumsum(gc, axis=2)
        o_inter = jnp.einsum('bhck,bhkv->bhcv', qc * jnp.exp(b), S)
        diff = b[:, :, :, None, :] - b[:, :, None, :, :]
        decay = jnp.exp(jnp.where(causal[:, :, None], diff, -jnp.inf))
        A = jnp.einsum('bhtk,bhtsk,bhsk->bhts', qc, decay, kc)
        o = o_inter + jnp.einsum('bhts,bhsv->bhtv', A, vc)
        b_last = b[:, :, -1:, :]
        S = jnp.exp(b_last[:, :, 0, :])[..., None] * S + \
            jnp.einsum('bhck,bhcv->bhkv', kc * jnp.exp(b_last - b), vc)
        return S, o

    S0 = jnp.zeros((B, HG_HEADS, HG_DK, HG_DV), f32)
    _, o = lax.scan(step, S0, xs)
    o = o.transpose(1, 0, 3, 2, 4).reshape(B, L, HG_HEADS, HG_DV)
    o = rmsnorm_2(o, out_gain) * jax.nn.silu(g.astype(f32))
    return o.reshape(B, L, HG_WIDTH).astype(q.dtype)

def dsa_mix(q, k, v, iq, ik, iw, q_gain, k_gain):
    B, L = q.shape[:2]
    topk = min(TOPK_MAX, L // 4)
    nb = L // Q_BLOCK
    q = rmsnorm_2(q, q_gain).astype(f32)
    k = rmsnorm_2(k, k_gain).astype(f32)
    v32 = v.astype(f32)
    ik32 = ik.astype(f32)
    iw32 = iw.astype(f32) * (IDX_HEADS ** -0.5 * IDX_DH ** -0.5)
    key_pos = jnp.arange(L)
    bidx = jnp.arange(B)[:, None, None]

    def blockify(a):
        return a.reshape(B, nb, Q_BLOCK, *a.shape[2:]).swapaxes(0, 1)

    def one_block(args):
        blk, qb, iqb, iwb = args
        qpos = blk * Q_BLOCK + jnp.arange(Q_BLOCK)
        s = jnp.einsum('bqhd,bsd->bqhs', iqb.astype(f32), ik32)
        score = jnp.einsum('bqh,bqhs->bqs', iwb, jax.nn.relu(s))
        visible = key_pos[None, :] <= qpos[:, None]
        score = jnp.where(visible[None], score, -jnp.inf)
        _, idx = lax.top_k(score, topk)
        valid = idx <= qpos[None, :, None]
        kg = k[bidx, idx]
        vg = v32[bidx, idx]
        logits = jnp.einsum('bqhd,bqkhd->bhqk', qb, kg) * (SA_DH ** -0.5)
        logits = jnp.where(valid[:, None], logits, -jnp.inf)
        p = jax.nn.softmax(logits, axis=-1)
        return jnp.einsum('bhqk,bqkhd->bqhd', p, vg)

    out = lax.map(one_block, (jnp.arange(nb), blockify(q), blockify(iq), blockify(iw32)))
    return out.swapaxes(0, 1).reshape(B, L, SA_WIDTH).astype(v.dtype)

def mem_mix(qm, mem_n, w_kv, q_gain, k_gain):
    B, L = qm.shape[:2]
    km, vm = jnp.split(mem_n @ w_kv, 2, axis=-1)
    M = mem_n.shape[1]
    km = km.reshape(B, M, MEM_HEADS, MEM_DH_2)
    vm = vm.reshape(B, M, MEM_HEADS, MEM_DH_2)
    qm = rmsnorm_2(qm, q_gain).astype(f32)
    km = rmsnorm_2(km, k_gain).astype(f32)
    logits = jnp.einsum('bqhd,bmhd->bhqm', qm, km) * (MEM_DH_2 ** -0.5)
    p = jax.nn.softmax(logits, axis=-1)
    out = jnp.einsum('bhqm,bmhd->bqhd', p, vm.astype(f32))
    return out.reshape(B, L, MEM_WIDTH).astype(mem_n.dtype)

def second_inputs(seed: int = 0) -> dict:
    key = jax.random.key(seed)
    ks = jax.random.split(key, 16)
    nrm = jax.random.normal

    def gain(k, n):
        return 1.0 + 0.02 * nrm(k, (DEPTH, n), f32)

    return {
        "x": nrm(ks[0], (BATCH, SEQ, D_MODEL), f32),
        "mem": nrm(ks[1], (BATCH, N_MEM, D_MODEL), f32),
        "w_in": nrm(ks[2], (DEPTH, D_MODEL, IN_WIDTH), f32) * D_MODEL ** -0.5,
        "w_out": nrm(ks[3], (DEPTH, MIX_WIDTH, D_MODEL), f32) * MIX_WIDTH ** -0.5,
        "w_mem_kv": nrm(ks[4], (DEPTH, D_MODEL, 2 * MEM_WIDTH), f32) * D_MODEL ** -0.5,
        "lb_logits": nrm(ks[5], (DEPTH, HG_HEADS * HG_DK), f32),
        "norm_mix": gain(ks[6], D_MODEL),
        "norm_mem": gain(ks[7], D_MODEL),
        "norm_ffn": gain(ks[8], D_MODEL),
        "hg_out_gain": gain(ks[9], HG_DV),
        "sa_q_gain": gain(ks[10], SA_DH),
        "sa_k_gain": gain(ks[11], SA_DH),
        "mem_q_gain": gain(ks[12], MEM_DH_2),
        "mem_k_gain": gain(ks[13], MEM_DH_2),
        "w_ffn_in": nrm(ks[14], (DEPTH, D_MODEL, 2 * D_FF_2), f32) * D_MODEL ** -0.5,
        "w_ffn_out": nrm(ks[15], (DEPTH, D_FF_2, D_MODEL), f32) * D_FF_2 ** -0.5,
    }

def second_block(x, mem, w_in, w_out, w_mem_kv, lb_logits, norm_mix, norm_mem, norm_ffn,
              hg_out_gain, sa_q_gain, sa_k_gain, mem_q_gain, mem_k_gain,
              w_ffn_in, w_ffn_out):
    B, L, _ = x.shape
    lb = jnp.cumsum(jax.nn.softmax(lb_logits.astype(f32), axis=0), axis=0)
    lb = lb - lb[0:1]
    for layer in range(DEPTH):
        h = rmsnorm_2(x, norm_mix[layer])
        hq, hf, hi, hg, sq, sk, sv, iq, ik, iw, mq = split_in(h @ w_in[layer])
        o_hg = hgrn2_mix(hq.reshape(B, L, HG_HEADS, HG_DK), hf.reshape(B, L, HG_HEADS, HG_DK),
                         hi.reshape(B, L, HG_HEADS, HG_DV), hg.reshape(B, L, HG_HEADS, HG_DV),
                         lb[layer], hg_out_gain[layer])
        o_sa = dsa_mix(sq.reshape(B, L, SA_HEADS, SA_DH), sk.reshape(B, L, SA_HEADS, SA_DH),
                       sv.reshape(B, L, SA_HEADS, SA_DH), iq.reshape(B, L, IDX_HEADS, IDX_DH),
                       ik, iw, sa_q_gain[layer], sa_k_gain[layer])
        mem_n = rmsnorm_2(mem, norm_mem[layer])
        o_mem = mem_mix(mq.reshape(B, L, MEM_HEADS, MEM_DH_2), mem_n, w_mem_kv[layer],
                        mem_q_gain[layer], mem_k_gain[layer])
        mixed = jnp.concatenate([o_hg, o_sa, o_mem], axis=-1)
        x = x + (mixed @ w_out[layer]).astype(x.dtype)
        h = rmsnorm_2(x, norm_ffn[layer])
        a, b = jnp.split(h @ w_ffn_in[layer], 2, axis=-1)
        x = x + ((jax.nn.silu(a) * b) @ w_ffn_out[layer]).astype(x.dtype)
    return x


def setup_inputs(seed=0):
    out = dict(first_inputs(seed))
    for name, value in second_inputs(seed + 1).items():
        if name != "x":
            out[name + "_2"] = value
    return out


def reference(
    x, mem, rel_bias, g_pre_mix, g_post_mix, g_pre_ffn, g_post_ffn, g_mem, w_in, b_gate,
    conv_mix_w, w_conv_out, w_attn_out, w_mem_kv, w_mem_out, w_out, w_up, ffn_conv_w,
    ffn_conv_b, w_down, mem_2, w_in_2, w_out_2, w_mem_kv_2, lb_logits_2, norm_mix_2, norm_mem_2,
    norm_ffn_2, hg_out_gain_2, sa_q_gain_2, sa_k_gain_2, mem_q_gain_2, mem_k_gain_2, w_ffn_in_2,
    w_ffn_out_2,
):
    x = first_block(
        x, mem, rel_bias, g_pre_mix, g_post_mix, g_pre_ffn, g_post_ffn, g_mem, w_in, b_gate,
        conv_mix_w, w_conv_out, w_attn_out, w_mem_kv, w_mem_out, w_out, w_up, ffn_conv_w,
        ffn_conv_b, w_down,
    )
    return second_block(
        x, mem_2, w_in_2, w_out_2, w_mem_kv_2, lb_logits_2, norm_mix_2, norm_mem_2, norm_ffn_2,
        hg_out_gain_2, sa_q_gain_2, sa_k_gain_2, mem_q_gain_2, mem_k_gain_2, w_ffn_in_2,
        w_ffn_out_2,
    )


_drawn_inputs = setup_inputs


def setup_inputs(seed=0):
    import zlib

    import numpy as np

    out = dict(_drawn_inputs(seed))
    spreads = {}
    factors = {'g_mem': 7.573,
     'b_gate': 8.0,
     'ffn_conv_b': 5.857,
     'norm_mix_2': 6.531,
     'norm_mem_2': 41.967,
     'norm_ffn_2': 16.492,
     'hg_out_gain_2': 21.643,
     'sa_q_gain_2': 141.559,
     'sa_k_gain_2': 97.483,
     'mem_q_gain_2': 37.76,
     'mem_k_gain_2': 46.289}
    for name, (base, spread) in spreads.items():
        noise = np.random.default_rng([zlib.crc32(name.encode()), seed]).standard_normal(out[name].shape)
        drawn = base * np.exp(spread * noise) if base else spread * noise
        out[name] = __import__('jax').numpy.asarray(drawn.astype(out[name].dtype))
    for name, factor in factors.items():
        out[name] = (out[name] * factor).astype(out[name].dtype)
    return out
```

```python
import math
from contextlib import ExitStack

import numpy as np

import concourse.bass as bass
from concourse import mybir

F32 = mybir.dt.float32
F32R = mybir.dt.float32r
U8 = mybir.dt.uint8
ACT = mybir.ActivationFunctionType
ALU = mybir.AluOpType
AX = mybir.AxisListType

P = 128
D = 1024
KT = D // P
S = 512
TT = S // P
M = 256
MT = M // P
SLOT = 2048
COLS = SLOT // KT
DFF = 2816
FT = DFF // P
HEADS, DH = 8, 64
MHEADS, MDH = 4, 128
NB, NB_EXACT, NB_DIST = 32, 16, 1024
HG, HDK = 4, 128
SAH = 4
IDXH = 8
TOPK = min(256, S // 4)
NEG = -1e30
TAKEN = -3e38
EPS = 1e-6
LEVELS = 7

VEC = {}
_at = 0
for _name, _n in [("g_pre_mix", 8), ("g_post_mix", 8), ("g_pre_ffn", 8), ("g_post_ffn", 8), ("g_mem", 8),
                  ("norm_mix_2", 8), ("norm_mem_2", 8), ("norm_ffn_2", 8), ("b_gate", 24),
                  ("conv_mix_w", 12), ("ffn_conv_w", 132), ("ffn_conv_b", 44)]:
    VEC[_name] = _at
    _at += _n
NVEC = _at
ROW = {"sa_q_gain": 0, "sa_k_gain": 64, "mem_q_gain": 128, "mem_k_gain": 192, "hg_out_gain": 256}
NROW = 384

LOADS = [("mem_kv", 4), ("qm", 2), ("q", 2), ("k", 2), ("v", 2), ("cc", 2), ("cv", 2), ("cb", 2),
         ("branch", 18), ("w_out", 4), ("up", 22), ("down", 12), ("mem_kv_2", 2), ("iq", 2), ("idx", 1),
         ("sq", 1), ("sk", 1), ("sv", 1), ("mq", 1), ("hf", 2), ("hq", 2), ("hi", 2), ("hg", 2),
         ("w_out_2", 4), ("up_2", 22), ("down_2", 12)]
FIRST = {}
_at = 0
for _name, _n in LOADS:
    FIRST[_name] = _at
    _at += _n
NLOADS = _at

UNITS = ([("mem", h, i, M) for h in range(MHEADS) for i in range(TT)]
         + [("att", h, i, P * (i + 1)) for h in range(HEADS) for i in range(TT)]
         + [("mem_2", h, i, M) for h in range(SAH) for i in range(TT)]
         + [("sa", h, i, P * (i + 1)) for h in range(SAH) for i in range(TT)])
UNIT0 = {"mem": 0, "att": 16, "mem_2": 48, "sa": 64}
IDX = [(i, h) for i in range(1, TT) for h in range(IDXH)]
S_BANKS, T_BANKS, O_BANKS = (4, 5), (6, 0), (7, 1)
NLP = 3


LOWS = [("mem", KT), ("x", KT), ("turn_mem", 4), ("turn_att", 4), ("conv", 4), ("merged", KT), ("ffn", KT),
        ("mem_2", KT), ("x_2", KT), ("turn_mix", KT), ("ffn_2", KT)]
LOW_END = {}
_at = 0
for _name, _n in LOWS:
    _at += _n
    LOW_END[_name] = _at
NORM_SUMS = {"mem": 8, "x": 16, "mix": 24, "ffn": 32, "mem_2": 40, "down": 48, "x_2": 56, "ffn_2": 68}


class Slot:

    def __init__(self, bank, before, ready, load, per=0, ready_per=0):
        self.bank, self.before, self.ready, self.load = bank, before, ready, load
        self.per, self.ready_per = per, ready_per


def plan_banks():
    used, told = [0] * 8, [0] * 8
    slot = {}

    def use(key, bank, load=None):
        if load is None:
            told[bank] += 1
        slot[key] = Slot(bank, used[bank], told[bank] if load is None else load + 1, load)
        used[bank] += 1

    def tiles(name, n, banks=(0, 1, 2, 3), first=None, per=1):
        for t in range(n):
            last = first is not None and t % per == per - 1
            use((name, t), banks[t % len(banks)], first + t // per if last else None)

    def loop(name, banks, times, ends, loads):
        own = [b for c, b in enumerate(banks) if c not in ends]
        for c, b in enumerate(banks):
            if c in ends:
                slot[name, c] = Slot(b, used[b] + banks[:c].count(b), ends[c] + 1, ends[c], banks.count(b), loads)
            else:
                earlier = [x for e, x in enumerate(banks[:c]) if e not in ends].count(b)
                slot[name, c] = Slot(b, used[b] + banks[:c].count(b), told[b] + earlier + 1, None, banks.count(b),
                                     own.count(b))
        for b in banks:
            used[b] += times
        for b in own:
            told[b] += times

    def norm(k):
        use(("sum", k), 7)
        use(("spread", k), 6)

    def attention(kind, n):
        for w in range(UNIT0[kind], UNIT0[kind] + n):
            use(("S", w), S_BANKS[w % 2])
            use(("T", w), T_BANKS[w % 2])
            use(("O", w), O_BANKS[w % 2])

    tiles("bias", 2)
    norm("mem")
    tiles("mem_k", 4, first=0, per=2)
    norm("x")
    tiles("mem_v", 4, first=2, per=2)
    tiles("qm", 4, first=FIRST["qm"], per=2)
    attention("mem", MHEADS * TT)
    tiles("turn_mem", 4)
    tiles("q", 4, first=FIRST["q"], per=2)
    tiles("k", 4, first=FIRST["k"], per=2)
    tiles("v", 8, first=FIRST["v"], per=4)
    attention("att", HEADS * TT)
    tiles("turn_att", 4)
    tiles("cc", 4, first=FIRST["cc"], per=2)
    tiles("cv", 4, first=FIRST["cv"], per=2)
    tiles("cb", 4, first=FIRST["cb"], per=2)
    loop("branch", [0, 1, 2, 3, 4, 5, 6, 7] * 2, 3,
         {c: FIRST["branch"] + m for m, c in enumerate((1, 3, 7, 9, 11, 15))}, 6)
    tiles("w_out", KT, first=FIRST["w_out"], per=2)
    norm("mix")
    norm("ffn")
    loop("up", [0, 1, 2, 3], FT // 2, {1: FIRST["up"], 3: FIRST["up"] + 1}, 2)
    loop("down", [0, 1, 2, 3], 2, {1: FIRST["down"] + 2, 3: FIRST["down"] + 5}, 6)
    norm("mem_2")
    norm("down")
    tiles("mem_kv_2", 4, first=FIRST["mem_kv_2"], per=2)
    norm("x_2")
    tiles("turn_km", 2, (4, 5))
    tiles("iq", 4, first=FIRST["iq"], per=2)
    tiles("ik", 1)
    use(("iw", 0), 1, FIRST["idx"])
    for w in range(len(IDX)):
        use(("idx", w), 4 + w % 4)
    tiles("sq", 4, first=FIRST["sq"], per=4)
    tiles("sk", 4, first=FIRST["sk"], per=4)
    tiles("turn_sq", 2, (4, 5))
    tiles("sv", 4, first=FIRST["sv"], per=4)
    tiles("turn_sk", 2, (6, 7))
    tiles("mq", 4, first=FIRST["mq"], per=4)
    tiles("hf", 4, first=FIRST["hf"], per=2)
    tiles("turn_mq", 2, (4, 5))
    tiles("hq", 4, first=FIRST["hq"], per=2)
    tiles("hi", 8, first=FIRST["hi"], per=4)
    tiles("hg", 8, first=FIRST["hg"], per=4)
    tiles("self", HG)
    for lv in range(LEVELS):
        for h in range(HG):
            use(("level", lv, h), 4 + h)
    tiles("turn_kd", TT - 1)
    tiles("state", TT - 1, (4, 5, 6))
    tiles("o_hg", TT)
    attention("mem_2", SAH * TT)
    attention("sa", SAH * TT)
    tiles("turn_mix", KT)
    tiles("w_out_2", KT, first=FIRST["w_out_2"], per=2)
    norm("ffn_2")
    loop("up_2", [0, 1, 2, 3], FT // 2, {1: FIRST["up_2"], 3: FIRST["up_2"] + 1}, 2)
    loop("down_2", [0, 1, 2, 3], 2, {1: FIRST["down_2"] + 2, 3: FIRST["down_2"] + 5}, 6)
    return slot


class Chain:

    def __init__(self, engine, sem):
        self.engine, self.sem, self.n, self.add = engine, sem, 0, 0

    def __call__(self, ins):
        ins.then_inc(self.sem, 1)
        self.n += 1
        self.engine.wait_ge(self.sem, self.n + self.add)

    def enter(self, i, per):
        self.start, self.per, self.add = self.n, per, i * per

    def leave(self, times):
        assert self.n - self.start == self.per, (self.n - self.start, self.per)
        self.n += self.per * (times - 1)
        self.add = 0


def build(nc, A, out):
    slot = plan_banks()
    ctx = ExitStack()
    with ctx:
        base = (nc.sbuf_base + 63) // 64 * 64
        K = 1024

        def at(name, offset, shape, dt=F32):
            return nc.alloc_sbuf_tensor_at(name, [P, *shape], dt, offset=base + offset)

        x = at("x", 0, [KT, S])
        h_hi = at("h_hi", 16 * K, [KT, S], F32R)
        h_lo = at("h_lo", 32 * K, [KT, S], F32R)
        raw = [at(f"raw{s}", (48 + 8 * s) * K, [SLOT]) for s in range(2)]
        w_hi = [at(f"w_hi{s}", (64 + 8 * s) * K, [SLOT], F32R) for s in range(2)]
        w_lo = [at(f"w_lo{s}", (80 + 8 * s) * K, [SLOT], F32R) for s in range(2)]
        ssq = at("ssq", 96 * K, [S])
        square = [at(f"square{s}", (98 + 2 * s) * K, [S]) for s in range(2)]
        diag = at("diag", 102 * K, [TT, P])
        ssq_mem2 = at("ssq_mem2", 102 * K, [M])
        small = 104 * K
        vec = at("vec", small, [NVEC])
        rows = at("rows", small + 1280, [NROW])
        ident = at("ident", small + 2816, [P])
        ones = at("ones", small + 3328, [P])
        st = at("st", small + 3840, [6, 16])
        mx = at("mx", small + 4224, [8, 4])
        AR = small + 4352

        br_hi = at("br_hi", AR, [3 * 4, S], F32R)
        br_lo = at("br_lo", AR + 24 * K, [3 * 4, S], F32R)
        memT = at("memT", AR + 48 * K, [KT, M])
        mn_hi = at("mn_hi", AR + 72 * K, [KT, M], F32R)
        mn_lo = at("mn_lo", AR + 80 * K, [KT, M], F32R)
        qm = at("qm", AR + 48 * K, [4, S])
        mk = at("mk", AR + 56 * K, [4, M])
        mv = at("mv", AR + 60 * K, [MT, S])
        q = at("q", AR + 48 * K, [4, S])
        k = at("k", AR + 56 * K, [4, S])
        v = at("v", AR + 64 * K, [TT, S])
        o_tok = at("o_tok", AR + 72 * K, [TT, S])
        row = [at(f"row{s}", AR + (80 + 2 * s) * K, [S]) for s in range(NLP)]
        pT = [at(f"pT{s}", AR + (86 + 2 * s) * K, [TT, P]) for s in range(2)]
        onehot = at("onehot", AR + 8 * K, [1024])
        relb = at("relb", AR + 12 * K, [HEADS])
        bias_row = at("bias_row", AR + 16 * K, [1024])
        toep = [at(f"toep{s}", AR + 24 * K * s, [2, 896]) for s in range(2)]
        cc = at("cc", AR + 48 * K, [4, S])
        u = at("u", AR + 56 * K, [4, S])
        cy = at("cy", AR + 64 * K, [4, S])
        gate = at("gate", AR + 48 * K, [4, S])
        merged = at("merged", AR + 56 * K, [KT, S])
        part = [at(f"part{s}", AR + (88 + 2 * s) * K, [S]) for s in range(2)]
        mixed = at("mixed", AR + 72 * K, [KT, S])
        a_hi = at("a_hi", AR, [FT * S], F32R)
        a_lo = at("a_lo", AR + 44 * K, [FT * S], F32R)
        y = [at(f"y{s}", AR + (88 + 2 * s) * K, [S]) for s in range(4)]
        down = at("down", 16 * K, [KT * S])
        mem2T = at("mem2T", 32 * K, [KT, M])
        mn2_hi = at("mn2_hi", 40 * K, [KT, M], F32R)
        mn2_lo = at("mn2_lo", AR + 88 * K, [KT, M], F32R)
        mix = at("mix", AR, [TT, D])
        g_tok = at("g_tok", AR + 16 * K, [TT, S])
        abs_z = at("abs_z", AR + 16 * K, [HG * S])
        km_tok = at("km_tok", AR + 24 * K, [MT, M])
        km_sq = at("km_sq", AR + 40 * K, [MT, M])
        kmT = at("kmT", AR + 26 * K, [2, M])
        vm = at("vm", AR + 28 * K, [MT, M])
        masks = at("masks", AR + 30 * K, [LEVELS + 1, P], U8)
        masks_in = at("masks_in", AR + 48 * K, [LEVELS + 1, P], mybir.dt.int32)
        causal = at("causal", AR + 31 * K, [P])
        iw = at("iw", AR + 31 * K + 512, [TT, IDXH])
        e_last = at("e_last", AR + 31 * K + 640, [HG, TT])
        iq = at("iq", AR + 32 * K, [4, S])
        v_hg = at("v_hg", AR + 32 * K, [TT, S])
        ik = at("ik", AR + 40 * K, [S])
        relu = [at(f"relu{s}", AR + (42 + 2 * s) * K, [S]) for s in range(2)]
        tok = at("tok", AR + 40 * K, [TT, M])
        tok_sq = at("tok_sq", AR + 44 * K, [TT, M])
        state = at("state", AR + 40 * K, [TT - 1, HG, HDK])
        sel = at("sel", AR + 48 * K, [TT, S])
        sqT = at("sqT", AR + 56 * K, [2, S])
        skT = at("skT", AR + 60 * K, [2, S])
        mqT = at("mqT", AR + 64 * K, [2, S])
        sv = at("sv", AR + 68 * K, [TT, M])
        lf = at("lf", AR + 72 * K, [HG * S])
        kk = at("kk", AR + 80 * K, [HG * S])
        qf = at("qf", AR + 88 * K, [HG * S])
        sfx = at("sfx", 16 * K, [HG * S])
        ex = at("ex", 24 * K, [HG * S])
        z = at("z", 32 * K, [HG * S])
        kT = at("kT", 32 * K, [TT - 1, HG, HDK])
        aT = at("aT", 40 * K, [HG, TT * P])
        row_2 = [at(f"row_2{s}", (16 + 2 * s) * K, [S]) for s in range(NLP)]
        pT_2 = [at(f"pT_2{s}", (22 + 2 * s) * K, [TT, P]) for s in range(2)]
        assert base + AR + 96 * K <= nc.sbuf_usable_end, (base, AR, nc.sbuf_usable_end)

        bank = [ctx.enter_context(nc.psum_tensor(f"bank{b}", [P, 512], F32)) for b in range(8)]

        def sem(name):
            return ctx.enter_context(nc.semaphore(name))

        raw_full = [sem(f"raw_full{s}") for s in range(2)]
        hi_ready = sem("hi_ready")
        lo_ready = sem("lo_ready")
        w_used = sem("w_used")
        bank_ready = [sem(f"bank_ready{b}") for b in range(8)]
        bank_free = [sem(f"bank_free{b}") for b in range(8)]
        mem_in, x_in, const_in, onehot_in = sem("mem_in"), sem("x_in"), sem("const_in"), sem("onehot_in")
        mem2_in, mask_in = sem("mem2_in"), sem("mask_in")
        set_up = sem("set_up")
        act_step, dve_step = sem("act_step"), sem("dve_step")
        squared = sem("squared")
        summed = sem("summed")
        root_ready = sem("root_ready")
        diag_ready = sem("diag_ready")
        scaled = sem("scaled")
        rounded = sem("rounded")
        split = sem("split")
        neg_max = sem("neg_max")
        exp_ready = sem("exp_ready")
        bias_saved = sem("bias_saved")
        toep_in = [sem("toep_in0"), sem("toep_in1")]
        merge_add = sem("merge_add")
        x_ready = sem("x_ready")
        seed = sem("seed")
        act_gate = sem("act_gate")
        prod = sem("prod")
        a_up = sem("a_up")
        a_down = sem("a_down")
        relu_used = sem("relu_used")
        heads_sq = sem("heads_sq")
        heads_ms = sem("heads_ms")
        heads_norm = sem("heads_norm")
        log_in, log_ready, log_used = sem("log_in"), sem("log_ready"), sem("log_used")
        e_ready, e_used, z_ready, prefix_ready = sem("e_ready"), sem("e_used"), sem("z_ready"), sem("prefix_ready")
        decayed, state_ready = sem("decayed"), sem("state_ready")
        stored = sem("stored")

        block = ctx.enter_context(nc.Block())

        def vcol(name, j):
            return vec[:, VEC[name] + j:VEC[name] + j + 1]

        def turn(key, i=None):
            return slot[key].before if i is None else slot[key].before + slot[key].per * i

        def completion(key, i=None):
            s_ = slot[key]
            value = s_.ready if i is None else s_.ready + s_.ready_per * i
            return (bank_ready[s_.bank] if s_.load is None else w_used), value

        def B(key):
            return bank[slot[key].bank]

        @block.sync
        def _(sp):
            def load(n):
                sp.dma_start(raw[n % 2][:, :], A["weights"][n, :, :]).then_inc(raw_full[n % 2], 16)

            def stream(first, last):
                if first % 2:
                    sp.wait_ge(lo_ready, first - 1)
                    load(first)
                    first += 1
                turns = (last - first) // 2
                with sp.Fori(0, turns) as i:
                    for c in range(2):
                        sp.wait_ge(lo_ready, first + c - 1 + 2 * i)
                        sp.dma_start(raw[c][:, :], A["weights"][bass.ds(first + c + 2 * i, 1), :, :]
                                     .rearrange("n p c -> p (n c)")).then_inc(raw_full[c], 16)
                if (last - first) % 2:
                    sp.wait_ge(lo_ready, last - 2)
                    load(last - 1)

            def toeplitz(pair):
                if pair >= 2:
                    sp.wait_ge(neg_max, UNIT0["att"] + 2 * TT * (pair - 1))
                src = A["bias_scratch"]
                for j in range(2):
                    sp.dma_start(toep[pair % 2][:, j, :],
                                 bass.AP(src.tensor, (2 * pair + j) * 1024, [[1, P], [1, 896]])
                                 ).then_inc(toep_in[pair % 2], 16)

            sp.dma_start(onehot[0:NB + 1, :], A["onehot"]).then_inc(onehot_in, 16)
            sp.dma_start(relb[0:NB, :], A["rel_bias"]).then_inc(onehot_in, 16)
            sp.dma_start(memT[:, :, :], A["memT"].rearrange("(k p) t -> p k t", p=P)).then_inc(mem_in, 16)
            sp.dma_start(vec[:, :], A["vec"]).then_inc(const_in, 16)
            sp.dma_start(rows[:, :], A["rows"]).then_inc(const_in, 16)
            sp.dma_start(ident[:, :], A["ident"]).then_inc(const_in, 16)
            load(0)
            load(1)
            sp.dma_start(x[:, :, :], A["xT"].rearrange("(k p) t -> p k t", p=P)).then_inc(x_in, 16)
            sp.wait_ge(bank_free[1], turn(("bias", 1)) + 1)
            sp.dma_start(A["bias_scratch"], bias_row[0:HEADS, :]).then_inc(bias_saved, 16)
            sp.wait_ge(bias_saved, 16)
            toeplitz(0)
            toeplitz(1)
            stream(2, FIRST["cv"])
            toeplitz(2)
            toeplitz(3)
            stream(FIRST["cv"], FIRST["down"] + 2)
            sp.wait_ge(w_used, FIRST["down"])
            sp.dma_start(mem2T[:, :, :], A["mem2T"].rearrange("(k p) t -> p k t", p=P)).then_inc(mem2_in, 16)
            stream(FIRST["down"] + 2, FIRST["mem_kv_2"])
            sp.wait_ge(w_used, FIRST["mem_kv_2"])
            sp.dma_start(masks_in[:, :, :], A["masks"]).then_inc(mask_in, 16)
            sp.dma_start(causal[:, :], A["causal"]).then_inc(mask_in, 16)
            stream(FIRST["mem_kv_2"], NLOADS)
            for j in range(KT):
                sp.wait_ge(bank_free[j % 4], turn(("down_2", j % 4), j // 4) + 1)
                sp.dma_start(out.rearrange("(k p) t -> k p t", p=P)[j, :, :], x[:, j, :]).then_inc(stored, 16)
            sp.wait_ge(stored, 16 * KT)

        @block.gpsimd
        def _(pool):
            nc.gpsimd.memset(ones[:, :], 1.0).then_inc(set_up, 1)
            pool.wait_ge(set_up, 1)
            nc.gpsimd.memset(relb[NB:NB + 1, :], NEG).then_inc(set_up, 1)
            pool.wait_ge(mask_in, 32)
            nc.gpsimd.tensor_copy(masks[:, :, :], masks_in[:, :, :]).then_inc(set_up, 1)

        @block.scalar
        def _(act):
            link = Chain(act, act_step)
            n = {"sq": 0, "root": 0, "scaled": 0, "heads": 0, "x": 0}

            def ready(key, i=None):
                act.wait_ge(*completion(key, i))

            def frees(key, ins):
                ins.then_inc(bank_free[slot[key].bank], 1)

            def round_w(m, i=None, per=0):
                if i is None:
                    if m >= NLOADS:
                        return
                    act.wait_ge(raw_full[m % 2], 16 * (m // 2 + 1))
                    if m >= 2:
                        act.wait_ge(w_used, m - 1)
                else:
                    act.wait_ge(raw_full[m % 2], 16 * (m // 2 + 1) + 8 * per * i)
                    act.wait_ge(w_used, m - 1 + per * i)
                nc.scalar.activation(w_hi[m % 2][:, :], raw[m % 2][:, :], ACT.Copy).then_inc(hi_ready, 1)

            def squares(src):
                if n["sq"] >= 2:
                    act.wait_ge(summed, n["sq"] - 1)
                nc.scalar.activation(square[n["sq"] % 2][:, 0:src.shape[-1]], src, ACT.Square).then_inc(squared, 1)
                n["sq"] += 1

            def root(width, sem_in, value):
                act.wait_ge(sem_in, value)
                nc.scalar.activation(st[:, 1, 0:width], st[:, 0, 0:width], ACT.Sqrt).then_inc(root_ready, 1)

            def norm_root(name, tokens):
                root(tokens // P, bank_free[7], turn(("sum", name)) + 1)

            def rounds(hi, tokens):
                for j in range(KT):
                    n["scaled"] += 1
                    act.wait_ge(scaled, n["scaled"])
                    nc.scalar.activation(hi[:, j, :], square[j % 2][:, 0:tokens], ACT.Copy).then_inc(rounded, 1)

            def copies(name, loads, per, dst, scale=1.0, func=ACT.Copy):
                for m in range(loads):
                    round_w(FIRST[name] + m + 1)
                    for t in range(per * m, per * m + per):
                        ready((name, t))
                        d = dst(t)
                        frees((name, t), nc.scalar.activation(d, B((name, t))[:, 0:d.shape[-1]], func, scale=scale))

            def turned(name, count, dst):
                for j in range(count):
                    ready((name, j))
                    nc.scalar.activation(dst(j), B((name, j))[:, :], ACT.Copy).then_inc(rounded, 1)

            def attention(kind, count):
                rb, tb = (row, pT) if kind in ("mem", "att") else (row_2, pT_2)
                for s in range(count + 2):
                    if s < count:
                        w = UNIT0[kind] + s
                        keys = UNITS[w][3]
                        act.wait_ge(neg_max, w + 1)
                        src = rb[w % NLP][:, 0:keys]
                        if kind in ("mem", "mem_2"):
                            src = B(("S", w))[:, 0:keys]
                            if w >= NLP:
                                ready(("T", w - NLP))
                        nc.scalar.activation(rb[w % NLP][:, 0:keys], src, ACT.Exp, bias=mx[:, w % 8, 1:2],
                                             scale=MDH ** -0.5 if kind == "mem" else 1.0,
                                             accum_out=mx[:, w % 8, 2:3]).then_inc(exp_ready, 1)
                    if s >= 2:
                        w = UNIT0[kind] + s - 2
                        keys = UNITS[w][3]
                        ready(("T", w))
                        if w >= 2:
                            ready(("O", w - 2))
                        frees(("T", w), nc.scalar.activation(
                            tb[w % 2][:, 0:keys // P, :], B(("T", w))[:, 0:keys].rearrange("p (c t) -> p c t", t=P),
                            ACT.Copy))

            def head_squares(src, dst):
                nc.scalar.activation(dst, src, ACT.Square).then_inc(heads_sq, 1)
                n["heads"] += 1
                root(src.shape[1] * SAH, heads_ms, n["heads"])

            def wait_own(key):
                act.wait_ge(bank_free[slot[key].bank], turn(key) + 1)

            for t in range(2):
                ready(("bias", t))
                frees(("bias", t), nc.scalar.activation(bias_row[0:HEADS, t * 512:(t + 1) * 512],
                                                        B(("bias", t))[0:HEADS, :], ACT.Copy))
            act.wait_ge(mem_in, 16)
            for j in range(KT):
                squares(memT[:, j, :])
            round_w(0)
            norm_root("mem", M)
            rounds(mn_hi, M)
            act.wait_ge(x_in, 16)
            act.wait_ge(split, LOW_END["mem"])
            for j in range(KT):
                squares(x[:, j, :])
            for m in range(2):
                round_w(m + 1)
                for t in (2 * m, 2 * m + 1):
                    ready(("mem_k", t))
                    if t == 0:
                        act.wait_ge(split, LOW_END["mem"])
                    frees(("mem_k", t), nc.scalar.activation(mk[:, t, :], B(("mem_k", t))[:, 0:M], ACT.Copy))
            norm_root("x", S)
            rounds(h_hi, S)
            for m in range(2):
                round_w(m + 3)
                for t in (2 * m, 2 * m + 1):
                    ready(("mem_v", t))
                    frees(("mem_v", t), nc.scalar.activation(mv[:, t % 2, m * COLS:(m + 1) * COLS],
                                                             B(("mem_v", t))[:, 0:COLS], ACT.Copy))
            copies("qm", 2, 2, lambda t: qm[:, t, :])
            attention("mem", MHEADS * TT)
            turned("turn_mem", 4, lambda j: br_hi[:, 8 + j, :])
            copies("q", 2, 2, lambda t: q[:, t, :], scale=DH ** -0.5)
            copies("k", 2, 2, lambda t: k[:, t, :])
            copies("v", 2, 4, lambda t: v[:, t % 4, t // 4 * COLS:(t // 4 + 1) * COLS])
            attention("att", HEADS * TT)
            turned("turn_att", 4, lambda j: br_hi[:, 4 + j, :])
            copies("cc", 2, 2, lambda t: cc[:, t, :])
            round_w(FIRST["cv"] + 1)
            round_w(FIRST["cv"] + 2)
            for m in range(2):
                round_w(FIRST["cb"] + m + 1)
                for t in (2 * m, 2 * m + 1):
                    act.wait_ge(bank_free[t], turn(("cb", t)) + 1)
                    nc.scalar.activation(br_hi[:, t, :], cy[:, t, :], ACT.Copy).then_inc(rounded, 1)
            with act.Fori(0, 3) as i:
                for half in range(2):
                    for m in range(3):
                        round_w(FIRST["branch"] + 3 * half + m + 1, i, 6)
                        for t in range(2 * m, 2 * m + 2) if m < 2 else ():
                            c = 8 * half + t
                            ready(("branch", c), i)
                            act.wait_ge(merge_add, 1 + 4 * half + t - 4 + 8 * i + 4)
                            frees(("branch", c), nc.scalar.activation(
                                gate[:, t, :], B(("branch", c))[:, :], ACT.Sigmoid,
                                bias=vec[:, bass.ds(8 * i + (VEC["b_gate"] + 4 * half + t), 1)]))
            for j in range(KT):
                act.wait_ge(merge_add, 4 + 16 + j + 1)
                if j == 0:
                    act.wait_ge(merge_add, 4 + 24)
                nc.scalar.activation(br_hi[:, j, :], merged[:, j, :], ACT.Copy).then_inc(rounded, 1)
            for m in range(4):
                round_w(FIRST["w_out"] + m + 1)
                for j in (2 * m, 2 * m + 1):
                    ready(("w_out", j))
                    squares(B(("w_out", j))[:, :])
                    frees(("w_out", j), nc.scalar.activation(mixed[:, j, :], B(("w_out", j))[:, :], ACT.Copy))

            def residual_squares():
                for j in range(KT):
                    n["x"] += 1
                    act.wait_ge(x_ready, n["x"])
                    squares(x[:, j, :])

            norm_root("mix", S)
            residual_squares()
            norm_root("ffn", S)
            rounds(h_hi, S)
            with act.Fori(0, FT // 2) as i:
                for m in range(2):
                    round_w(FIRST["up"] + m + 1, i, 2)
                    for c in (2 * m, 2 * m + 1):
                        ready(("up", c), i)
                        j = 2 * i + (c % 2 + (FT if m else 0))
                        if c == 0:
                            act.wait_ge(a_down, 2 * i + 2)
                        nc.scalar.activation(y[c][:, :], B(("up", c))[:, :], ACT.Identity,
                                             bias=vec[:, bass.ds(j + VEC["ffn_conv_b"], 1)],
                                             scale=vec[:, bass.ds(j + (VEC["ffn_conv_w"] + 2 * 2 * FT), 1)]
                                             ).then_inc(seed, 1)
                        if m == 0:
                            act.wait_ge(bank_free[c], turn(("up", c), i) + 1)
                            nc.scalar.activation(y[c][:, :], y[c][:, :], ACT.Gelu_apprx_tanh).then_inc(act_gate, 1)
                for c in range(2):
                    act.wait_ge(prod, 2 * i + (c + 1))
                    nc.scalar.activation(a_hi[:, bass.ds(1024 * i + 512 * c, 512)], y[2 + c][:, :], ACT.Copy
                                         ).then_inc(a_up, 1)
            act.wait_ge(mem2_in, 16)
            for j in range(KT):
                squares(mem2T[:, j, :])
            with act.Fori(0, 2) as i:
                for c in range(4):
                    for m in (0, 1, 2) if c % 2 == 0 else ():
                        round_w(FIRST["down"] + 3 * (c // 2) + m + 1, i, 6)
                    ready(("down", c), i)
                    act.wait_ge(summed, n["sq"] + c - 1 + 4 * i)
                    nc.scalar.activation(square[c % 2][:, :], B(("down", c))[:, :], ACT.Square).then_inc(squared, 1)
                    frees(("down", c), nc.scalar.activation(down[:, bass.ds(2048 * i + 512 * c, 512)],
                                                            B(("down", c))[:, :], ACT.Copy))
            n["sq"] += 8
            norm_root("mem_2", M)
            rounds(mn2_hi, M)
            norm_root("down", S)
            act.wait_ge(split, LOW_END["mem_2"])
            residual_squares()
            round_w(FIRST["mem_kv_2"] + 1)
            round_w(FIRST["mem_kv_2"] + 2)
            for t in range(4):
                ready(("mem_kv_2", t))
                dst = km_tok if t < 2 else vm
                frees(("mem_kv_2", t), nc.scalar.activation(dst[:, t % 2, :], B(("mem_kv_2", t))[:, 0:M], ACT.Copy))
            wait_own(("mem_kv_2", 1))
            head_squares(km_tok[:, :, :], km_sq[:, :, :])
            norm_root("x_2", S)
            rounds(h_hi, S)
            for f in range(2):
                ready(("turn_km", f))
                frees(("turn_km", f), nc.scalar.activation(kmT[:, f, :], B(("turn_km", f))[:, 0:M], ACT.Copy))
            copies("iq", 2, 2, lambda t: iq[:, t, :])
            round_w(FIRST["idx"] + 1)
            ready(("ik", 0))
            frees(("ik", 0), nc.scalar.activation(ik[:, :], B(("ik", 0))[:, :], ACT.Copy))
            ready(("iw", 0))
            frees(("iw", 0), nc.scalar.activation(iw[:, :, :], B(("iw", 0))[:, 0:TT * IDXH]
                                                  .rearrange("p (t h) -> p t h", h=IDXH), ACT.Copy,
                                                  scale=IDXH ** -0.5 * 64 ** -0.5))
            for w, (i, h) in enumerate(IDX):
                ready(("idx", w))
                if w >= 2:
                    act.wait_ge(relu_used, w - 1)
                keys = P * (i + 1)
                frees(("idx", w), nc.scalar.activation(relu[w % 2][:, 0:keys], B(("idx", w))[:, 0:keys], ACT.Relu))
            act.wait_ge(relu_used, len(IDX))

            def turned_heads(name, dst, scale):
                for f in range(2):
                    ready((name, f))
                    frees((name, f), nc.scalar.activation(dst[:, f, :], B((name, f))[:, :], ACT.Copy, scale=scale))

            copies("sq", 1, 4, lambda t: tok[:, t, :])
            wait_own(("sq", 3))
            head_squares(tok[:, :, :], tok_sq[:, :, :])
            round_w(FIRST["sk"] + 1)
            turned_heads("turn_sq", sqT, 64 ** -0.5)
            for t in range(4):
                ready(("sk", t))
                frees(("sk", t), nc.scalar.activation(tok[:, t, :], B(("sk", t))[:, 0:M], ACT.Copy))
            wait_own(("sk", 3))
            head_squares(tok[:, :, :], tok_sq[:, :, :])
            copies("sv", 1, 4, lambda t: sv[:, t, :])
            turned_heads("turn_sk", skT, 1.0)
            copies("mq", 1, 4, lambda t: tok[:, t, :])
            wait_own(("mq", 3))
            head_squares(tok[:, :, :], tok_sq[:, :, :])
            for m in range(2):
                round_w(FIRST["hf"] + m + 1)
                for t in (2 * m, 2 * m + 1):
                    ready(("hf", t))
                    nc.scalar.activation(abs_z[:, t * S:(t + 1) * S], B(("hf", t))[:, :], ACT.Abs)
                    nc.scalar.activation(kk[:, t * S:(t + 1) * S], B(("hf", t))[:, :], ACT.Sigmoid, scale=-1.0
                                         ).then_inc(log_in, 1)
            turned_heads("turn_mq", mqT, 64 ** -0.5)
            act.wait_ge(log_in, 4)
            link(nc.scalar.activation(abs_z[:, :], abs_z[:, :], ACT.Exp, scale=-1.0))
            nc.scalar.activation(abs_z[:, :], abs_z[:, :], ACT.Ln, bias=1.0).then_inc(log_ready, 1)
            copies("hq", 2, 2, lambda t: qf[:, t * S:(t + 1) * S], func=ACT.Silu)
            copies("hi", 2, 4, lambda t: v_hg[:, t % 4, t // 4 * COLS:(t // 4 + 1) * COLS])
            act.wait_ge(log_used, 1)
            copies("hg", 2, 4, lambda t: g_tok[:, t % 4, t // 4 * COLS:(t // 4 + 1) * COLS], func=ACT.Silu)
            for lv in range(LEVELS):
                half = 1 << lv
                pairs = lambda a: a[:, :].rearrange("p (n two l) -> p n two l", two=2, l=half)
                act.wait_ge(prefix_ready, lv + 1)
                if lv:
                    act.wait_ge(e_used, lv)
                nc.scalar.activation(pairs(ex)[:, :, 0, :], pairs(sfx)[:, :, 0, :], ACT.Exp)
                nc.scalar.activation(pairs(ex)[:, :, 1, :], pairs(lf)[:, :, 1, :], ACT.Exp).then_inc(e_ready, 1)
            act.wait_ge(prefix_ready, LEVELS + 1)
            act.wait_ge(e_used, LEVELS)
            nc.scalar.activation(ex[:, :], lf[:, :], ACT.Exp).then_inc(e_ready, 1)
            act.wait_ge(e_used, LEVELS + 1)
            nc.scalar.activation(ex[:, :], sfx[:, :], ACT.Exp).then_inc(e_ready, 1)
            for c in range(TT - 1):
                ready(("turn_kd", c))
                frees(("turn_kd", c), nc.scalar.activation(kT[:, c, :, :], B(("turn_kd", c))[:, :]
                                                           .rearrange("p (h d) -> p h d", d=HDK), ACT.Copy))
            for c in range(TT):
                ready(("o_hg", c))
                if n["sq"] >= 2:
                    act.wait_ge(summed, n["sq"] - 1)
                nc.scalar.activation(square[n["sq"] % 2][:, :], B(("o_hg", c))[:, :], ACT.Square).then_inc(squared, 1)
                n["sq"] += 1
            n["heads"] += 1
            root(HG * TT, heads_ms, n["heads"])
            attention("mem_2", SAH * TT)
            attention("sa", SAH * TT)
            turned("turn_mix", KT, lambda j: h_hi[:, j, :])
            for m in range(4):
                round_w(FIRST["w_out_2"] + m + 1)
                for j in (2 * m, 2 * m + 1):
                    n["x"] += 1
                    act.wait_ge(bank_free[j % 4], turn(("w_out_2", j)) + 1)
                    squares(x[:, j, :])
            norm_root("ffn_2", S)
            rounds(h_hi, S)
            with act.Fori(0, FT // 2) as i:
                round_w(FIRST["up_2"] + 1, i, 2)
                for c in range(2):
                    ready(("up_2", c), i)
                    act.wait_ge(prod, FT + 2 * i)
                    frees(("up_2", c), nc.scalar.activation(y[c][:, :], B(("up_2", c))[:, :], ACT.Silu))
                round_w(FIRST["up_2"] + 2, i, 2)
                for c in range(2):
                    act.wait_ge(prod, FT + 2 * i + (c + 1))
                    nc.scalar.activation(a_hi[:, bass.ds(1024 * i + 512 * c, 512)], y[2 + c][:, :], ACT.Copy
                                         ).then_inc(a_up, 1)
            for m in range(1, 12):
                round_w(FIRST["down_2"] + m)

        @block.vector
        def _(dve):
            link = Chain(dve, dve_step)
            n = {"sum": 0, "root": 0, "scaled": 0, "low": 0, "diag": 0, "heads": 0, "x": 0}

            def ready(key, i=None):
                dve.wait_ge(*completion(key, i))

            def frees(key, ins):
                ins.then_inc(bank_free[slot[key].bank], 1)

            def wait_free(key, i=None):
                dve.wait_ge(bank_free[slot[key].bank], turn(key, i) + 1)

            def split_w(m, i=None, per=0):
                if i is None and m >= NLOADS:
                    return
                dve.wait_ge(hi_ready, m + 1 if i is None else m + 1 + per * i)
                nc.vector.tensor_tensor(w_lo[m % 2][:, :], raw[m % 2][:, :], w_hi[m % 2][:, :].bitcast(F32),
                                        ALU.subtract).then_inc(lo_ready, 1)

            def add_squares(first, tokens=S, into=None):
                into = ssq if into is None else into
                src = square[n["sum"] % 2][:, 0:tokens]
                dve.wait_ge(squared, n["sum"] + 1)
                if first:
                    nc.vector.tensor_copy(into[:, 0:tokens], src).then_inc(summed, 1)
                else:
                    dve.wait_ge(summed, n["sum"])
                    nc.vector.tensor_tensor(into[:, 0:tokens], into[:, 0:tokens], src, ALU.add).then_inc(summed, 1)
                n["sum"] += 1

            def inverse_root(width):
                n["root"] += 1
                ms, r, t = st[:, 0, 0:width], st[:, 2, 0:width], st[:, 3, 0:width]
                dve.wait_ge(root_ready, n["root"])
                link(nc.vector.reciprocal(r, st[:, 1, 0:width]))
                link(nc.vector.tensor_tensor(t, r, r, ALU.mult))
                link(nc.vector.tensor_tensor(t, t, ms, ALU.mult))
                link(nc.vector.tensor_scalar(t, t, -0.5, 1.5, ALU.mult, ALU.add))
                link(nc.vector.tensor_tensor(r, r, t, ALU.mult))

            def norm_scale(name, tokens):
                ready(("sum", name))
                frees(("sum", name), nc.vector.tensor_scalar(st[:, 0, 0:tokens // P], B(("sum", name))[:, 0:tokens // P],
                                                             1.0 / D, EPS, ALU.mult, ALU.add))
                wait_free(("sum", name))
                inverse_root(tokens // P)
                for c in range(tokens // P):
                    ins = nc.vector.tensor_scalar(diag[:, c, :], ident[:, :], st[:, 2, c:c + 1], None, ALU.mult)
                ins.then_inc(diag_ready, 1)
                n["diag"] += 1
                ready(("spread", name))

            def low_part(lo, src, hi, key=None):
                n["low"] += 1
                dve.wait_ge(rounded, n["low"])
                nc.vector.tensor_tensor(lo, src, hi.bitcast(F32), ALU.subtract).then_inc(split, 1)
                if key is not None:
                    dve.wait_ge(split, n["low"])
                    dve.sem_inc(bank_free[slot[key].bank], 1)

            def normalise(name, src, gain, hi, lo, tokens):
                spread = B(("spread", name))[:, 0:tokens]
                for j in range(KT + 1):
                    if j < KT:
                        if j >= 2:
                            dve.wait_ge(split, n["low"])
                        n["scaled"] += 1
                        nc.vector.scalar_tensor_tensor(out=square[j % 2][:, 0:tokens], in0=src[:, j, :],
                                                       scalar=vcol(gain, j), in1=spread, op0=ALU.mult,
                                                       op1=ALU.mult).then_inc(scaled, 1)
                    if j == KT - 1:
                        dve.wait_ge(scaled, n["scaled"])
                        dve.sem_inc(bank_free[slot["spread", name].bank], 1)
                    if j >= 1:
                        low_part(lo[:, j - 1, :], square[(j - 1) % 2][:, 0:tokens], hi[:, j - 1, :])

            def residual(name, src, gain):
                spread = B(("spread", name))[:, :]
                for j in range(KT):
                    ins = nc.vector.scalar_tensor_tensor(out=src(j), in0=src(j), scalar=vcol(gain, j), in1=spread,
                                                         op0=ALU.mult, op1=ALU.mult)
                    if j == KT - 1:
                        frees(("spread", name), ins)
                        wait_free(("spread", name))
                    else:
                        link(ins)
                    nc.vector.tensor_tensor(x[:, j, :], x[:, j, :], src(j), ALU.add).then_inc(x_ready, 1)
                    if j >= 1:
                        add_squares(j == 1)
                add_squares(False)

            def attention(kind, count, bias_of, dst):
                rb = row if kind in ("mem", "att") else row_2
                for s in range(count + 3):
                    if s < count:
                        w = UNIT0[kind] + s
                        _, h, i, keys = UNITS[w]
                        ready(("S", w))
                        S_ = B(("S", w))[:, 0:keys]
                        scale = 1.0
                        if bias_of is None:
                            link(nc.vector.reduce_max(mx[:, w % 8, 0:1], S_, AX.X))
                            scale = MDH ** -0.5 if kind == "mem" else 1.0
                        else:
                            if w >= NLP:
                                ready(("T", w - NLP))
                            frees(("S", w), nc.vector.tensor_tensor_reduce(
                                out=rb[w % NLP][:, 0:keys], in0=S_, in1=bias_of(h, i), scale=1.0, scalar=-3e38,
                                op0=ALU.add, op1=ALU.max, accum_out=mx[:, w % 8, 0:1]))
                            wait_free(("S", w))
                        nc.vector.tensor_scalar(mx[:, w % 8, 1:2], mx[:, w % 8, 0:1], -scale, None, ALU.mult
                                                ).then_inc(neg_max, 1)
                    if s >= 3:
                        w = UNIT0[kind] + s - 3
                        _, h, i, keys = UNITS[w]
                        dve.wait_ge(exp_ready, w + 1)
                        link(nc.vector.reciprocal(mx[:, w % 8, 3:4], mx[:, w % 8, 2:3]))
                        ready(("O", w))
                        d = dst(h, i)
                        frees(("O", w), nc.vector.tensor_scalar(d, B(("O", w))[:, 0:d.shape[-1]], mx[:, w % 8, 3:4],
                                                                None, ALU.mult))

            def turned(name, count, hi, lo):
                for j in range(count):
                    low_part(lo(j), B((name, j))[:, :], hi(j), (name, j))

            for j in range(KT):
                add_squares(j == 0, M)
            split_w(0)
            dve.wait_ge(const_in, 48)
            norm_scale("mem", M)
            normalise("mem", memT, "g_mem", mn_hi, mn_lo, M)
            for j in range(KT):
                add_squares(j == 0)
            split_w(1)
            split_w(2)
            norm_scale("x", S)
            normalise("x", x, "g_pre_mix", h_hi, h_lo, S)
            split_w(3)
            split_w(4)
            split_w(5)
            split_w(6)
            attention("mem", MHEADS * TT, None, lambda h, i: o_tok[:, i, h * MDH:(h + 1) * MDH])
            turned("turn_mem", 4, lambda j: br_hi[:, 8 + j, :], lambda j: br_lo[:, 8 + j, :])
            for m in range(6):
                split_w(FIRST["q"] + m + 1)

            def toeplitz(h, i):
                if i == 0 and h % 2 == 0:
                    dve.wait_ge(toep_in[h // 2 % 2], 32 * (h // 4 + 1))
                return toep[h // 2 % 2][:, h % 2, P * i + 511:383:-1]

            attention("att", HEADS * TT, toeplitz, lambda h, i: o_tok[:, i, h * DH:(h + 1) * DH])
            turned("turn_att", 4, lambda j: br_hi[:, 4 + j, :], lambda j: br_lo[:, 4 + j, :])
            split_w(FIRST["cc"] + 1)
            split_w(FIRST["cc"] + 2)
            for m in range(2):
                split_w(FIRST["cv"] + m + 1)
                for t in (2 * m, 2 * m + 1):
                    wait_free(("cc", t))
                    ready(("cv", t))
                    frees(("cv", t), nc.vector.tensor_tensor(u[:, t, :], B(("cv", t))[:, :], cc[:, t, :], ALU.mult))
                    wait_free(("cv", t))
                    link(nc.vector.tensor_scalar(cy[:, t, :], u[:, t, :], vcol("conv_mix_w", 8 + t), None, ALU.mult))
                    for back in (1, 2):
                        link(nc.vector.scalar_tensor_tensor(
                            out=cy[:, t, back:], in0=u[:, t, 0:S - back], scalar=vcol("conv_mix_w", 4 * (2 - back) + t),
                            in1=cy[:, t, back:], op0=ALU.mult, op1=ALU.add))
            for m in range(2):
                split_w(FIRST["cb"] + m + 1)
                for t in (2 * m, 2 * m + 1):
                    ready(("cb", t))
                    frees(("cb", t), nc.vector.tensor_tensor(cy[:, t, :], B(("cb", t))[:, :], cy[:, t, :], ALU.mult))
                for t in (2 * m, 2 * m + 1):
                    low_part(br_lo[:, t, :], cy[:, t, :], br_hi[:, t, :])
            dve.wait_ge(split, n["low"])
            for t in range(4):
                nc.vector.memset(merged[:, 2 * t:2 * t + 2, :], 0.0).then_inc(merge_add, 1)
            with dve.Fori(0, 3) as i:
                link.enter(i, 8)
                for half in range(2):
                    for m in range(3):
                        split_w(FIRST["branch"] + 3 * half + m + 1, i, 6)
                    for t in range(4):
                        c = 8 * half + 4 + t
                        dve.wait_ge(bank_free[t], turn(("branch", 8 * half + t), i) + 1)
                        ready(("branch", c), i)
                        link(nc.vector.tensor_tensor(part[t % 2][:, :], B(("branch", c))[:, :], gate[:, t, :],
                                                     ALU.mult))
                        dve.sem_inc(bank_free[4 + t], 1)
                        dve.wait_ge(merge_add, 4 + 4 * half + t + 8 * i)
                        nc.vector.tensor_tensor(merged[:, 4 * half + t, :], merged[:, 4 * half + t, :],
                                                part[t % 2][:, :], ALU.add).then_inc(merge_add, 1)
            link.leave(3)
            for j in range(KT):
                low_part(br_lo[:, j, :], merged[:, j, :], br_hi[:, j, :])
            for m in range(4):
                split_w(FIRST["w_out"] + m + 1)
                for j in (2 * m, 2 * m + 1):
                    add_squares(j == 0)
            norm_scale("mix", S)
            wait_free(("w_out", KT - 1))
            residual("mix", lambda j: mixed[:, j, :], "g_post_mix")
            norm_scale("ffn", S)
            normalise("ffn", x, "g_pre_ffn", h_hi, h_lo, S)
            for c in range(2):
                nc.vector.memset(y[2 + c][:, :], 0.0).then_inc(a_down, 1)
            with dve.Fori(0, FT // 2) as i:
                link.enter(i, 4)
                for m in range(2):
                    split_w(FIRST["up"] + m + 1, i, 2)
                    for c in (2 * m, 2 * m + 1):
                        dve.wait_ge(seed, 4 * i + (c + 1))
                        tap = VEC["ffn_conv_w"] + c % 2 + (FT if m else 0)
                        link(nc.vector.scalar_tensor_tensor(
                            out=y[c][:, 1:], in0=B(("up", c))[:, 0:S - 1],
                            scalar=vec[:, bass.ds(2 * i + (tap + 2 * FT), 1)], in1=y[c][:, 1:], op0=ALU.mult,
                            op1=ALU.add))
                        frees(("up", c), nc.vector.scalar_tensor_tensor(
                            out=y[c][:, 2:], in0=B(("up", c))[:, 0:S - 2], scalar=vec[:, bass.ds(2 * i + tap, 1)],
                            in1=y[c][:, 2:], op0=ALU.mult, op1=ALU.add))
                for c in range(2):
                    wait_free(("up", 2 + c), i)
                    dve.wait_ge(act_gate, 2 * i + (c + 1))
                    nc.vector.tensor_tensor(y[2 + c][:, :], y[2 + c][:, :], y[c][:, :], ALU.mult).then_inc(prod, 1)
                for c in range(2):
                    dve.wait_ge(a_up, 2 * i + (c + 1))
                    nc.vector.tensor_tensor(a_lo[:, bass.ds(1024 * i + 512 * c, 512)], y[2 + c][:, :],
                                            a_hi[:, bass.ds(1024 * i + 512 * c, 512)].bitcast(F32), ALU.subtract
                                            ).then_inc(a_down, 1)
            link.leave(FT // 2)
            for j in range(KT):
                add_squares(j == 0, M, ssq_mem2)
            link(nc.vector.memset(ssq[:, :], 0.0))
            with dve.Fori(0, 2) as i:
                for c in range(4):
                    for m in (0, 1, 2) if c % 2 == 0 else ():
                        split_w(FIRST["down"] + 3 * (c // 2) + m + 1, i, 6)
                    dve.wait_ge(squared, n["sum"] + c + 1 + 4 * i)
                    dve.wait_ge(summed, n["sum"] + c + 4 * i)
                    nc.vector.tensor_tensor(ssq[:, :], ssq[:, :], square[c % 2][:, :], ALU.add).then_inc(summed, 1)
            n["sum"] += 8
            norm_scale("mem_2", M)
            normalise("mem_2", mem2T, "norm_mem_2", mn2_hi, mn2_lo, M)
            norm_scale("down", S)
            dve.wait_ge(bank_free[3], turn(("down", 3), 1) + 1)
            residual("down", lambda j: down[:, j * S:(j + 1) * S], "g_post_ffn")
            split_w(FIRST["mem_kv_2"] + 1)
            split_w(FIRST["mem_kv_2"] + 2)

            def head_norm(name, src, sq, tokens, gain, extra=None):
                width = tokens // P * SAH
                n["heads"] += 1
                dve.wait_ge(heads_sq, n["heads"] if extra is None else extra)
                heads = lambda a: a[:, :, :].rearrange("p t (h d) -> p (t h) d", d=64)
                link(nc.vector.tensor_reduce(st[:, 0, 0:width], heads(sq), AX.X, ALU.add))
                link(nc.vector.tensor_scalar(st[:, 0, 0:width], st[:, 0, 0:width], 1.0 / 64, EPS, ALU.mult, ALU.add))
                dve.sem_inc(heads_ms, 1)
                inverse_root(width)
                link(nc.vector.tensor_tensor(heads(src), heads(src), st[:, 2, 0:width].unsqueeze(2)
                                             .to_broadcast([P, width, 64]), ALU.mult))
                nc.vector.tensor_tensor(heads(src), heads(src), rows[:, ROW[gain]:ROW[gain] + 64].unsqueeze(1)
                                        .to_broadcast([P, width, 64]), ALU.mult).then_inc(heads_norm, 1)

            head_norm("km", km_tok, km_sq, M, "mem_k_gain")
            norm_scale("x_2", S)
            normalise("x_2", x, "norm_mix_2", h_hi, h_lo, S)
            for m in range(3):
                split_w(FIRST["iq"] + m + 1)
            dve.wait_ge(set_up, 3)
            link(nc.vector.memset(sel[:, :, :], 0.0))
            wait_free(("iw", 0))
            for w, (i, h) in enumerate(IDX):
                keys = P * (i + 1)
                wait_free(("idx", w))
                if w:
                    dve.wait_ge(relu_used, w)
                nc.vector.scalar_tensor_tensor(out=sel[:, i, 0:keys], in0=relu[w % 2][:, 0:keys],
                                               scalar=iw[:, i, h:h + 1], in1=sel[:, i, 0:keys], op0=ALU.mult,
                                               op1=ALU.add).then_inc(relu_used, 1)
            dve.wait_ge(relu_used, len(IDX))
            for i in range(1, TT):
                link(nc.vector.tensor_tensor(sel[:, i, P * i:P * (i + 1)], sel[:, i, P * i:P * (i + 1)], causal[:, :],
                                             ALU.add))

            def top_keys(first, last):
                for r in range(first, last):
                    i, step = 1 + r // (TOPK // 8), r % (TOPK // 8)
                    scores = sel[:, i, 0:P * (i + 1)]
                    link(nc.vector.max(st[:, 4, 0:8], scores))
                    link(nc.vector.match_replace(scores, in_to_replace=st[:, 4, 0:8], in_values=scores,
                                                 imm_value=TAKEN))
                    if step == TOPK // 8 - 1:
                        link(nc.vector.tensor_scalar(scores, scores, TAKEN, NEG, ALU.not_equal, ALU.mult))

            split_w(FIRST["sq"] + 1)
            top_keys(0, 3)
            head_norm("sq", tok, tok_sq, S, "sa_q_gain")
            split_w(FIRST["sk"] + 1)
            top_keys(3, 7)
            head_norm("sk", tok, tok_sq, S, "sa_k_gain")
            split_w(FIRST["sv"] + 1)
            top_keys(7, 11)
            split_w(FIRST["mq"] + 1)
            top_keys(11, 14)
            head_norm("mq", tok, tok_sq, S, "mem_q_gain")
            for m in range(2):
                split_w(FIRST["hf"] + m + 1)
                for t in (2 * m, 2 * m + 1):
                    dve.wait_ge(log_in, t + 1)
                    frees(("hf", t), nc.vector.tensor_scalar(lf[:, t * S:(t + 1) * S], B(("hf", t))[:, :], 0.0, None,
                                                             ALU.min))
                top_keys(14 + 4 * m, 18 + 4 * m)
            wait_free(("hf", 3))
            dve.wait_ge(log_ready, 1)
            nc.vector.tensor_tensor(lf[:, :], lf[:, :], abs_z[:, :], ALU.subtract).then_inc(log_used, 1)
            for m in range(6):
                split_w(FIRST["hq"] + m + 1)
                top_keys(22 + 5 * m, min(22 + 5 * m + 5, 48))
            for t in range(4, 8):
                wait_free(("hg", t))
            link(nc.vector.tensor_tensor(g_tok[:, :, :].rearrange("p t (h d) -> p (t h) d", d=HDK),
                                         g_tok[:, :, :].rearrange("p t (h d) -> p (t h) d", d=HDK),
                                         rows[:, ROW["hg_out_gain"]:ROW["hg_out_gain"] + HDK].unsqueeze(1)
                                         .to_broadcast([P, TT * HG, HDK]), ALU.mult))
            dve.wait_ge(w_used, FIRST["hg"] + 2)
            link(nc.vector.memset(aT[:, :, :], 0.0))
            nc.vector.memset(sfx[:, :], 0.0).then_inc(prefix_ready, 1)

            def keep(h, lv, key):
                ready(key)
                frees(key, nc.vector.copy_predicated(
                    aT[:, h, :].rearrange("p (c t) -> p c t", t=P),
                    masks[:, lv, :].unsqueeze(1).to_broadcast([P, TT, P]),
                    B(key)[:, :].rearrange("p (c t) -> p c t", t=P)))

            for h in range(HG):
                keep(h, LEVELS, ("self", h))
            for lv in range(LEVELS):
                half = 1 << lv
                pairs = lambda a: a[:, :].rearrange("p (n two l) -> p n two l", two=2, l=half)
                blocks = HG * S // (2 * half)
                dve.wait_ge(e_ready, lv + 1)
                if lv:
                    ready(("level", lv - 1, HG - 1))
                nc.vector.tensor_tensor(pairs(z)[:, :, 0, :], pairs(kk)[:, :, 0, :], pairs(ex)[:, :, 0, :], ALU.mult)
                link(nc.vector.tensor_tensor(pairs(z)[:, :, 1, :], pairs(qf)[:, :, 1, :], pairs(ex)[:, :, 1, :],
                                             ALU.mult))
                dve.sem_inc(z_ready, 1)
                dve.sem_inc(e_used, 1)
                link(nc.vector.tensor_tensor(pairs(sfx)[:, :, 0, :], pairs(sfx)[:, :, 0, :],
                                             pairs(lf)[:, :, 1, half - 1:half].to_broadcast([P, blocks, half]),
                                             ALU.add))
                nc.vector.tensor_tensor(pairs(lf)[:, :, 1, :], pairs(lf)[:, :, 1, :],
                                        pairs(lf)[:, :, 0, half - 1:half].to_broadcast([P, blocks, half]),
                                        ALU.add).then_inc(prefix_ready, 1)
                for h in range(HG):
                    keep(h, lv, ("level", lv, h))
            dve.wait_ge(e_ready, LEVELS + 1)
            nc.vector.tensor_copy(e_last[:, :, :], ex[:, :].rearrange("p (h c t) -> p h c t", h=HG, t=P)[:, :, :, P - 1])
            link(nc.vector.tensor_tensor(qf[:, :], qf[:, :], ex[:, :], ALU.mult))
            dve.sem_inc(e_used, 1)
            dve.wait_ge(e_ready, LEVELS + 2)
            nc.vector.tensor_tensor(kk[:, :], kk[:, :], ex[:, :], ALU.mult).then_inc(decayed, 1)
            for c in range(TT - 1):
                ready(("state", c))
                if c == 0:
                    link(nc.vector.tensor_copy(state[:, 0, :, :], B(("state", 0))[:, :]
                                               .rearrange("p (h d) -> p h d", d=HDK)))
                else:
                    for h in range(HG):
                        ins = nc.vector.scalar_tensor_tensor(
                            out=state[:, c, h, :], in0=state[:, c - 1, h, :], scalar=e_last[:, h, c:c + 1],
                            in1=B(("state", c))[:, h * HDK:(h + 1) * HDK], op0=ALU.mult, op1=ALU.add)
                    link(ins)
                dve.sem_inc(bank_free[slot["state", c].bank], 1)
                dve.sem_inc(state_ready, 1)
            for c in range(TT):
                dve.wait_ge(squared, n["sum"] + 1)
                nc.vector.tensor_reduce(st[:, 0, HG * c:HG * (c + 1)], square[n["sum"] % 2][:, :]
                                        .rearrange("p (h d) -> p h d", d=HDK), AX.X, ALU.add).then_inc(summed, 1)
                n["sum"] += 1
            dve.wait_ge(summed, n["sum"])
            link(nc.vector.tensor_scalar(st[:, 0, :], st[:, 0, :], 1.0 / HDK, EPS, ALU.mult, ALU.add))
            dve.sem_inc(heads_ms, 1)
            n["heads"] += 1
            inverse_root(HG * TT)
            for c in range(TT):
                for h in range(HG):
                    ins = nc.vector.scalar_tensor_tensor(
                        out=mix[:, c, h * HDK:(h + 1) * HDK], in0=B(("o_hg", c))[:, h * HDK:(h + 1) * HDK],
                        scalar=st[:, 2, HG * c + h:HG * c + h + 1], in1=g_tok[:, c, h * HDK:(h + 1) * HDK],
                        op0=ALU.mult, op1=ALU.mult)
                frees(("o_hg", c), ins)
            attention("mem_2", SAH * TT, None, lambda h, i: mix[:, i, 768 + h * 64:768 + (h + 1) * 64])
            attention("sa", SAH * TT, lambda h, i: sel[:, i, 0:P * (i + 1)] if i else causal[:, :],
                      lambda h, i: mix[:, i, 512 + h * 64:512 + (h + 1) * 64])
            turned("turn_mix", KT, lambda j: h_hi[:, j, :], lambda j: h_lo[:, j, :])
            for m in range(4):
                split_w(FIRST["w_out_2"] + m + 1)
                for j in (2 * m, 2 * m + 1):
                    ready(("w_out_2", j))
                    frees(("w_out_2", j), nc.vector.tensor_tensor(x[:, j, :], B(("w_out_2", j))[:, :], x[:, j, :],
                                                                  ALU.add))
                for j in (2 * m, 2 * m + 1):
                    add_squares(j == 0)
            norm_scale("ffn_2", S)
            normalise("ffn_2", x, "norm_ffn_2", h_hi, h_lo, S)
            with dve.Fori(0, FT // 2) as i:
                split_w(FIRST["up_2"] + 1, i, 2)
                split_w(FIRST["up_2"] + 2, i, 2)
                for c in range(2):
                    wait_free(("up_2", c), i)
                    ready(("up_2", 2 + c), i)
                    dve.wait_ge(a_down, FT + 2 + 2 * i)
                    nc.vector.tensor_tensor(y[2 + c][:, :], y[c][:, :], B(("up_2", 2 + c))[:, :], ALU.mult
                                            ).then_inc(prod, 1)
                    dve.wait_ge(prod, FT + 2 * i + (c + 1))
                    dve.sem_inc(bank_free[2 + c], 1)
                for c in range(2):
                    dve.wait_ge(a_up, FT + 2 * i + (c + 1))
                    nc.vector.tensor_tensor(a_lo[:, bass.ds(1024 * i + 512 * c, 512)], y[2 + c][:, :],
                                            a_hi[:, bass.ds(1024 * i + 512 * c, 512)].bitcast(F32), ALU.subtract
                                            ).then_inc(a_down, 1)
            for g in range(4):
                for m in range(3):
                    split_w(FIRST["down_2"] + 3 * g + m + 1)
                for j in (2 * g, 2 * g + 1):
                    ready(("down_2", j % 4), j // 4)
                    frees(("down_2", j % 4), nc.vector.tensor_tensor(x[:, j, :], B(("down_2", j % 4))[:, :],
                                                                     x[:, j, :], ALU.add))

        @block.tensor
        def _(pe):
            n = {"sum": 0, "diag": 0, "heads": 0}

            def claim(key, i=None):
                if slot[key].before or i is not None:
                    pe.wait_ge(bank_free[slot[key].bank], turn(key, i))

            def done(key, ins):
                ins.then_inc(completion(key)[0], 1)

            def weights(m, i=None, per=0):
                pe.wait_ge(lo_ready, m + 1 if i is None else m + 1 + per * i)

            def product(o, lh, ll, rh, rl, first, last):
                nc.tensor.matmul(o, lh, rh, start=first, stop=False)
                nc.tensor.matmul(o, lh, rl, start=False, stop=False)
                return nc.tensor.matmul(o, ll, rh, start=False, stop=last)

            def w(m, hi, ktiles=KT):
                return (w_hi if hi else w_lo)[m % 2][:, :].rearrange("p (k c) -> p k c", k=ktiles)

            def feature_tile(o, m, c, ah, al, tokens=S, ktiles=KT, fresh=None, first=True, last=True, kk_=None):
                for kt in range(kk_ or ktiles):
                    if fresh is not None:
                        pe.wait_ge(split, fresh + kt + 1)
                    cs = slice(c * P, (c + 1) * P)
                    ins = product(o[:, 0:tokens], w(m, 1, ktiles)[:, kt, cs], w(m, 0, ktiles)[:, kt, cs], ah(kt),
                                  al(kt), first and kt == 0, last and kt == (kk_ or ktiles) - 1)
                return ins

            def token_tile(o, m, t, ah, al, lo=0, hi=COLS, fresh=None):
                ts = slice(t * P, (t + 1) * P)
                for kt in range(KT):
                    if fresh is not None:
                        pe.wait_ge(split, fresh + kt + 1)
                    ins = product(o, ah[:, kt, ts], al[:, kt, ts], w(m, 1)[:, kt, lo:hi], w(m, 0)[:, kt, lo:hi],
                                  kt == 0, kt == KT - 1)
                return ins

            H = (lambda kt: h_hi[:, kt, :], lambda kt: h_lo[:, kt, :])

            def feature_loads(name, loads, fresh=None):
                for m in range(loads):
                    weights(FIRST[name] + m)
                    for c in range(2):
                        t = 2 * m + c
                        claim((name, t))
                        ins = feature_tile(B((name, t)), FIRST[name] + m, c, *H, fresh=fresh if t == 0 else None)
                        done((name, t), ins)

            def token_loads(name, loads):
                for m in range(loads):
                    weights(FIRST[name] + m)
                    for t in range(TT):
                        key = (name, TT * m + t)
                        claim(key)
                        done(key, token_tile(B(key)[:, 0:COLS], FIRST[name] + m, t, h_hi, h_lo))

            def norm(name, tokens, sums=None):
                src = ssq if sums is None else sums
                claim(("sum", name))
                n["sum"] += 1
                pe.wait_ge(summed, NORM_SUMS[name])
                for c in range(tokens // P):
                    ins = nc.tensor.matmul(B(("sum", name))[:, c:c + 1], src[:, c * P:(c + 1) * P], ones[:, 0:1],
                                           start=True, stop=True)
                done(("sum", name), ins)
                n["diag"] += 1
                claim(("spread", name))
                pe.wait_ge(diag_ready, n["diag"])
                done(("spread", name), nc.tensor.matmul(B(("spread", name))[:, 0:tokens], ones[:, :],
                                                        diag[:, 0:tokens // P, :].rearrange("p c t -> p (c t)"),
                                                        start=True, stop=True))

            def attention(kind, count, qk, vv):
                rb, tb = (row, pT) if kind in ("mem", "att") else (row_2, pT_2)
                for s in range(count + 3):
                    if kind in ("mem", "mem_2") and 2 <= s < count + 2:
                        u_ = UNIT0[kind] + s - 2
                        pe.wait_ge(exp_ready, u_ + 1)
                        pe.sem_inc(bank_free[slot["S", u_].bank], 1)
                    if s < count:
                        u_ = UNIT0[kind] + s
                        _, h, i, keys = UNITS[u_]
                        claim(("S", u_))
                        q_, k_ = qk(h, i, keys)
                        done(("S", u_), nc.tensor.matmul(B(("S", u_))[:, 0:keys], q_, k_, start=True, stop=True))
                    if 2 <= s < count + 2:
                        u_ = UNIT0[kind] + s - 2
                        keys = UNITS[u_][3]
                        claim(("T", u_))
                        pe.wait_ge(exp_ready, u_ + 1)
                        for c in range(keys // P):
                            ins = nc.tensor.transpose(B(("T", u_))[:, c * P:(c + 1) * P],
                                                      rb[u_ % NLP][:, c * P:(c + 1) * P], ident[:, :])
                        done(("T", u_), ins)
                    if s >= 3:
                        u_ = UNIT0[kind] + s - 3
                        _, h, i, keys = UNITS[u_]
                        claim(("O", u_))
                        pe.wait_ge(bank_free[slot["T", u_].bank], turn(("T", u_)) + 1)
                        for c in range(keys // P):
                            v_ = vv(h, c)
                            ins = nc.tensor.matmul(B(("O", u_))[:, 0:v_.shape[-1]], tb[u_ % 2][:, c, :], v_,
                                                   start=c == 0, stop=c == keys // P - 1)
                        done(("O", u_), ins)

            def turns(name, count, src, blocks):
                for j in range(count):
                    claim((name, j))
                    for t in range(blocks):
                        ins = nc.tensor.transpose(B((name, j))[:, t * P:(t + 1) * P], src(j, t), ident[:, :])
                    done((name, j), ins)

            def wait_all(name, keys):
                for key in keys:
                    pe.wait_ge(bank_free[slot[name, key].bank], turn((name, key)) + 1)

            pe.wait_ge(onehot_in, 32)
            pe.wait_ge(set_up, 2)
            for t in range(2):
                done(("bias", t), nc.tensor.matmul(B(("bias", t))[0:HEADS, :], relb[0:NB + 1, :],
                                                   onehot[0:NB + 1, t * 512:(t + 1) * 512], start=True, stop=True))
            pe.wait_ge(const_in, 48)
            norm("mem", M)
            for m in range(2):
                weights(m)
                for c in range(2):
                    key = ("mem_k", 2 * m + c)
                    claim(key)
                    done(key, feature_tile(B(key), m, c, lambda kt: mn_hi[:, kt, :], lambda kt: mn_lo[:, kt, :],
                                           tokens=M, fresh=0 if m + c == 0 else None))
            norm("x", S)
            for m in range(2):
                weights(2 + m)
                for t in range(MT):
                    key = ("mem_v", 2 * m + t)
                    claim(key)
                    done(key, token_tile(B(key)[:, 0:COLS], 2 + m, t, mn_hi, mn_lo))
            feature_loads("qm", 2, fresh=LOW_END["mem"])
            wait_all("mem_v", range(4))
            wait_all("qm", range(4))
            attention("mem", MHEADS * TT, lambda h, i, keys: (qm[:, h, i * P:(i + 1) * P], mk[:, h, :]),
                      lambda h, c: mv[:, c, h * MDH:(h + 1) * MDH])

            def all_read(kind, count):
                for w_ in range(UNIT0[kind] + count - 2, UNIT0[kind] + count):
                    pe.wait_ge(bank_free[slot["O", w_].bank], turn(("O", w_)) + 1)

            all_read("mem", MHEADS * TT)
            turns("turn_mem", 4, lambda j, t: o_tok[:, t, j * P:(j + 1) * P], TT)
            feature_loads("q", 2)
            feature_loads("k", 2)
            token_loads("v", 2)
            wait_all("k", range(4))
            wait_all("v", range(4, 8))

            def head64(a, h, lo, hi):
                return a[64 * (h % 2):64 * (h % 2) + 64, h // 2, lo:hi]

            attention("att", HEADS * TT,
                      lambda h, i, keys: (head64(q, h, i * P, (i + 1) * P), head64(k, h, 0, keys)),
                      lambda h, c: v[:, c, h * DH:(h + 1) * DH])
            all_read("att", HEADS * TT)
            turns("turn_att", 4, lambda j, t: o_tok[:, t, j * P:(j + 1) * P], TT)
            feature_loads("cc", 2)
            feature_loads("cv", 2)
            feature_loads("cb", 2)
            pe.wait_ge(split, LOW_END["conv"])
            with pe.Fori(0, 3) as i:
                for half in range(2):
                    for m in range(3):
                        ld = FIRST["branch"] + 3 * half + m
                        weights(ld, i, 6)
                        for c in range(2 if m < 2 else 4):
                            key = ("branch", 8 * half + 2 * m + c)
                            claim(key, i)
                            if m < 2:
                                ins = feature_tile(B(key), ld, c, *H)
                            else:
                                ins = feature_tile(
                                    B(key), ld, c, lambda kt: branch(br_hi, i, kt), lambda kt: branch(br_lo, i, kt),
                                    ktiles=4)
                            done(key, ins)
            for m in range(4):
                weights(FIRST["w_out"] + m)
                for c in range(2):
                    key = ("w_out", 2 * m + c)
                    claim(key)
                    done(key, feature_tile(B(key), FIRST["w_out"] + m, c, lambda kt: br_hi[:, kt, :],
                                           lambda kt: br_lo[:, kt, :],
                                           fresh=LOW_END["conv"] if m + c == 0 else None))
            norm("mix", S)
            norm("ffn", S)
            pe.wait_ge(split, LOW_END["ffn"])

            def up(name):
                with pe.Fori(0, FT // 2) as i:
                    for m in range(2):
                        weights(FIRST[name] + m, i, 2)
                        for c in range(2):
                            claim((name, 2 * m + c), i)
                            done((name, 2 * m + c), feature_tile(B((name, 2 * m + c)), FIRST[name] + m, c, *H))

            def down_(name):
                with pe.Fori(0, 2) as i:
                    for g in range(2):
                        for c in range(2):
                            claim((name, 2 * g + c), i)
                        for m in range(3):
                            ld = FIRST[name] + 3 * g + m
                            weights(ld, i, 6)
                            for c in range(2):
                                ins = feature_tile(
                                    B((name, 2 * g + c)), ld, c,
                                    lambda kt: a_hi[:, (8 * m + kt) * S:(8 * m + kt + 1) * S],
                                    lambda kt: a_lo[:, (8 * m + kt) * S:(8 * m + kt + 1) * S],
                                    first=m == 0, last=m == 2, kk_=min(8, FT - 8 * m))
                                if m == 2:
                                    done((name, 2 * g + c), ins)
                            if m < 2:
                                ins.then_inc(w_used, 1)

            up("up")
            pe.wait_ge(a_down, FT + 2)
            down_("down")
            norm("mem_2", M, ssq_mem2)
            norm("down", S)
            pe.wait_ge(split, LOW_END["mem_2"])
            for m in range(2):
                weights(FIRST["mem_kv_2"] + m)
                for t in range(MT):
                    key = ("mem_kv_2", 2 * m + t)
                    claim(key)
                    done(key, token_tile(B(key)[:, 0:COLS], FIRST["mem_kv_2"] + m, t, mn2_hi, mn2_lo))
            norm("x_2", S)

            def turn_heads(name, src, tokens):
                n["heads"] += 1
                pe.wait_ge(heads_norm, n["heads"])
                turns(name, 2, lambda f, t: src[:, t, f * P:(f + 1) * P], tokens // P)

            turn_heads("turn_km", km_tok, M)
            feature_loads("iq", 2, fresh=LOW_END["mem_2"])
            ld = FIRST["idx"]
            weights(ld)
            claim(("ik", 0))
            done(("ik", 0), feature_tile(B(("ik", 0)), ld, 0, *H))
            claim(("iw", 0))
            for t in range(TT):
                ins = token_tile(B(("iw", 0))[:, t * IDXH:(t + 1) * IDXH], ld, t, h_hi, h_lo, P, P + IDXH)
            done(("iw", 0), ins)
            wait_all("iq", range(4))
            wait_all("ik", range(1))
            for w_, (i, h) in enumerate(IDX):
                claim(("idx", w_))
                done(("idx", w_), nc.tensor.matmul(
                    B(("idx", w_))[:, 0:P * (i + 1)], head64(iq, h, i * P, (i + 1) * P),
                    ik[64 * (h % 2):64 * (h % 2) + 64, 0:P * (i + 1)], start=True, stop=True))
            token_loads("sq", 1)
            token_loads("sk", 1)
            turn_heads("turn_sq", tok, S)
            token_loads("sv", 1)
            turn_heads("turn_sk", tok, S)
            token_loads("mq", 1)
            feature_loads("hf", 2)
            turn_heads("turn_mq", tok, S)
            feature_loads("hq", 2)
            token_loads("hi", 2)
            token_loads("hg", 2)
            wait_all("hq", range(4))
            wait_all("hi", range(4, 8))

            def chunk(a, h, c):
                return a[:, h * S + c * P:h * S + (c + 1) * P]

            for h in range(HG):
                claim(("self", h))
                for c in range(TT):
                    ins = nc.tensor.matmul(B(("self", h))[:, c * P:(c + 1) * P], chunk(kk, h, c), chunk(qf, h, c),
                                           start=True, stop=True)
                done(("self", h), ins)
            for lv in range(LEVELS):
                pe.wait_ge(z_ready, lv + 1)
                for h in range(HG):
                    claim(("level", lv, h))
                    for c in range(TT):
                        ins = nc.tensor.matmul(B(("level", lv, h))[:, c * P:(c + 1) * P], chunk(z, h, c),
                                               chunk(z, h, c), start=True, stop=True)
                    done(("level", lv, h), ins)
            pe.wait_ge(decayed, 1)
            turns("turn_kd", TT - 1, lambda c, h: chunk(kk, h, c), HG)
            for c in range(TT - 1):
                claim(("state", c))
                pe.wait_ge(bank_free[slot["turn_kd", c].bank], turn(("turn_kd", c)) + 1)
                for h in range(HG):
                    ins = nc.tensor.matmul(B(("state", c))[:, h * HDK:(h + 1) * HDK], kT[:, c, h, :],
                                           v_hg[:, c, h * HDK:(h + 1) * HDK], start=True, stop=True)
                done(("state", c), ins)
            for c in range(TT):
                claim(("o_hg", c))
                if c:
                    pe.wait_ge(state_ready, c)
                for h in range(HG):
                    o = B(("o_hg", c))[:, h * HDK:(h + 1) * HDK]
                    ins = nc.tensor.matmul(o, aT[:, h, c * P:(c + 1) * P], v_hg[:, c, h * HDK:(h + 1) * HDK],
                                           start=True, stop=c == 0)
                    if c:
                        ins = nc.tensor.matmul(o, chunk(qf, h, c), state[:, c - 1, h, :], start=False, stop=True)
                done(("o_hg", c), ins)
            attention("mem_2", SAH * TT,
                      lambda h, i, keys: (head64(mqT, h, i * P, (i + 1) * P), head64(kmT, h, 0, M)),
                      lambda h, c: vm[:, c, h * 64:(h + 1) * 64])
            attention("sa", SAH * TT,
                      lambda h, i, keys: (head64(sqT, h, i * P, (i + 1) * P), head64(skT, h, 0, keys)),
                      lambda h, c: sv[:, c, h * 64:(h + 1) * 64])
            all_read("sa", SAH * TT)
            turns("turn_mix", KT, lambda j, t: mix[:, t, j * P:(j + 1) * P], TT)
            pe.wait_ge(split, LOW_END["turn_mix"])
            feature_loads("w_out_2", 4)
            norm("ffn_2", S)
            pe.wait_ge(split, LOW_END["ffn_2"])
            up("up_2")
            pe.wait_ge(a_down, 2 * FT + 2)
            down_("down_2")


def branch(a, i, kt):
    return a[:, :, :].rearrange("p j t -> p (j t)")[:, bass.ds(4 * S * i + kt * S, S)]


def bucket_onehot():
    dist = np.arange(1024) - (S - 1)
    n = np.maximum(dist, NB_EXACT).astype(np.float32)
    large = NB_EXACT + (np.log(n / np.float32(NB_EXACT)) / np.float32(math.log(NB_DIST / NB_EXACT))
                        * np.float32(NB - NB_EXACT)).astype(np.int32)
    bucket = np.where(dist < NB_EXACT, dist, np.minimum(large, NB - 1))
    bucket = np.where(dist < 0, NB, bucket)
    return (bucket[None, :] == np.arange(NB + 1)[:, None]).astype(np.float32)


def level_masks():
    s, t = np.arange(P)[:, None], np.arange(P)[None, :]
    out = np.zeros((P, LEVELS + 1, P), np.int32)
    for lv in range(LEVELS):
        out[:, lv, :] = (s >> lv + 1 == t >> lv + 1) & (s >> lv & 1 == 0) & (t >> lv & 1 == 1)
    out[:, LEVELS, :] = s == t
    return out


def packed(w, cols=COLS, ktiles=KT):
    return w.reshape(ktiles, P, -1, cols).transpose(2, 1, 0, 3).reshape(-1, P, ktiles * cols)


def lay_out_weights(a):
    w_in, w_in2 = a["w_in"][0], a["w_in_2"][0]
    o = np.cumsum([0, 512, 512, 512, 512, 512, 512, 512, 1024, 1024, 1024])
    cb, cc, cv, q, k, v, qm, ga, gb, gc = (packed(w_in[:, o[j]:o[j + 1]]) for j in range(10))
    branches = []
    for g, w in ((ga, a["w_conv_out"]), (gb, a["w_attn_out"]), (gc, a["w_mem_out"])):
        w = packed(w[0], 512, 4)
        branches += [g[0:2], w[0:1], g[2:4], w[1:2]]

    def up(w):
        a_, g_ = packed(w[:, :DFF]), packed(w[:, DFF:])
        return np.stack([a_, g_], 1).reshape(2 * DFF // COLS, P, SLOT)

    def down(w):
        w = np.pad(w, ((0, 3 * 8 * P - DFF), (0, 0))).reshape(3, 8, P, 4, COLS)
        return w.transpose(3, 0, 2, 1, 4).reshape(12, P, SLOT)

    o = np.cumsum([0, 512, 512, 512, 512, 256, 256, 256, 512, 64, 8, 256])
    hq, hf, hi, hg, sq, sk, sv, iq, ik, iw, mq = (w_in2[:, o[j]:o[j + 1]] for j in range(11))
    idx = packed(np.pad(np.concatenate([ik, ik, iw], 1), ((0, 0), (0, COLS - 136))))
    parts = [packed(a["w_mem_kv"][0]), qm, q, k, v, cc, cv, cb, *branches, packed(a["w_out"][0]),
             up(a["w_up"][0]), down(a["w_down"][0]), packed(a["w_mem_kv_2"][0]), packed(iq), idx, packed(sq),
             packed(sk), packed(sv), packed(mq), packed(hf), packed(hq), packed(hi), packed(hg),
             packed(a["w_out_2"][0]), up(a["w_ffn_in_2"][0]), down(a["w_ffn_out_2"][0])]
    return np.ascontiguousarray(np.concatenate(parts, 0))


def columns(a):
    col = lambda x: x.reshape(-1, P).T
    names = ["g_pre_mix", "g_post_mix", "g_pre_ffn", "g_post_ffn", "g_mem", "norm_mix_2", "norm_mem_2",
             "norm_ffn_2", "b_gate", "conv_mix_w", "ffn_conv_w", "ffn_conv_b"]
    return np.ascontiguousarray(np.concatenate([col(a[x]) for x in names], 1))


def kernel(**inputs):
    import concourse.bacc as bacc
    from concourse.bass_utils import run_bass_kernel_spmd

    a = {name: np.asarray(value) for name, value in inputs.items()}
    gains = np.concatenate([a[x + "_2"].reshape(-1) for x in ROW])
    arrays = {
        "weights": lay_out_weights(a),
        "xT": np.ascontiguousarray(a["x"][0].T),
        "memT": np.ascontiguousarray(a["mem"][0].T),
        "mem2T": np.ascontiguousarray(a["mem_2"][0].T),
        "vec": columns(a),
        "rows": np.ascontiguousarray(np.broadcast_to(gains, (P, NROW))),
        "rel_bias": a["rel_bias"],
        "ident": np.eye(P, dtype=np.float32),
        "onehot": bucket_onehot(),
        "masks": level_masks(),
        "causal": np.where(np.arange(P)[None, :] <= np.arange(P)[:, None], 0, NEG).astype(np.float32),
    }
    nc = bacc.Bacc("TRN2", target_bir_lowering=False, num_devices=1)
    A = {name: nc.dram_tensor(name, value.shape, mybir.dt.from_np(value.dtype), kind="ExternalInput").ap()
         for name, value in arrays.items()}
    A["bias_scratch"] = nc.dram_tensor("bias_scratch", (HEADS, 1024), F32, kind="Internal").ap()
    out = nc.dram_tensor("outT", (D, S), F32, kind="ExternalOutput").ap()
    build(nc, A, out)
    r = run_bass_kernel_spmd(nc, [arrays], core_ids=[0])
    return np.ascontiguousarray(r.results[0]["outT"].T)[None]
```

```python
import math
from contextlib import ExitStack

import numpy as np

import concourse.bass as bass
from concourse import mybir

F32 = mybir.dt.float32
F32R = mybir.dt.float32r
U8 = mybir.dt.uint8
ACT = mybir.ActivationFunctionType
ALU = mybir.AluOpType
AX = mybir.AxisListType

P = 128
D = 1024
KT = D // P
S = 512
TT = S // P
M = 256
MT = M // P
SLOT = 2048
COLS = SLOT // KT
DFF = 2816
FT = DFF // P
HEADS, DH = 8, 64
MHEADS, MDH = 4, 128
NB, NB_EXACT, NB_DIST = 32, 16, 1024
HG, HDK = 4, 128
SAH = 4
IDXH = 8
TOPK = min(256, S // 4)
NEG = -1e30
TAKEN = -3e38
EPS = 1e-6
LEVELS = 7

VEC = {}
_at = 0
for _name, _n in [("g_pre_mix", 8), ("g_post_mix", 8), ("g_pre_ffn", 8), ("g_post_ffn", 8), ("g_mem", 8),
                  ("norm_mix_2", 8), ("norm_mem_2", 8), ("norm_ffn_2", 8), ("b_gate", 24),
                  ("conv_mix_w", 12), ("ffn_conv_w", 132), ("ffn_conv_b", 44)]:
    VEC[_name] = _at
    _at += _n
NVEC = _at
ROW = {"sa_q_gain": 0, "sa_k_gain": 64, "mem_q_gain": 128, "mem_k_gain": 192, "hg_out_gain": 256}
NROW = 384

LOADS = [("mem_kv", 4), ("qm", 2), ("q", 2), ("k", 2), ("v", 2), ("cc", 2), ("cv", 2), ("cb", 2),
         ("branch", 18), ("w_out", 4), ("up", 22), ("down", 12), ("mem_kv_2", 2), ("iq", 2), ("idx", 1),
         ("hf", 2), ("hq", 2), ("sq", 1), ("sk", 1), ("sv", 1), ("mq", 1), ("hg", 2), ("hi", 2),
         ("w_out_2", 4), ("up_2", 22), ("down_2", 12)]
FIRST = {}
_at = 0
for _name, _n in LOADS:
    FIRST[_name] = _at
    _at += _n
NLOADS = _at

UNITS = ([("mem", h, i, M) for h in range(MHEADS) for i in range(TT)]
         + [("att", h, i, P * (i + 1)) for h in range(HEADS) for i in range(TT)]
         + [("mem_2", h, i, M) for h in range(SAH) for i in range(TT)]
         + [("sa", h, i, P * (i + 1)) for h in range(SAH) for i in range(TT)])
UNIT0 = {"mem": 0, "att": 16, "mem_2": 48, "sa": 64}
IDX = [(i, h) for i in range(1, TT) for h in range(IDXH)]
S_BANKS, T_BANKS, O_BANKS = (4, 5, 2, 3), (6, 0), (7, 1)
NLP = 4
LAG = 3


LOWS = [("mem", KT), ("x", KT), ("turn_mem", 4), ("turn_att", 4), ("conv", 4), ("merged", KT), ("ffn", KT),
        ("mem_2", KT), ("x_2", KT), ("turn_mix", KT), ("ffn_2", KT)]
LOW_END = {}
_at = 0
for _name, _n in LOWS:
    _at += _n
    LOW_END[_name] = _at
NORM_SUMS = {"mem": 8, "x": 16, "mix": 24, "ffn": 32, "mem_2": 40, "down": 48, "x_2": 56, "ffn_2": 68}
IW_SCALE = IDXH ** -0.5 * 64 ** -0.5


class Slot:

    def __init__(self, bank, before, ready, load, per=0, ready_per=0):
        self.bank, self.before, self.ready, self.load = bank, before, ready, load
        self.per, self.ready_per = per, ready_per


def plan_banks():
    used, told = [0] * 8, [0] * 8
    slot = {}

    def use(key, bank, load=None):
        if load is None:
            told[bank] += 1
        slot[key] = Slot(bank, used[bank], told[bank] if load is None else load + 1, load)
        used[bank] += 1

    def tiles(name, n, banks=(0, 1, 2, 3), first=None, per=1):
        for t in range(n):
            last = first is not None and t % per == per - 1
            use((name, t), banks[t % len(banks)], first + t // per if last else None)

    def together(name, first):
        for t in range(4):
            use((name, t), 2 + t, {1: first, 3: first + 1}.get(t))

    def loop(name, banks, times, ends, loads):
        own = [b for c, b in enumerate(banks) if c not in ends]
        for c, b in enumerate(banks):
            if c in ends:
                slot[name, c] = Slot(b, used[b] + banks[:c].count(b), ends[c] + 1, ends[c], banks.count(b), loads)
            else:
                earlier = [x for e, x in enumerate(banks[:c]) if e not in ends].count(b)
                slot[name, c] = Slot(b, used[b] + banks[:c].count(b), told[b] + earlier + 1, None, banks.count(b),
                                     own.count(b))
        for b in banks:
            used[b] += times
        for b in own:
            told[b] += times

    def norm(k):
        use(("sum", k), 7)
        use(("spread", k), 6)

    def attention(kind, n):
        for w in range(UNIT0[kind], UNIT0[kind] + n):
            use(("S", w), S_BANKS[w % 4])
            use(("T", w), T_BANKS[w % 2])
            use(("O", w), O_BANKS[w % 2])

    tiles("bias", 2)
    tiles("mem_k", 4, first=0, per=2)
    norm("mem")
    tiles("mem_v", 4, first=2, per=2)
    tiles("qm", 4, first=FIRST["qm"], per=2)
    norm("x")
    attention("mem", MHEADS * TT)
    tiles("turn_mem", 4)
    tiles("q", 4, first=FIRST["q"], per=2)
    tiles("k", 4, first=FIRST["k"], per=2)
    tiles("v", 8, first=FIRST["v"], per=4)
    attention("att", HEADS * TT)
    tiles("turn_att", 4)
    tiles("cc", 4, first=FIRST["cc"], per=2)
    tiles("cv", 4, first=FIRST["cv"], per=2)
    tiles("cb", 4, first=FIRST["cb"], per=2)
    loop("branch", [0, 1, 2, 3, 4, 5, 6, 7] * 2, 3,
         {c: FIRST["branch"] + m for m, c in enumerate((1, 3, 7, 9, 11, 15))}, 6)
    tiles("w_out", KT, first=FIRST["w_out"], per=2)
    norm("mix")
    together("up_first", FIRST["up"])
    norm("ffn")
    loop("up", [0, 1, 2, 3], FT // 2 - 1, {1: FIRST["up"] + 2, 3: FIRST["up"] + 3}, 2)
    loop("down", [0, 1, 2, 3], 2, {1: FIRST["down"] + 2, 3: FIRST["down"] + 5}, 6)
    use(("sum", "mem_2"), 6)
    norm("down")
    tiles("mem_kv_2", 4, first=FIRST["mem_kv_2"], per=2)
    together("iq", FIRST["iq"])
    norm("x_2")
    tiles("ik", 1)
    use(("iwT", 0), 1, FIRST["idx"])
    use(("iw", 0), 2)
    tiles("turn_km", 2, (4, 5))
    for w in range(len(IDX)):
        use(("idx", w), 4 + w % 4)
    tiles("hf", 4, first=FIRST["hf"], per=2)
    tiles("hq", 4, first=FIRST["hq"], per=2)
    tiles("self", HG)
    for lv in range(LEVELS):
        if lv < 4:
            tiles(("sq", "sk", "sv", "mq")[lv], 4, first=FIRST[("sq", "sk", "sv", "mq")[lv]], per=4)
        elif lv < 6:
            tiles(f"hg{lv - 4}", 4, first=FIRST["hg"] + lv - 4, per=4)
        else:
            tiles("hi0", 4, first=FIRST["hi"], per=4)
        if 1 <= lv <= 4 and lv != 3:
            tiles({1: "turn_sq", 2: "turn_sk", 4: "turn_mq"}[lv], 2, (4, 5))
        for h in range(HG):
            use(("level", lv, h), 4 + h)
    tiles("hi1", 4, first=FIRST["hi"] + 1, per=4)
    tiles("turn_kd", TT - 1, (4, 5, 6))
    tiles("state", TT - 1, (4, 5, 6))
    tiles("o_hg", TT)
    attention("mem_2", SAH * TT)
    attention("sa", SAH * TT)
    tiles("turn_mix", KT)
    tiles("w_out_2", KT, first=FIRST["w_out_2"], per=2)
    together("up_2_first", FIRST["up_2"])
    norm("ffn_2")
    loop("up_2", [0, 1, 2, 3], FT // 2 - 1, {1: FIRST["up_2"] + 2, 3: FIRST["up_2"] + 3}, 2)
    loop("down_2", [0, 1, 2, 3], 2, {1: FIRST["down_2"] + 2, 3: FIRST["down_2"] + 5}, 6)
    return slot


class Chain:

    def __init__(self, engine, sem):
        self.engine, self.sem, self.n, self.add = engine, sem, 0, 0

    def __call__(self, ins):
        ins.then_inc(self.sem, 1)
        self.n += 1
        self.engine.wait_ge(self.sem, self.n + self.add)

    def enter(self, i, per):
        self.start, self.per, self.add = self.n, per, i * per

    def leave(self, times):
        assert self.n - self.start == self.per, (self.n - self.start, self.per)
        self.n += self.per * (times - 1)
        self.add = 0


def build(nc, A, out):
    slot = plan_banks()
    ctx = ExitStack()
    with ctx:
        base = (nc.sbuf_base + 63) // 64 * 64
        K = 1024

        def at(name, offset, shape, dt=F32):
            return nc.alloc_sbuf_tensor_at(name, [P, *shape], dt, offset=base + offset)

        x = at("x", 0, [KT, S])
        h_hi = at("h_hi", 16 * K, [KT, S], F32R)
        h_lo = at("h_lo", 32 * K, [KT, S], F32R)
        raw = [at(f"raw{s}", (48 + 8 * s) * K, [SLOT]) for s in range(2)]
        w_hi = [at(f"w_hi{s}", (64 + 8 * s) * K, [SLOT], F32R) for s in range(2)]
        w_lo = [at(f"w_lo{s}", (80 + 8 * s) * K, [SLOT], F32R) for s in range(2)]
        ssq = at("ssq", 96 * K, [S])
        square = [at(f"square{s}", (98 + 2 * s) * K, [S]) for s in range(2)]
        tap = [at(f"tap{s}", (98 + 2 * s) * K, [S]) for s in range(2)]
        diag = at("diag", 102 * K, [TT, P])
        ssq_mem = at("ssq_mem", 102 * K, [M])
        small = 104 * K
        vec = at("vec", small, [NVEC])
        rows = at("rows", small + 1280, [NROW])
        ident = at("ident", small + 2816, [P])
        ones = at("ones", small + 3328, [P])
        st = at("st", small + 3840, [6, 16])
        mx = at("mx", small + 4224, [8, 4])
        AR = small + 4352

        rms = at("rms", AR + 96 * K, [S])

        br_hi = at("br_hi", AR, [3 * 4, S], F32R)
        br_lo = at("br_lo", AR + 24 * K, [3 * 4, S], F32R)
        memT = at("memT", AR + 48 * K, [KT, M])
        mn_hi = at("mn_hi", AR + 72 * K, [KT, M], F32R)
        mn_lo = at("mn_lo", AR + 80 * K, [KT, M], F32R)
        qm = at("qm", AR + 48 * K, [4, S])
        mk = at("mk", AR + 56 * K, [4, M])
        mv = at("mv", AR + 60 * K, [MT, S])
        q = at("q", AR + 48 * K, [4, S])
        k = at("k", AR + 56 * K, [4, S])
        v = at("v", AR + 64 * K, [TT, S])
        o_tok = at("o_tok", AR + 72 * K, [TT, S])
        row = [at(f"row{s}", AR + (80 + 2 * s) * K, [S]) for s in range(NLP)]
        pT = [at(f"pT{s}", AR + (88 + 2 * s) * K, [TT, P]) for s in range(2)]
        rms_mem = at("rms_mem", AR + 92 * K, [M])
        onehot = at("onehot", AR + 8 * K, [1024])
        relb = at("relb", AR + 12 * K, [HEADS])
        bias_row = at("bias_row", AR + 16 * K, [1024])
        toep = [at(f"toep{s}", AR + 24 * K * s, [2, 896]) for s in range(2)]
        cc = at("cc", AR + 48 * K, [4, S])
        u = at("u", AR + 56 * K, [4, S])
        cy = at("cy", AR + 64 * K, [4, S])
        gate = at("gate", AR + 48 * K, [4, S])
        merged = at("merged", AR + 56 * K, [KT, S])
        part = [at(f"part{s}", AR + (88 + 2 * s) * K, [S]) for s in range(2)]
        mixed = at("mixed", AR + 72 * K, [KT, S])
        a_hi = at("a_hi", AR, [FT * S], F32R)
        a_lo = at("a_lo", AR + 44 * K, [FT * S], F32R)
        y = [at(f"y{s}", AR + (88 + 2 * s) * K, [S]) for s in range(4)]
        down = at("down", 16 * K, [KT * S])
        mem2T = at("mem2T", 32 * K, [KT, M])
        mn2_hi = at("mn2_hi", 40 * K, [KT, M], F32R)
        mn2_lo = at("mn2_lo", AR + 88 * K, [KT, M], F32R)
        mix = at("mix", AR, [TT, D])
        g_tok = at("g_tok", AR + 16 * K, [TT, S])
        abs_z = at("abs_z", AR + 16 * K, [HG * S])
        km_tok = at("km_tok", AR + 24 * K, [MT, M])
        km_sq = at("km_sq", AR + 40 * K, [MT, M])
        kmT = at("kmT", AR + 26 * K, [2, M])
        vm = at("vm", AR + 28 * K, [MT, M])
        masks = at("masks", AR + 30 * K, [LEVELS + 1, P], U8)
        masks_in = at("masks_in", AR + 48 * K, [LEVELS + 1, P], mybir.dt.int32)
        causal = at("causal", AR + 31 * K, [P])
        iw = at("iw", AR + 31 * K + 512, [TT, IDXH])
        e_last = at("e_last", AR + 31 * K + 640, [HG, TT])
        iq = at("iq", AR + 32 * K, [4, S])
        v_hg = at("v_hg", AR + 32 * K, [TT, S])
        ik = [at(f"ik{s}", AR + (40 + 2 * s) * K, [S]) for s in range(2)]
        relu = [at(f"relu{s}", AR + (44 + 2 * s) * K, [S]) for s in range(2)]
        iwT = at("iwT", AR + 16 * K, [S])
        tok = at("tok", AR + 40 * K, [TT, M])
        tok_sq = at("tok_sq", AR + 44 * K, [TT, M])
        state = at("state", AR + 40 * K, [TT - 1, HG, HDK])
        sel = at("sel", AR + 48 * K, [TT, S])
        sqT = at("sqT", AR + 56 * K, [2, S])
        skT = at("skT", AR + 60 * K, [2, S])
        mqT = at("mqT", AR + 64 * K, [2, S])
        sv = at("sv", AR + 68 * K, [TT, M])
        lf = at("lf", AR + 72 * K, [HG * S])
        kk = at("kk", AR + 80 * K, [HG * S])
        qf = at("qf", AR + 88 * K, [HG * S])
        sfx = at("sfx", AR, [HG * S])
        ex = at("ex", AR + 8 * K, [HG * S])
        z = at("z", AR + 32 * K, [HG * S])
        kT = at("kT", AR + 8 * K, [TT - 1, HG, HDK])
        hg_sq = [at(f"hg_sq{s}", AR + (72 + 2 * s) * K, [S]) for s in range(2)]
        mo_hi = at("mo_hi", AR + 16 * K, [KT, S], F32R)
        mo_lo = at("mo_lo", AR + 72 * K, [KT, S], F32R)
        aT = at("aT", 96 * K, [HG, TT * P])
        row_2 = [at(f"row_2{s}", (16 + 2 * s) * K, [S]) for s in range(NLP)]
        pT_2 = [at(f"pT_2{s}", (24 + 2 * s) * K, [TT, P]) for s in range(2)]
        assert base + AR + 98 * K <= nc.sbuf_usable_end, (base, AR, nc.sbuf_usable_end)

        bank = [ctx.enter_context(nc.psum_tensor(f"bank{b}", [P, 512], F32)) for b in range(8)]

        def sem(name):
            return ctx.enter_context(nc.semaphore(name))

        raw_full = [sem(f"raw_full{s}") for s in range(2)]
        hi_ready = sem("hi_ready")
        lo_ready = sem("lo_ready")
        w_used = sem("w_used")
        bank_ready = [sem(f"bank_ready{b}") for b in range(8)]
        bank_free = [sem(f"bank_free{b}") for b in range(8)]
        mem_in, x_in, const_in, onehot_in = sem("mem_in"), sem("x_in"), sem("const_in"), sem("onehot_in")
        mem2_in, mask_in = sem("mem2_in"), sem("mask_in")
        set_up = sem("set_up")
        act_step, dve_step = sem("act_step"), sem("dve_step")
        squared = sem("squared")
        summed = sem("summed")
        root_ready = sem("root_ready")
        diag_ready = sem("diag_ready")
        gated = sem("gated")
        conv_done = sem("conv_done")
        rounded = sem("rounded")
        split = sem("split")
        neg_max = sem("neg_max")
        exp_ready = sem("exp_ready")
        bias_saved = sem("bias_saved")
        toep_in = [sem("toep_in0"), sem("toep_in1")]
        merge_add = sem("merge_add")
        x_ready = sem("x_ready")
        seed = sem("seed")
        act_gate = sem("act_gate")
        prod = sem("prod")
        a_up = sem("a_up")
        a_down = sem("a_down")
        relu_used = sem("relu_used")
        heads_sq = sem("heads_sq")
        heads_ms = sem("heads_ms")
        heads_norm = sem("heads_norm")
        log_in, log_ready, log_used = sem("log_in"), sem("log_ready"), sem("log_used")
        hq_ready = sem("hq_ready")
        rms_col = sem("rms_col")
        e_ready, e_used, z_ready, prefix_ready = sem("e_ready"), sem("e_used"), sem("z_ready"), sem("prefix_ready")
        decayed, state_ready = sem("decayed"), sem("state_ready")
        stored = sem("stored")

        block = ctx.enter_context(nc.Block())

        def vcol(name, j):
            return vec[:, VEC[name] + j:VEC[name] + j + 1]

        def turn(key, i=None):
            return slot[key].before if i is None else slot[key].before + slot[key].per * i

        def completion(key, i=None):
            s_ = slot[key]
            value = s_.ready if i is None else s_.ready + s_.ready_per * i
            return (bank_ready[s_.bank] if s_.load is None else w_used), value

        def B(key):
            return bank[slot[key].bank]

        @block.sync
        def _(sp):
            def load(n):
                sp.dma_start(raw[n % 2][:, :], A["weights"][n, :, :]).then_inc(raw_full[n % 2], 16)

            def stream(first, last):
                if first % 2:
                    sp.wait_ge(lo_ready, first - 1)
                    load(first)
                    first += 1
                turns = (last - first) // 2
                with sp.Fori(0, turns) as i:
                    for c in range(2):
                        sp.wait_ge(lo_ready, first + c - 1 + 2 * i)
                        sp.dma_start(raw[c][:, :], A["weights"][bass.ds(first + c + 2 * i, 1), :, :]
                                     .rearrange("n p c -> p (n c)")).then_inc(raw_full[c], 16)
                if (last - first) % 2:
                    sp.wait_ge(lo_ready, last - 2)
                    load(last - 1)

            def toeplitz(pair):
                if pair >= 2:
                    sp.wait_ge(neg_max, UNIT0["att"] + 2 * TT * (pair - 1))
                src = A["bias_scratch"]
                for j in range(2):
                    sp.dma_start(toep[pair % 2][:, j, :],
                                 bass.AP(src.tensor, (2 * pair + j) * 1024, [[1, P], [1, 896]])
                                 ).then_inc(toep_in[pair % 2], 16)

            sp.dma_start(onehot[0:NB + 1, :], A["onehot"]).then_inc(onehot_in, 16)
            sp.dma_start(relb[0:NB, :], A["rel_bias"]).then_inc(onehot_in, 16)
            sp.dma_start(memT[:, :, :], A["memT"].rearrange("(k p) t -> p k t", p=P)).then_inc(mem_in, 16)
            sp.dma_start(vec[:, :], A["vec"]).then_inc(const_in, 16)
            sp.dma_start(rows[:, :], A["rows"]).then_inc(const_in, 16)
            sp.dma_start(ident[:, :], A["ident"]).then_inc(const_in, 16)
            load(0)
            load(1)
            sp.dma_start(x[:, :, :], A["xT"].rearrange("(k p) t -> p k t", p=P)).then_inc(x_in, 16)
            sp.wait_ge(bank_free[1], turn(("bias", 1)) + 1)
            sp.dma_start(A["bias_scratch"], bias_row[0:HEADS, :]).then_inc(bias_saved, 16)
            sp.wait_ge(bias_saved, 16)
            toeplitz(0)
            toeplitz(1)
            stream(2, FIRST["cv"])
            toeplitz(2)
            toeplitz(3)
            stream(FIRST["cv"], FIRST["down"] + 2)
            sp.wait_ge(w_used, FIRST["down"])
            sp.dma_start(mem2T[:, :, :], A["mem2T"].rearrange("(k p) t -> p k t", p=P)).then_inc(mem2_in, 16)
            stream(FIRST["down"] + 2, FIRST["mem_kv_2"])
            sp.wait_ge(w_used, FIRST["mem_kv_2"])
            sp.dma_start(masks_in[:, :, :], A["masks"]).then_inc(mask_in, 16)
            sp.dma_start(causal[:, :], A["causal"]).then_inc(mask_in, 16)
            stream(FIRST["mem_kv_2"], NLOADS)
            for j in range(KT):
                sp.wait_ge(bank_free[j % 4], turn(("down_2", j % 4), j // 4) + 1)
                sp.dma_start(out.rearrange("(k p) t -> k p t", p=P)[j, :, :], x[:, j, :]).then_inc(stored, 16)
            sp.wait_ge(stored, 16 * KT)

        @block.gpsimd
        def _(pool):
            nc.gpsimd.memset(ones[:, :], 1.0).then_inc(set_up, 1)
            pool.wait_ge(set_up, 1)
            nc.gpsimd.memset(relb[NB:NB + 1, :], NEG).then_inc(set_up, 1)
            pool.wait_ge(mask_in, 32)
            nc.gpsimd.tensor_copy(masks[:, :, :], masks_in[:, :, :]).then_inc(set_up, 1)

        @block.scalar
        def _(act):
            link = Chain(act, act_step)
            n = {"sq": 0, "root": 0, "scaled": 0, "heads": 0, "x": 0}

            def ready(key, i=None):
                act.wait_ge(*completion(key, i))

            def frees(key, ins):
                ins.then_inc(bank_free[slot[key].bank], 1)

            def round_w(m, i=None, per=0):
                if i is None:
                    if m >= NLOADS:
                        return
                    act.wait_ge(raw_full[m % 2], 16 * (m // 2 + 1))
                    if m >= 2:
                        act.wait_ge(w_used, m - 1)
                else:
                    act.wait_ge(raw_full[m % 2], 16 * (m // 2 + 1) + 8 * per * i)
                    act.wait_ge(w_used, m - 1 + per * i)
                nc.scalar.activation(w_hi[m % 2][:, :], raw[m % 2][:, :], ACT.Copy).then_inc(hi_ready, 1)

            def squares(src):
                if n["sq"] >= 2:
                    act.wait_ge(summed, n["sq"] - 1)
                nc.scalar.activation(square[n["sq"] % 2][:, 0:src.shape[-1]], src, ACT.Square).then_inc(squared, 1)
                n["sq"] += 1

            def root(width, sem_in, value):
                act.wait_ge(sem_in, value)
                nc.scalar.activation(st[:, 1, 0:width], st[:, 0, 0:width], ACT.Sqrt).then_inc(root_ready, 1)

            def norm_root(name, tokens):
                root(tokens // P, bank_free[7], turn(("sum", name)) + 1)

            def raised(hi, src, gain, j):
                nc.scalar.activation(hi, src, ACT.Copy, scale=vcol(gain, j)).then_inc(rounded, 1)

            def keep_rms(name, dst, tokens=S):
                ready(("spread", name))
                frees(("spread", name), nc.scalar.activation(dst[:, 0:tokens], B(("spread", name))[:, 0:tokens],
                                                             ACT.Copy))

            def tokens_out(name, dst, func=ACT.Copy, first=0, count=TT):
                for t in range(first, first + count):
                    ready((name, t))
                    frees((name, t), nc.scalar.activation(dst(t), B((name, t))[:, 0:COLS], func,
                                                          scale=st[:, 5, t % TT:t % TT + 1]))

            def turned(name, count, dst):
                for j in range(count):
                    ready((name, j))
                    nc.scalar.activation(dst(j), B((name, j))[:, :], ACT.Copy).then_inc(rounded, 1)

            def attention(kind, count):
                rb, tb = (row, pT) if kind in ("mem", "att") else (row_2, pT_2)
                for s in range(count + LAG):
                    if s < count:
                        w = UNIT0[kind] + s
                        keys = UNITS[w][3]
                        act.wait_ge(neg_max, w + 1)
                        src = rb[w % NLP][:, 0:keys]
                        if kind in ("mem", "mem_2"):
                            src = B(("S", w))[:, 0:keys]
                            if w >= NLP:
                                ready(("T", w - NLP))
                        nc.scalar.activation(rb[w % NLP][:, 0:keys], src, ACT.Exp, bias=mx[:, w % 8, 1:2],
                                             scale=MDH ** -0.5 if kind == "mem" else 1.0,
                                             accum_out=mx[:, w % 8, 2:3]).then_inc(exp_ready, 1)
                    if s >= LAG:
                        w = UNIT0[kind] + s - LAG
                        keys = UNITS[w][3]
                        ready(("T", w))
                        if w >= 2:
                            ready(("O", w - 2))
                        frees(("T", w), nc.scalar.activation(
                            tb[w % 2][:, 0:keys // P, :], B(("T", w))[:, 0:keys].rearrange("p (c t) -> p c t", t=P),
                            ACT.Copy))

            def head_squares(src, dst):
                nc.scalar.activation(dst, src, ACT.Square).then_inc(heads_sq, 1)

            def head_root(width):
                n["heads"] += 1
                root(width, heads_ms, n["heads"])

            def wait_own(key):
                act.wait_ge(bank_free[slot[key].bank], turn(key) + 1)

            for t in range(2):
                ready(("bias", t))
                frees(("bias", t), nc.scalar.activation(bias_row[0:HEADS, t * 512:(t + 1) * 512],
                                                        B(("bias", t))[0:HEADS, :], ACT.Copy))
            round_w(0)
            act.wait_ge(mem_in, 16)
            act.wait_ge(const_in, 48)
            for j in range(KT):
                raised(mn_hi[:, j, :], memT[:, j, :], "g_mem", j)
                squares(memT[:, j, :])
            round_w(1)
            act.wait_ge(x_in, 16)
            for j in range(KT):
                raised(h_hi[:, j, :], x[:, j, :], "g_pre_mix", j)
                squares(x[:, j, :])
            round_w(2)
            norm_root("mem", M)
            keep_rms("mem", rms_mem, M)
            act.wait_ge(rms_col, 1)
            for m in range(2):
                round_w(m + 3)
                for t in (2 * m, 2 * m + 1):
                    ready(("mem_v", t))
                    frees(("mem_v", t), nc.scalar.activation(mv[:, t % 2, m * COLS:(m + 1) * COLS],
                                                             B(("mem_v", t))[:, 0:COLS], ACT.Copy,
                                                             scale=st[:, 5, 8 + t % 2:9 + t % 2]))
            round_w(FIRST["qm"] + 1)
            round_w(FIRST["qm"] + 2)
            norm_root("x", S)
            keep_rms("x", rms)
            attention("mem", MHEADS * TT)
            turned("turn_mem", 4, lambda j: br_hi[:, 8 + j, :])
            for m in range(4):
                round_w(FIRST["q"] + m + 1)
            for m in range(2):
                round_w(FIRST["v"] + m + 1)
                tokens_out("v", lambda t: v[:, t % 4, t // 4 * COLS:(t // 4 + 1) * COLS], first=4 * m)
            attention("att", HEADS * TT)
            turned("turn_att", 4, lambda j: br_hi[:, 4 + j, :])
            for m in range(4):
                round_w(FIRST["cc"] + m + 1)
            for m in range(2):
                round_w(FIRST["cb"] + m + 1)
                for t in (2 * m, 2 * m + 1):
                    wait_own(("cb", t))
                    nc.scalar.activation(br_hi[:, t, :], cy[:, t, :], ACT.Copy).then_inc(rounded, 1)
            with act.Fori(0, 3) as i:
                for half in range(2):
                    for m in range(3):
                        round_w(FIRST["branch"] + 3 * half + m + 1, i, 6)
                        for t in range(2 * m, 2 * m + 2) if m < 2 else ():
                            c = 8 * half + t
                            act.wait_ge(bank_free[slot["branch", c].bank], turn(("branch", c), i) + 1)
                            nc.scalar.activation(gate[:, t, :], gate[:, t, :], ACT.Sigmoid,
                                                 bias=vec[:, bass.ds(8 * i + (VEC["b_gate"] + 4 * half + t), 1)]
                                                 ).then_inc(gated, 1)
            act.wait_ge(merge_add, 4 + 24)
            for j in range(KT):
                nc.scalar.activation(br_hi[:, j, :], merged[:, j, :], ACT.Copy).then_inc(rounded, 1)
            for m in range(4):
                round_w(FIRST["w_out"] + m + 1)
                for j in (2 * m, 2 * m + 1):
                    ready(("w_out", j))
                    squares(B(("w_out", j))[:, :])
                    frees(("w_out", j), nc.scalar.activation(mixed[:, j, :], B(("w_out", j))[:, :], ACT.Copy))

            def next_input(gain, j):
                n["x"] += 1
                act.wait_ge(x_ready, n["x"])
                raised(h_hi[:, j, :], x[:, j, :], gain, j)
                squares(x[:, j, :])

            norm_root("mix", S)
            round_w(FIRST["up"] + 1)
            for j in range(KT):
                next_input("g_pre_ffn", j)
            norm_root("ffn", S)
            round_w(FIRST["up"] + 2)
            keep_rms("ffn", rms)

            def up_turn(name, i=None):
                it = 0 if i is None else i + 1
                for m in range(2):
                    if i is not None:
                        round_w(FIRST["up"] + m + 3, i, 2)
                    for c in (2 * m, 2 * m + 1):
                        key = (name, c)
                        act.wait_ge(bank_free[slot[key].bank], turn(key, i) + 1)
                        if c == 0:
                            act.wait_ge(a_down, 2 * it + 2)
                        j = 2 * it + (c % 2 + (FT if m else 0))
                        nc.scalar.activation(y[c][:, :], tap[c % 2][:, :], ACT.Identity,
                                             bias=vec[:, bass.ds(j + VEC["ffn_conv_b"], 1)],
                                             scale=vec[:, bass.ds(j + (VEC["ffn_conv_w"] + 2 * 2 * FT), 1)]
                                             ).then_inc(seed, 1)
                    if m == 0:
                        for c in range(2):
                            act.wait_ge(conv_done, 4 * it + c + 1)
                            nc.scalar.activation(y[c][:, :], y[c][:, :], ACT.Gelu_apprx_tanh).then_inc(act_gate, 1)
                for c in range(2):
                    act.wait_ge(prod, 2 * it + (c + 1))
                    nc.scalar.activation(a_hi[:, bass.ds(1024 * it + 512 * c, 512)], y[2 + c][:, :], ACT.Copy
                                         ).then_inc(a_up, 1)

            up_turn("up_first")
            with act.Fori(0, FT // 2 - 1) as i:
                up_turn("up", i)
            act.wait_ge(mem2_in, 16)
            for j in range(KT):
                if j == 0:
                    act.wait_ge(a_down, FT + 2)
                raised(mn2_hi[:, j, :], mem2T[:, j, :], "norm_mem_2", j)
                squares(mem2T[:, j, :])
            with act.Fori(0, 2) as i:
                for c in range(4):
                    for m in (0, 1, 2) if c % 2 == 0 else ():
                        round_w(FIRST["down"] + 3 * (c // 2) + m + 1, i, 6)
                    ready(("down", c), i)
                    act.wait_ge(summed, n["sq"] + c - 1 + 4 * i)
                    nc.scalar.activation(square[c % 2][:, :], B(("down", c))[:, :], ACT.Square).then_inc(squared, 1)
                    frees(("down", c), nc.scalar.activation(down[:, bass.ds(2048 * i + 512 * c, 512)],
                                                            B(("down", c))[:, :], ACT.Copy))
            n["sq"] += 8
            root(MT, bank_free[6], turn(("sum", "mem_2")) + 1)
            norm_root("down", S)
            round_w(FIRST["mem_kv_2"] + 1)
            for j in range(4):
                next_input("norm_mix_2", j)
            act.wait_ge(rms_col, 3)
            for t in range(4):
                if t % 2 == 0:
                    round_w(FIRST["mem_kv_2"] + t // 2 + 2)
                ready(("mem_kv_2", t))
                dst = km_tok if t < 2 else vm
                frees(("mem_kv_2", t), nc.scalar.activation(dst[:, t % 2, :], B(("mem_kv_2", t))[:, 0:M], ACT.Copy,
                                                            scale=st[:, 5, 10 + t % 2:11 + t % 2]))
            for j in range(4, KT):
                next_input("norm_mix_2", j)
            wait_own(("mem_kv_2", 1))
            head_squares(km_tok[:, :, :], km_sq[:, :, :])
            norm_root("x_2", S)
            round_w(FIRST["idx"])
            keep_rms("x_2", rms)
            head_root(MT * SAH)
            ready(("iwT", 0))
            frees(("iwT", 0), nc.scalar.activation(iwT[0:IDXH, :], B(("iwT", 0))[0:IDXH, :], ACT.Copy))
            ready(("iw", 0))
            act.wait_ge(rms_col, 4)
            for t in range(TT):
                ins = nc.scalar.activation(iw[:, t, :], B(("iw", 0))[:, t * IDXH:(t + 1) * IDXH], ACT.Copy,
                                           scale=st[:, 5, 4 + t:5 + t])
            frees(("iw", 0), ins)
            round_w(FIRST["hf"])
            for f in range(2):
                ready(("turn_km", f))
                frees(("turn_km", f), nc.scalar.activation(kmT[:, f, :], B(("turn_km", f))[:, 0:M], ACT.Copy))
            for w, (i, h) in enumerate(IDX):
                ready(("idx", w))
                if w >= 2:
                    act.wait_ge(relu_used, w - 1)
                keys = P * (i + 1)
                frees(("idx", w), nc.scalar.activation(relu[w % 2][:, 0:keys], B(("idx", w))[:, 0:keys], ACT.Relu))

            def turned_heads(name, dst, scale):
                for f in range(2):
                    ready((name, f))
                    frees((name, f), nc.scalar.activation(dst[:, f, :], B((name, f))[:, :], ACT.Copy, scale=scale))

            for m in range(2):
                round_w(FIRST["hf"] + m + 1)
                for t in (2 * m, 2 * m + 1):
                    wait_own(("hf", t))
                    nc.scalar.activation(abs_z[:, t * S:(t + 1) * S], lf[:, t * S:(t + 1) * S], ACT.Abs)
                    nc.scalar.activation(kk[:, t * S:(t + 1) * S], lf[:, t * S:(t + 1) * S], ACT.Sigmoid, scale=-1.0
                                         ).then_inc(log_in, 1)
            act.wait_ge(log_in, 4)
            link(nc.scalar.activation(abs_z[:, :], abs_z[:, :], ACT.Exp, scale=-1.0))
            nc.scalar.activation(abs_z[:, :], abs_z[:, :], ACT.Ln, bias=1.0).then_inc(log_ready, 1)
            for m in range(2):
                round_w(FIRST["hq"] + m + 1)
                for t in (2 * m, 2 * m + 1):
                    wait_own(("hq", t))
                    nc.scalar.activation(qf[:, t * S:(t + 1) * S], qf[:, t * S:(t + 1) * S], ACT.Silu
                                         ).then_inc(hq_ready, 1)
            act.wait_ge(relu_used, len(IDX))
            for lv in range(LEVELS):
                round_w(FIRST["sq"] + lv + 1)
                half = 1 << lv
                pairs = lambda a: a[:, :].rearrange("p (n two l) -> p n two l", two=2, l=half)
                act.wait_ge(prefix_ready, lv + 1)
                if lv:
                    act.wait_ge(e_used, lv)
                nc.scalar.activation(pairs(ex)[:, :, 0, :], pairs(sfx)[:, :, 0, :], ACT.Exp)
                nc.scalar.activation(pairs(ex)[:, :, 1, :], pairs(lf)[:, :, 1, :], ACT.Exp).then_inc(e_ready, 1)
                if lv in (1, 2, 4):
                    head_root(TT * SAH)
                    turned_heads(*{1: ("turn_sq", sqT, 64 ** -0.5), 2: ("turn_sk", skT, 1.0),
                                   4: ("turn_mq", mqT, 64 ** -0.5)}[lv])
                if lv in (0, 1, 3):
                    name = ("sq", "sk", "", "mq")[lv]
                    tokens_out(name, lambda t: tok[:, t, :])
                    wait_own((name, 3))
                    head_squares(tok[:, :, :], tok_sq[:, :, :])
                elif lv == 2:
                    tokens_out("sv", lambda t: sv[:, t, :])
                elif lv < 6:
                    act.wait_ge(log_used, 1)
                    tokens_out(f"hg{lv - 4}", lambda t: g_tok[:, t, (lv - 4) * COLS:(lv - 3) * COLS], func=ACT.Silu)
                else:
                    ready(("level", lv, HG - 1))
                    tokens_out("hi0", lambda t: v_hg[:, t, 0:COLS])
            round_w(FIRST["w_out_2"])
            act.wait_ge(prefix_ready, LEVELS + 1)
            act.wait_ge(e_used, LEVELS)
            nc.scalar.activation(ex[:, :], lf[:, :], ACT.Exp).then_inc(e_ready, 1)
            act.wait_ge(e_used, LEVELS + 1)
            nc.scalar.activation(ex[:, :], sfx[:, :], ACT.Exp).then_inc(e_ready, 1)
            tokens_out("hi1", lambda t: v_hg[:, t, COLS:2 * COLS])
            for c in range(TT - 1):
                ready(("turn_kd", c))
                frees(("turn_kd", c), nc.scalar.activation(kT[:, c, :, :], B(("turn_kd", c))[:, :]
                                                           .rearrange("p (h d) -> p h d", d=HDK), ACT.Copy))
            for c in range(TT):
                ready(("o_hg", c))
                if c >= 2:
                    act.wait_ge(summed, n["sq"] - 1)
                nc.scalar.activation(hg_sq[c % 2][:, :], B(("o_hg", c))[:, :], ACT.Square).then_inc(squared, 1)
                n["sq"] += 1
            head_root(HG * TT)
            attention("mem_2", SAH * TT)
            attention("sa", SAH * TT)
            turned("turn_mix", KT, lambda j: mo_hi[:, j, :])
            for m in range(4):
                round_w(FIRST["w_out_2"] + m + 1)
                for j in (2 * m, 2 * m + 1):
                    wait_own(("w_out_2", j))
                    raised(h_hi[:, j, :], x[:, j, :], "norm_ffn_2", j)
                    squares(x[:, j, :])
            round_w(FIRST["up_2"] + 1)
            norm_root("ffn_2", S)
            round_w(FIRST["up_2"] + 2)
            keep_rms("ffn_2", rms)

            def up_2_turn(name, i=None):
                it = 0 if i is None else i + 1
                if i is not None:
                    round_w(FIRST["up_2"] + 3, i, 2)
                for c in range(2):
                    act.wait_ge(bank_free[slot[name, c].bank], turn((name, c), i) + 1)
                    nc.scalar.activation(y[c][:, :], y[c][:, :], ACT.Silu).then_inc(act_gate, 1)
                if i is not None:
                    round_w(FIRST["up_2"] + 4, i, 2)
                for c in range(2):
                    act.wait_ge(prod, FT + 2 * it + (c + 1))
                    nc.scalar.activation(a_hi[:, bass.ds(1024 * it + 512 * c, 512)], y[2 + c][:, :], ACT.Copy
                                         ).then_inc(a_up, 1)

            up_2_turn("up_2_first")
            with act.Fori(0, FT // 2 - 1) as i:
                up_2_turn("up_2", i)
            for m in range(1, 12):
                round_w(FIRST["down_2"] + m)

        @block.vector
        def _(dve):
            link = Chain(dve, dve_step)
            n = {"sum": 0, "root": 0, "scaled": 0, "low": 0, "diag": 0, "heads": 0, "x": 0}

            def ready(key, i=None):
                dve.wait_ge(*completion(key, i))

            def frees(key, ins):
                ins.then_inc(bank_free[slot[key].bank], 1)

            def wait_free(key, i=None):
                dve.wait_ge(bank_free[slot[key].bank], turn(key, i) + 1)

            def split_w(m, i=None, per=0):
                if i is None and m >= NLOADS:
                    return
                dve.wait_ge(hi_ready, m + 1 if i is None else m + 1 + per * i)
                nc.vector.tensor_tensor(w_lo[m % 2][:, :], raw[m % 2][:, :], w_hi[m % 2][:, :].bitcast(F32),
                                        ALU.subtract).then_inc(lo_ready, 1)

            def add_squares(first, tokens=S, into=None):
                into = ssq if into is None else into
                src = square[n["sum"] % 2][:, 0:tokens]
                dve.wait_ge(squared, n["sum"] + 1)
                if first:
                    nc.vector.tensor_copy(into[:, 0:tokens], src).then_inc(summed, 1)
                else:
                    dve.wait_ge(summed, n["sum"])
                    nc.vector.tensor_tensor(into[:, 0:tokens], into[:, 0:tokens], src, ALU.add).then_inc(summed, 1)
                n["sum"] += 1

            def inverse_root(width):
                n["root"] += 1
                ms, r, t = st[:, 0, 0:width], st[:, 2, 0:width], st[:, 3, 0:width]
                dve.wait_ge(root_ready, n["root"])
                link(nc.vector.reciprocal(r, st[:, 1, 0:width]))
                link(nc.vector.tensor_tensor(t, r, r, ALU.mult))
                link(nc.vector.tensor_tensor(t, t, ms, ALU.mult))
                link(nc.vector.tensor_scalar(t, t, -0.5, 1.5, ALU.mult, ALU.add))
                link(nc.vector.tensor_tensor(r, r, t, ALU.mult))

            def norm_scale(name, tokens, keep=None, spread=True):
                ready(("sum", name))
                frees(("sum", name), nc.vector.tensor_scalar(st[:, 0, 0:tokens // P], B(("sum", name))[:, 0:tokens // P],
                                                             1.0 / D, EPS, ALU.mult, ALU.add))
                wait_free(("sum", name))
                inverse_root(tokens // P)
                if keep is not None:
                    ins = nc.vector.tensor_copy(st[:, 5, keep:keep + tokens // P], st[:, 2, 0:tokens // P])
                    if name == "x_2":
                        link(ins)
                        ins = nc.vector.tensor_scalar(st[:, 5, 4:8], st[:, 5, 0:4], IW_SCALE, None, ALU.mult)
                    ins.then_inc(rms_col, 1)
                if not spread:
                    return
                for c in range(tokens // P):
                    ins = nc.vector.tensor_scalar(diag[:, c, :], ident[:, :], st[:, 2, c:c + 1], None, ALU.mult)
                ins.then_inc(diag_ready, 1)

            def low_part(lo, src, hi, key=None):
                n["low"] += 1
                dve.wait_ge(rounded, n["low"])
                nc.vector.tensor_tensor(lo, src, hi.bitcast(F32), ALU.subtract).then_inc(split, 1)
                if key is not None:
                    dve.wait_ge(split, n["low"])
                    dve.sem_inc(bank_free[slot[key].bank], 1)

            def low_gained(lo, src, gain, hi, j):
                n["low"] += 1
                dve.wait_ge(rounded, n["low"])
                nc.vector.scalar_tensor_tensor(out=lo, in0=src, scalar=vcol(gain, j), in1=hi.bitcast(F32),
                                               op0=ALU.mult, op1=ALU.subtract).then_inc(split, 1)

            def residual(name, src, gain, next_gain, tiles):
                spread = B(("spread", name))[:, :]
                ready(("spread", name))
                for j in tiles:
                    ins = nc.vector.scalar_tensor_tensor(out=src(j), in0=src(j), scalar=vcol(gain, j), in1=spread,
                                                         op0=ALU.mult, op1=ALU.mult)
                    if j == KT - 1:
                        frees(("spread", name), ins)
                        wait_free(("spread", name))
                    else:
                        link(ins)
                    nc.vector.tensor_tensor(x[:, j, :], x[:, j, :], src(j), ALU.add).then_inc(x_ready, 1)
                    if j:
                        low_gained(h_lo[:, j - 1, :], x[:, j - 1, :], next_gain, h_hi[:, j - 1, :], j - 1)
                        add_squares(j == 1)
                if j == KT - 1:
                    low_gained(h_lo[:, j, :], x[:, j, :], next_gain, h_hi[:, j, :], j)
                    add_squares(False)

            def times_rms(name, loads, dst, scale=None):
                for m in range(loads):
                    split_w(FIRST[name] + m + 1)
                    for t in (2 * m, 2 * m + 1):
                        ready((name, t))
                        normal(name, t, dst(t), scale)

            def normal(name, t, dst, scale=None, i=None):
                src = B((name, t))[:, :]
                if scale is None:
                    ins = nc.vector.tensor_tensor(dst, src, rms[:, :], ALU.mult)
                else:
                    ins = nc.vector.scalar_tensor_tensor(out=dst, in0=src, scalar=scale, in1=rms[:, :],
                                                         op0=ALU.mult, op1=ALU.mult)
                frees((name, t), ins)

            def attention(kind, count, bias_of, dst, between=None):
                rb = row if kind in ("mem", "att") else row_2
                for s in range(count + LAG + 1):
                    if between is not None:
                        between(s)
                    if s < count:
                        w = UNIT0[kind] + s
                        _, h, i, keys = UNITS[w]
                        ready(("S", w))
                        S_ = B(("S", w))[:, 0:keys]
                        scale = 1.0
                        if bias_of is None:
                            link(nc.vector.reduce_max(mx[:, w % 8, 0:1], S_, AX.X))
                            scale = MDH ** -0.5 if kind == "mem" else 1.0
                        else:
                            if w >= NLP:
                                ready(("T", w - NLP))
                            frees(("S", w), nc.vector.tensor_tensor_reduce(
                                out=rb[w % NLP][:, 0:keys], in0=S_, in1=bias_of(h, i), scale=1.0, scalar=-3e38,
                                op0=ALU.add, op1=ALU.max, accum_out=mx[:, w % 8, 0:1]))
                            wait_free(("S", w))
                        nc.vector.tensor_scalar(mx[:, w % 8, 1:2], mx[:, w % 8, 0:1], -scale, None, ALU.mult
                                                ).then_inc(neg_max, 1)
                    if s >= LAG + 1:
                        w = UNIT0[kind] + s - LAG - 1
                        _, h, i, keys = UNITS[w]
                        dve.wait_ge(exp_ready, w + 1)
                        link(nc.vector.reciprocal(mx[:, w % 8, 3:4], mx[:, w % 8, 2:3]))
                        ready(("O", w))
                        d = dst(h, i)
                        frees(("O", w), nc.vector.tensor_scalar(d, B(("O", w))[:, 0:d.shape[-1]], mx[:, w % 8, 3:4],
                                                                None, ALU.mult))

            def turned(name, count, hi, lo):
                for j in range(count):
                    low_part(lo(j), B((name, j))[:, :], hi(j), (name, j))

            split_w(0)
            dve.wait_ge(const_in, 48)
            for j in range(KT):
                low_gained(mn_lo[:, j, :], memT[:, j, :], "g_mem", mn_hi[:, j, :], j)
                add_squares(j == 0, M, ssq_mem)
            split_w(1)
            for j in range(KT):
                low_gained(h_lo[:, j, :], x[:, j, :], "g_pre_mix", h_hi[:, j, :], j)
                add_squares(j == 0)
            split_w(2)
            norm_scale("mem", M, keep=8)
            dve.wait_ge(bank_free[6], turn(("spread", "mem")) + 1)
            for t in range(4):
                ready(("mem_k", t))
                frees(("mem_k", t), nc.vector.tensor_tensor(mk[:, t, :], B(("mem_k", t))[:, 0:M], rms_mem[:, :],
                                                            ALU.mult))
            split_w(3)
            split_w(4)
            split_w(5)
            split_w(6)
            norm_scale("x", S, keep=0)
            wait_free(("spread", "x"))
            for t in range(4):
                ready(("qm", t))
                normal("qm", t, qm[:, t, :])
            attention("mem", MHEADS * TT, None, lambda h, i: o_tok[:, i, h * MDH:(h + 1) * MDH])
            turned("turn_mem", 4, lambda j: br_hi[:, 8 + j, :], lambda j: br_lo[:, 8 + j, :])
            times_rms("q", 2, lambda t: q[:, t, :], DH ** -0.5)
            times_rms("k", 2, lambda t: k[:, t, :])
            split_w(FIRST["v"] + 1)
            split_w(FIRST["v"] + 2)

            def toeplitz(h, i):
                if i == 0 and h % 2 == 0:
                    dve.wait_ge(toep_in[h // 2 % 2], 32 * (h // 4 + 1))
                return toep[h // 2 % 2][:, h % 2, P * i + 511:383:-1]

            attention("att", HEADS * TT, toeplitz, lambda h, i: o_tok[:, i, h * DH:(h + 1) * DH])
            turned("turn_att", 4, lambda j: br_hi[:, 4 + j, :], lambda j: br_lo[:, 4 + j, :])
            times_rms("cc", 2, lambda t: cc[:, t, :])
            for m in range(2):
                split_w(FIRST["cv"] + m + 1)
                for t in (2 * m, 2 * m + 1):
                    wait_free(("cc", t))
                    link(nc.vector.tensor_tensor(cc[:, t, :], cc[:, t, :], rms[:, :], ALU.mult))
                    ready(("cv", t))
                    frees(("cv", t), nc.vector.tensor_tensor(u[:, t, :], B(("cv", t))[:, :], cc[:, t, :], ALU.mult))
                    wait_free(("cv", t))
                    link(nc.vector.tensor_scalar(cy[:, t, :], u[:, t, :], vcol("conv_mix_w", 8 + t), None, ALU.mult))
                    for back in (1, 2):
                        link(nc.vector.scalar_tensor_tensor(
                            out=cy[:, t, back:], in0=u[:, t, 0:S - back], scalar=vcol("conv_mix_w", 4 * (2 - back) + t),
                            in1=cy[:, t, back:], op0=ALU.mult, op1=ALU.add))
                    link(nc.vector.tensor_tensor(cy[:, t, :], cy[:, t, :], rms[:, :], ALU.mult))
            for m in range(2):
                split_w(FIRST["cb"] + m + 1)
                for t in (2 * m, 2 * m + 1):
                    ready(("cb", t))
                    frees(("cb", t), nc.vector.tensor_tensor(cy[:, t, :], B(("cb", t))[:, :], cy[:, t, :], ALU.mult))
                for t in (2 * m, 2 * m + 1):
                    low_part(br_lo[:, t, :], cy[:, t, :], br_hi[:, t, :])
            dve.wait_ge(split, n["low"])
            for t in range(4):
                nc.vector.memset(merged[:, 2 * t:2 * t + 2, :], 0.0).then_inc(merge_add, 1)
            with dve.Fori(0, 3) as i:
                link.enter(i, 8)
                for half in range(2):
                    for m in range(3):
                        split_w(FIRST["branch"] + 3 * half + m + 1, i, 6)
                        for t in range(2 * m, 2 * m + 2) if m < 2 else ():
                            dve.wait_ge(merge_add, 1 + 4 * half + t + 8 * i)
                            ready(("branch", 8 * half + t), i)
                            normal("branch", 8 * half + t, gate[:, t, :])
                    for t in range(4):
                        c = 8 * half + 4 + t
                        dve.wait_ge(gated, 4 * half + t + 1 + 8 * i)
                        ready(("branch", c), i)
                        link(nc.vector.tensor_tensor(part[t % 2][:, :], B(("branch", c))[:, :], gate[:, t, :],
                                                     ALU.mult))
                        dve.sem_inc(bank_free[4 + t], 1)
                        dve.wait_ge(merge_add, 4 + 4 * half + t + 8 * i)
                        nc.vector.tensor_tensor(merged[:, 4 * half + t, :], merged[:, 4 * half + t, :],
                                                part[t % 2][:, :], ALU.add).then_inc(merge_add, 1)
            link.leave(3)
            for j in range(KT):
                low_part(br_lo[:, j, :], merged[:, j, :], br_hi[:, j, :])
            for m in range(4):
                split_w(FIRST["w_out"] + m + 1)
                for j in (2 * m, 2 * m + 1):
                    add_squares(j == 0)
            norm_scale("mix", S)
            wait_free(("w_out", KT - 1))
            residual("mix", lambda j: mixed[:, j, :], "g_post_mix", "g_pre_ffn", range(1))
            split_w(FIRST["up"] + 1)
            residual("mix", lambda j: mixed[:, j, :], "g_post_mix", "g_pre_ffn", range(1, KT))
            norm_scale("ffn", S)
            split_w(FIRST["up"] + 2)
            for c in range(2):
                nc.vector.memset(y[2 + c][:, :], 0.0).then_inc(a_down, 1)
            wait_free(("spread", "ffn"))

            def up_turn(name, i=None):
                it = 0 if i is None else i + 1
                for m in range(2):
                    if i is not None:
                        split_w(FIRST["up"] + m + 3, i, 2)
                    for c in (2 * m, 2 * m + 1):
                        ready((name, c), i)
                        normal(name, c, tap[c % 2][:, :])
                    for c in (2 * m, 2 * m + 1):
                        wait_free((name, c), i)
                        dve.wait_ge(seed, 4 * it + (c + 1))
                        col = VEC["ffn_conv_w"] + c % 2 + (FT if m else 0)
                        link(nc.vector.scalar_tensor_tensor(
                            out=y[c][:, 1:], in0=tap[c % 2][:, 0:S - 1],
                            scalar=vec[:, bass.ds(2 * it + (col + 2 * FT), 1)], in1=y[c][:, 1:], op0=ALU.mult,
                            op1=ALU.add))
                        nc.vector.scalar_tensor_tensor(
                            out=y[c][:, 2:], in0=tap[c % 2][:, 0:S - 2], scalar=vec[:, bass.ds(2 * it + col, 1)],
                            in1=y[c][:, 2:], op0=ALU.mult, op1=ALU.add).then_inc(conv_done, 1)
                    dve.wait_ge(conv_done, 4 * it + (2 * m + 2))
                for c in range(2):
                    dve.wait_ge(act_gate, 2 * it + (c + 1))
                    nc.vector.tensor_tensor(y[2 + c][:, :], y[2 + c][:, :], y[c][:, :], ALU.mult).then_inc(prod, 1)
                for c in range(2):
                    dve.wait_ge(a_up, 2 * it + (c + 1))
                    nc.vector.tensor_tensor(a_lo[:, bass.ds(1024 * it + 512 * c, 512)], y[2 + c][:, :],
                                            a_hi[:, bass.ds(1024 * it + 512 * c, 512)].bitcast(F32), ALU.subtract
                                            ).then_inc(a_down, 1)

            up_turn("up_first")
            with dve.Fori(0, FT // 2 - 1) as i:
                link.enter(i, 4)
                up_turn("up", i)
            link.leave(FT // 2 - 1)
            dve.wait_ge(a_down, FT + 2)
            for j in range(KT):
                low_gained(mn2_lo[:, j, :], mem2T[:, j, :], "norm_mem_2", mn2_hi[:, j, :], j)
                add_squares(j == 0, M, ssq_mem)
            link(nc.vector.memset(ssq[:, :], 0.0))
            with dve.Fori(0, 2) as i:
                for c in range(4):
                    for m in (0, 1, 2) if c % 2 == 0 else ():
                        split_w(FIRST["down"] + 3 * (c // 2) + m + 1, i, 6)
                    dve.wait_ge(squared, n["sum"] + c + 1 + 4 * i)
                    dve.wait_ge(summed, n["sum"] + c + 4 * i)
                    nc.vector.tensor_tensor(ssq[:, :], ssq[:, :], square[c % 2][:, :], ALU.add).then_inc(summed, 1)
            n["sum"] += 8
            norm_scale("mem_2", M, keep=10, spread=False)
            norm_scale("down", S)
            dve.wait_ge(bank_free[3], turn(("down", 3), 1) + 1)
            out_tile = lambda j: down[:, j * S:(j + 1) * S]
            residual("down", out_tile, "g_post_ffn", "norm_mix_2", range(1))
            split_w(FIRST["mem_kv_2"] + 1)
            residual("down", out_tile, "g_post_ffn", "norm_mix_2", range(1, 4))
            split_w(FIRST["mem_kv_2"] + 2)
            split_w(FIRST["mem_kv_2"] + 3)
            dve.wait_ge(w_used, FIRST["mem_kv_2"] + 2)
            residual("down", out_tile, "g_post_ffn", "norm_mix_2", range(4, KT))
            norm_scale("x_2", S, keep=0)

            def head_norm(name, src, sq, tokens, gain):
                width = tokens // P * SAH
                n["heads"] += 1
                dve.wait_ge(heads_sq, n["heads"])
                heads = lambda a: a[:, :, :].rearrange("p t (h d) -> p (t h) d", d=64)
                link(nc.vector.tensor_reduce(st[:, 0, 0:width], heads(sq), AX.X, ALU.add))
                link(nc.vector.tensor_scalar(st[:, 0, 0:width], st[:, 0, 0:width], 1.0 / 64, EPS, ALU.mult, ALU.add))
                dve.sem_inc(heads_ms, 1)
                inverse_root(width)
                link(nc.vector.tensor_tensor(heads(src), heads(src), st[:, 2, 0:width].unsqueeze(2)
                                             .to_broadcast([P, width, 64]), ALU.mult))
                nc.vector.tensor_tensor(heads(src), heads(src), rows[:, ROW[gain]:ROW[gain] + 64].unsqueeze(1)
                                        .to_broadcast([P, width, 64]), ALU.mult).then_inc(heads_norm, 1)

            split_w(FIRST["idx"])
            wait_free(("spread", "x_2"))
            for t in range(4):
                ready(("iq", t))
                normal("iq", t, iq[:, t, :])
            head_norm("km", km_tok, km_sq, M, "mem_k_gain")
            link(nc.vector.memset(ik[0][64:P, :], 0.0))
            link(nc.vector.memset(ik[1][0:64, :], 0.0))
            ready(("ik", 0))
            link(nc.vector.tensor_tensor(ik[0][0:64, :], B(("ik", 0))[0:64, :], rms[0:64, :], ALU.mult))
            frees(("ik", 0), nc.vector.tensor_tensor(ik[1][64:P, :], B(("ik", 0))[64:P, :], rms[64:P, :], ALU.mult))
            split_w(FIRST["hf"])
            dve.wait_ge(set_up, 3)
            link(nc.vector.memset(sel[:, :, :], 0.0))
            wait_free(("iw", 0))
            for w, (i, h) in enumerate(IDX):
                keys = P * (i + 1)
                wait_free(("idx", w))
                if w:
                    dve.wait_ge(relu_used, w)
                nc.vector.scalar_tensor_tensor(out=sel[:, i, 0:keys], in0=relu[w % 2][:, 0:keys],
                                               scalar=iw[:, i, h:h + 1], in1=sel[:, i, 0:keys], op0=ALU.mult,
                                               op1=ALU.add).then_inc(relu_used, 1)
            dve.wait_ge(relu_used, len(IDX))
            for i in range(1, TT):
                link(nc.vector.tensor_tensor(sel[:, i, P * i:P * (i + 1)], sel[:, i, P * i:P * (i + 1)], causal[:, :],
                                             ALU.add))

            def top_keys(first, last):
                for r in range(first, last):
                    i, step = 1 + r // (TOPK // 8), r % (TOPK // 8)
                    scores = sel[:, i, 0:P * (i + 1)]
                    link(nc.vector.max(st[:, 4, 0:8], scores))
                    link(nc.vector.match_replace(scores, in_to_replace=st[:, 4, 0:8], in_values=scores,
                                                 imm_value=TAKEN))
                    if step == TOPK // 8 - 1:
                        link(nc.vector.tensor_scalar(scores, scores, TAKEN, NEG, ALU.not_equal, ALU.mult))

            for m in range(2):
                split_w(FIRST["hf"] + m + 1)
                top_keys(5 * m, 5 * m + 5)
                for t in (2 * m, 2 * m + 1):
                    ready(("hf", t))
                    normal("hf", t, lf[:, t * S:(t + 1) * S])
            for m in range(2):
                split_w(FIRST["hq"] + m + 1)
                if m == 0:
                    dve.wait_ge(log_in, 4)
                    link(nc.vector.tensor_scalar(lf[:, :], lf[:, :], 0.0, None, ALU.min))
                    dve.wait_ge(log_ready, 1)
                    nc.vector.tensor_tensor(lf[:, :], lf[:, :], abs_z[:, :], ALU.subtract).then_inc(log_used, 1)
                top_keys(10 + 5 * m, 15 + 5 * m)
                for t in (2 * m, 2 * m + 1):
                    ready(("hq", t))
                    normal("hq", t, qf[:, t * S:(t + 1) * S])
            link(nc.vector.memset(aT[:, :, :], 0.0))
            dve.wait_ge(log_used, 1)
            nc.vector.memset(sfx[:, :], 0.0).then_inc(prefix_ready, 1)
            dve.wait_ge(hq_ready, 4)

            def keep(h, lv, key):
                ready(key)
                frees(key, nc.vector.copy_predicated(
                    aT[:, h, :].rearrange("p (c t) -> p c t", t=P),
                    masks[:, lv, :].unsqueeze(1).to_broadcast([P, TT, P]),
                    B(key)[:, :].rearrange("p (c t) -> p c t", t=P)))

            for lv in range(LEVELS + 1):
                split_w(FIRST["sq"] + lv + 1)
                for h in range(HG):
                    if lv == 0:
                        keep(h, LEVELS, ("self", h))
                    else:
                        if lv == 1:
                            wait_free(("self", h))
                        else:
                            wait_free(("level", lv - 2, h))
                        keep(h, lv - 1, ("level", lv - 1, h))
                if lv == LEVELS:
                    break
                half = 1 << lv
                pairs = lambda a: a[:, :].rearrange("p (n two l) -> p n two l", two=2, l=half)
                blocks = HG * S // (2 * half)
                dve.wait_ge(e_ready, lv + 1)
                nc.vector.tensor_tensor(pairs(z)[:, :, 0, :], pairs(kk)[:, :, 0, :], pairs(ex)[:, :, 0, :], ALU.mult)
                link(nc.vector.tensor_tensor(pairs(z)[:, :, 1, :], pairs(qf)[:, :, 1, :], pairs(ex)[:, :, 1, :],
                                             ALU.mult))
                dve.sem_inc(z_ready, 1)
                dve.sem_inc(e_used, 1)
                link(nc.vector.tensor_tensor(pairs(sfx)[:, :, 0, :], pairs(sfx)[:, :, 0, :],
                                             pairs(lf)[:, :, 1, half - 1:half].to_broadcast([P, blocks, half]),
                                             ALU.add))
                nc.vector.tensor_tensor(pairs(lf)[:, :, 1, :], pairs(lf)[:, :, 1, :],
                                        pairs(lf)[:, :, 0, half - 1:half].to_broadcast([P, blocks, half]),
                                        ALU.add).then_inc(prefix_ready, 1)
                dve.wait_ge(prefix_ready, lv + 2)
                if lv in (1, 2, 4):
                    head_norm("", tok, tok_sq, S, {1: "sa_q_gain", 2: "sa_k_gain", 4: "mem_q_gain"}[lv])
                top_keys(20 + 2 * lv, 22 + 2 * lv)
            dve.wait_ge(e_ready, LEVELS + 1)
            nc.vector.tensor_copy(e_last[:, :, :], ex[:, :].rearrange("p (h c t) -> p h c t", h=HG, t=P)[:, :, :, P - 1])
            link(nc.vector.tensor_tensor(qf[:, :], qf[:, :], ex[:, :], ALU.mult))
            dve.sem_inc(e_used, 1)
            dve.wait_ge(e_ready, LEVELS + 2)
            nc.vector.tensor_tensor(kk[:, :], kk[:, :], ex[:, :], ALU.mult).then_inc(decayed, 1)
            wait_free(("hg1", TT - 1))
            link(nc.vector.tensor_tensor(g_tok[:, :, :].rearrange("p t (h d) -> p (t h) d", d=HDK),
                                         g_tok[:, :, :].rearrange("p t (h d) -> p (t h) d", d=HDK),
                                         rows[:, ROW["hg_out_gain"]:ROW["hg_out_gain"] + HDK].unsqueeze(1)
                                         .to_broadcast([P, TT * HG, HDK]), ALU.mult))
            for c in range(TT - 1):
                ready(("state", c))
                if c == 0:
                    link(nc.vector.tensor_copy(state[:, 0, :, :], B(("state", 0))[:, :]
                                               .rearrange("p (h d) -> p h d", d=HDK)))
                else:
                    for h in range(HG):
                        ins = nc.vector.scalar_tensor_tensor(
                            out=state[:, c, h, :], in0=state[:, c - 1, h, :], scalar=e_last[:, h, c:c + 1],
                            in1=B(("state", c))[:, h * HDK:(h + 1) * HDK], op0=ALU.mult, op1=ALU.add)
                    link(ins)
                dve.sem_inc(bank_free[slot["state", c].bank], 1)
                dve.sem_inc(state_ready, 1)
            for c in range(TT):
                dve.wait_ge(squared, n["sum"] + 1)
                nc.vector.tensor_reduce(st[:, 0, HG * c:HG * (c + 1)], hg_sq[c % 2][:, :]
                                        .rearrange("p (h d) -> p h d", d=HDK), AX.X, ALU.add).then_inc(summed, 1)
                n["sum"] += 1
            dve.wait_ge(summed, n["sum"])
            link(nc.vector.tensor_scalar(st[:, 0, :], st[:, 0, :], 1.0 / HDK, EPS, ALU.mult, ALU.add))
            dve.sem_inc(heads_ms, 1)
            n["heads"] += 1
            inverse_root(HG * TT)
            for c in range(TT):
                for h in range(HG):
                    ins = nc.vector.scalar_tensor_tensor(
                        out=mix[:, c, h * HDK:(h + 1) * HDK], in0=B(("o_hg", c))[:, h * HDK:(h + 1) * HDK],
                        scalar=st[:, 2, HG * c + h:HG * c + h + 1], in1=g_tok[:, c, h * HDK:(h + 1) * HDK],
                        op0=ALU.mult, op1=ALU.mult)
                frees(("o_hg", c), ins)
            attention("mem_2", SAH * TT, None, lambda h, i: mix[:, i, 768 + h * 64:768 + (h + 1) * 64],
                      between=lambda s: top_keys(min(34 + s, 48), min(35 + s, 48)))
            attention("sa", SAH * TT, lambda h, i: sel[:, i, 0:P * (i + 1)] if i else causal[:, :],
                      lambda h, i: mix[:, i, 512 + h * 64:512 + (h + 1) * 64])
            turned("turn_mix", KT, lambda j: mo_hi[:, j, :], lambda j: mo_lo[:, j, :])
            for m in range(4):
                split_w(FIRST["w_out_2"] + m + 1)
                for j in (2 * m, 2 * m + 1):
                    ready(("w_out_2", j))
                    frees(("w_out_2", j), nc.vector.tensor_tensor(x[:, j, :], B(("w_out_2", j))[:, :], x[:, j, :],
                                                                  ALU.add))
                for j in (2 * m, 2 * m + 1):
                    low_gained(h_lo[:, j, :], x[:, j, :], "norm_ffn_2", h_hi[:, j, :], j)
                    add_squares(j == 0)
            split_w(FIRST["up_2"] + 1)
            norm_scale("ffn_2", S)
            split_w(FIRST["up_2"] + 2)
            wait_free(("spread", "ffn_2"))

            def up_2_turn(name, i=None):
                it = 0 if i is None else i + 1
                if i is not None:
                    split_w(FIRST["up_2"] + 3, i, 2)
                dve.wait_ge(prod, FT + 2 * it)
                for c in range(2):
                    ready((name, c), i)
                    normal(name, c, y[c][:, :])
                if i is not None:
                    split_w(FIRST["up_2"] + 4, i, 2)
                dve.wait_ge(a_down, FT + 2 + 2 * it)
                for c in range(2):
                    ready((name, 2 + c), i)
                    normal(name, 2 + c, y[2 + c][:, :])
                for c in range(2):
                    wait_free((name, 2 + c), i)
                    dve.wait_ge(act_gate, FT + 2 * it + (c + 1))
                    nc.vector.tensor_tensor(y[2 + c][:, :], y[2 + c][:, :], y[c][:, :], ALU.mult).then_inc(prod, 1)
                for c in range(2):
                    dve.wait_ge(a_up, FT + 2 * it + (c + 1))
                    nc.vector.tensor_tensor(a_lo[:, bass.ds(1024 * it + 512 * c, 512)], y[2 + c][:, :],
                                            a_hi[:, bass.ds(1024 * it + 512 * c, 512)].bitcast(F32), ALU.subtract
                                            ).then_inc(a_down, 1)

            up_2_turn("up_2_first")
            with dve.Fori(0, FT // 2 - 1) as i:
                up_2_turn("up_2", i)
            for g in range(4):
                for m in range(3):
                    split_w(FIRST["down_2"] + 3 * g + m + 1)
                for j in (2 * g, 2 * g + 1):
                    ready(("down_2", j % 4), j // 4)
                    frees(("down_2", j % 4), nc.vector.tensor_tensor(x[:, j, :], B(("down_2", j % 4))[:, :],
                                                                     x[:, j, :], ALU.add))

        @block.tensor
        def _(pe):
            n = {"sum": 0, "diag": 0, "heads": 0}

            def claim(key, i=None):
                if slot[key].before or i is not None:
                    pe.wait_ge(bank_free[slot[key].bank], turn(key, i))

            def done(key, ins):
                ins.then_inc(completion(key)[0], 1)

            def weights(m, i=None, per=0):
                pe.wait_ge(lo_ready, m + 1 if i is None else m + 1 + per * i)

            def product(o, lh, ll, rh, rl, first, last):
                nc.tensor.matmul(o, lh, rh, start=first, stop=False)
                nc.tensor.matmul(o, lh, rl, start=False, stop=False)
                return nc.tensor.matmul(o, ll, rh, start=False, stop=last)

            def w(m, hi, ktiles=KT):
                return (w_hi if hi else w_lo)[m % 2][:, :].rearrange("p (k c) -> p k c", k=ktiles)

            def feature_tile(o, m, c, ah, al, tokens=S, ktiles=KT, fresh=None, first=True, last=True, kk_=None):
                for kt in range(kk_ or ktiles):
                    if fresh is not None:
                        pe.wait_ge(split, fresh + kt + 1)
                    cs = slice(c * P, (c + 1) * P)
                    ins = product(o[:, 0:tokens], w(m, 1, ktiles)[:, kt, cs], w(m, 0, ktiles)[:, kt, cs], ah(kt),
                                  al(kt), first and kt == 0, last and kt == (kk_ or ktiles) - 1)
                return ins

            def token_tile(o, m, t, ah, al, lo=0, hi=COLS, fresh=None):
                ts = slice(t * P, (t + 1) * P)
                for kt in range(KT):
                    if fresh is not None:
                        pe.wait_ge(split, fresh + kt + 1)
                    ins = product(o, ah[:, kt, ts], al[:, kt, ts], w(m, 1)[:, kt, lo:hi], w(m, 0)[:, kt, lo:hi],
                                  kt == 0, kt == KT - 1)
                return ins

            H = (lambda kt: h_hi[:, kt, :], lambda kt: h_lo[:, kt, :])

            def feature_loads(name, loads, fresh=None, act=H):
                for m in range(loads):
                    weights(FIRST[name] + m)
                    for c in range(2):
                        t = 2 * m + c
                        claim((name, t))
                        ins = feature_tile(B((name, t)), FIRST[name] + m, c, *act, fresh=fresh if t == 0 else None)
                        done((name, t), ins)

            def token_loads(name, loads):
                for m in range(loads):
                    weights(FIRST[name] + m)
                    for t in range(TT):
                        key = (name, TT * m + t)
                        claim(key)
                        done(key, token_tile(B(key)[:, 0:COLS], FIRST[name] + m, t, h_hi, h_lo))

            def norm_sum(name, tokens, src=None):
                src = ssq if src is None else src
                claim(("sum", name))
                pe.wait_ge(summed, NORM_SUMS[name])
                for c in range(tokens // P):
                    ins = nc.tensor.matmul(B(("sum", name))[:, c:c + 1], src[:, c * P:(c + 1) * P], ones[:, 0:1],
                                           start=True, stop=True)
                done(("sum", name), ins)

            def norm_spread(name, tokens=S):
                n["diag"] += 1
                claim(("spread", name))
                pe.wait_ge(diag_ready, n["diag"])
                done(("spread", name), nc.tensor.matmul(B(("spread", name))[:, 0:tokens], ones[:, :],
                                                        diag[:, 0:tokens // P, :].rearrange("p c t -> p (c t)"),
                                                        start=True, stop=True))

            def together(name, first, fresh, norm_name):
                for t in range(4):
                    claim((name, t))
                for kt in range(KT):
                    pe.wait_ge(split, fresh + kt + 1)
                    for t in range(4):
                        m = first + t // 2
                        if kt == 0:
                            weights(m)
                        cs = slice(t % 2 * P, (t % 2 + 1) * P)
                        ins = product(B((name, t))[:, :], w(m, 1)[:, kt, cs], w(m, 0)[:, kt, cs], h_hi[:, kt, :],
                                      h_lo[:, kt, :], kt == 0, kt == KT - 1)
                        if kt == KT - 1:
                            done((name, t), ins)
                            if t == 1:
                                norm_sum(norm_name, S)

            def attention(kind, count, qk, vv):
                rb, tb = (row, pT) if kind in ("mem", "att") else (row_2, pT_2)
                for s in range(count + LAG + 1):
                    if kind in ("mem", "mem_2") and LAG <= s < count + LAG:
                        u_ = UNIT0[kind] + s - LAG
                        pe.wait_ge(exp_ready, u_ + 1)
                        pe.sem_inc(bank_free[slot["S", u_].bank], 1)
                    if s < count:
                        u_ = UNIT0[kind] + s
                        _, h, i, keys = UNITS[u_]
                        claim(("S", u_))
                        q_, k_ = qk(h, i, keys)
                        done(("S", u_), nc.tensor.matmul(B(("S", u_))[:, 0:keys], q_, k_, start=True, stop=True))
                    if LAG <= s < count + LAG:
                        u_ = UNIT0[kind] + s - LAG
                        keys = UNITS[u_][3]
                        claim(("T", u_))
                        pe.wait_ge(exp_ready, u_ + 1)
                        for c in range(keys // P):
                            ins = nc.tensor.transpose(B(("T", u_))[:, c * P:(c + 1) * P],
                                                      rb[u_ % NLP][:, c * P:(c + 1) * P], ident[:, :])
                        done(("T", u_), ins)
                    if s >= LAG + 1:
                        u_ = UNIT0[kind] + s - LAG - 1
                        _, h, i, keys = UNITS[u_]
                        claim(("O", u_))
                        pe.wait_ge(bank_free[slot["T", u_].bank], turn(("T", u_)) + 1)
                        for c in range(keys // P):
                            v_ = vv(h, c)
                            ins = nc.tensor.matmul(B(("O", u_))[:, 0:v_.shape[-1]], tb[u_ % 2][:, c, :], v_,
                                                   start=c == 0, stop=c == keys // P - 1)
                        done(("O", u_), ins)

            def turns(name, count, src, blocks):
                for j in range(count):
                    claim((name, j))
                    for t in range(blocks):
                        ins = nc.tensor.transpose(B((name, j))[:, t * P:(t + 1) * P], src(j, t), ident[:, :])
                    done((name, j), ins)

            def wait_all(name, keys):
                for key in keys:
                    pe.wait_ge(bank_free[slot[name, key].bank], turn((name, key)) + 1)

            pe.wait_ge(onehot_in, 32)
            pe.wait_ge(set_up, 2)
            for t in range(2):
                done(("bias", t), nc.tensor.matmul(B(("bias", t))[0:HEADS, :], relb[0:NB + 1, :],
                                                   onehot[0:NB + 1, t * 512:(t + 1) * 512], start=True, stop=True))
            pe.wait_ge(const_in, 48)
            for m in range(2):
                weights(m)
                for c in range(2):
                    key = ("mem_k", 2 * m + c)
                    claim(key)
                    done(key, feature_tile(B(key), m, c, lambda kt: mn_hi[:, kt, :], lambda kt: mn_lo[:, kt, :],
                                           tokens=M, fresh=0 if m + c == 0 else None))
            norm_sum("mem", M, ssq_mem)
            norm_spread("mem", M)
            for m in range(2):
                weights(2 + m)
                for t in range(MT):
                    key = ("mem_v", 2 * m + t)
                    claim(key)
                    done(key, token_tile(B(key)[:, 0:COLS], 2 + m, t, mn_hi, mn_lo))
            feature_loads("qm", 2, fresh=LOW_END["mem"])
            norm_sum("x", S)
            norm_spread("x")
            wait_all("mem_v", range(4))
            wait_all("qm", range(4))
            attention("mem", MHEADS * TT, lambda h, i, keys: (qm[:, h, i * P:(i + 1) * P], mk[:, h, :]),
                      lambda h, c: mv[:, c, h * MDH:(h + 1) * MDH])

            def all_read(kind, count):
                for w_ in range(UNIT0[kind] + count - 2, UNIT0[kind] + count):
                    pe.wait_ge(bank_free[slot["O", w_].bank], turn(("O", w_)) + 1)

            all_read("mem", MHEADS * TT)
            turns("turn_mem", 4, lambda j, t: o_tok[:, t, j * P:(j + 1) * P], TT)
            feature_loads("q", 2)
            feature_loads("k", 2)
            token_loads("v", 2)
            wait_all("k", range(4))
            wait_all("v", range(4, 8))

            def head64(a, h, lo, hi):
                return a[64 * (h % 2):64 * (h % 2) + 64, h // 2, lo:hi]

            attention("att", HEADS * TT,
                      lambda h, i, keys: (head64(q, h, i * P, (i + 1) * P), head64(k, h, 0, keys)),
                      lambda h, c: v[:, c, h * DH:(h + 1) * DH])
            all_read("att", HEADS * TT)
            turns("turn_att", 4, lambda j, t: o_tok[:, t, j * P:(j + 1) * P], TT)
            feature_loads("cc", 2)
            feature_loads("cv", 2)
            feature_loads("cb", 2)
            pe.wait_ge(split, LOW_END["conv"])
            with pe.Fori(0, 3) as i:
                for half in range(2):
                    for m in range(3):
                        ld = FIRST["branch"] + 3 * half + m
                        weights(ld, i, 6)
                        for c in range(2 if m < 2 else 4):
                            key = ("branch", 8 * half + 2 * m + c)
                            claim(key, i)
                            if m < 2:
                                ins = feature_tile(B(key), ld, c, *H)
                            else:
                                ins = feature_tile(
                                    B(key), ld, c, lambda kt: branch(br_hi, i, kt), lambda kt: branch(br_lo, i, kt),
                                    ktiles=4)
                            done(key, ins)
            for m in range(4):
                weights(FIRST["w_out"] + m)
                for c in range(2):
                    key = ("w_out", 2 * m + c)
                    claim(key)
                    done(key, feature_tile(B(key), FIRST["w_out"] + m, c, lambda kt: br_hi[:, kt, :],
                                           lambda kt: br_lo[:, kt, :],
                                           fresh=LOW_END["conv"] if m + c == 0 else None))
            norm_sum("mix", S)
            norm_spread("mix")
            together("up_first", FIRST["up"], LOW_END["merged"], "ffn")
            norm_spread("ffn")

            def up(name):
                with pe.Fori(0, FT // 2 - 1) as i:
                    for m in range(2):
                        weights(FIRST[name] + 2 + m, i, 2)
                        for c in range(2):
                            claim((name, 2 * m + c), i)
                            done((name, 2 * m + c), feature_tile(B((name, 2 * m + c)), FIRST[name] + m, c, *H))

            def down_(name, hidden):
                with pe.Fori(0, 2) as i:
                    for g in range(2):
                        for c in range(2):
                            claim((name, 2 * g + c), i)
                        for m in range(3):
                            ld = FIRST[name] + 3 * g + m
                            weights(ld, i, 6)
                            pe.wait_ge(a_down, hidden + min(8 * m + 8, FT))
                            for c in range(2):
                                ins = feature_tile(
                                    B((name, 2 * g + c)), ld, c,
                                    lambda kt: a_hi[:, (8 * m + kt) * S:(8 * m + kt + 1) * S],
                                    lambda kt: a_lo[:, (8 * m + kt) * S:(8 * m + kt + 1) * S],
                                    first=m == 0, last=m == 2, kk_=min(8, FT - 8 * m))
                                if m == 2:
                                    done((name, 2 * g + c), ins)
                            if m < 2:
                                ins.then_inc(w_used, 1)

            up("up")
            down_("down", 2)
            norm_sum("mem_2", M, ssq_mem)
            norm_sum("down", S)
            norm_spread("down")
            for m in range(2):
                weights(FIRST["mem_kv_2"] + m)
                for t in range(MT):
                    key = ("mem_kv_2", 2 * m + t)
                    claim(key)
                    done(key, token_tile(B(key)[:, 0:COLS], FIRST["mem_kv_2"] + m, t, mn2_hi, mn2_lo))
            together("iq", FIRST["iq"], LOW_END["mem_2"], "x_2")
            norm_spread("x_2")

            def turn_heads(name, src, tokens):
                n["heads"] += 1
                pe.wait_ge(heads_norm, n["heads"])
                turns(name, 2, lambda f, t: src[:, t, f * P:(f + 1) * P], tokens // P)

            ld = FIRST["idx"]
            weights(ld)
            claim(("ik", 0))
            done(("ik", 0), feature_tile(B(("ik", 0)), ld, 0, *H))
            claim(("iwT", 0))
            for kt in range(KT):
                ins = product(B(("iwT", 0))[0:IDXH, :], w(ld, 1)[:, kt, P:P + IDXH], w(ld, 0)[:, kt, P:P + IDXH],
                              h_hi[:, kt, :], h_lo[:, kt, :], kt == 0, kt == KT - 1)
            done(("iwT", 0), ins)
            claim(("iw", 0))
            pe.wait_ge(bank_free[slot["iwT", 0].bank], turn(("iwT", 0)) + 1)
            for t in range(TT):
                ins = nc.tensor.transpose(B(("iw", 0))[:, t * IDXH:(t + 1) * IDXH],
                                          iwT[0:IDXH, t * P:(t + 1) * P], ident[0:IDXH, 0:IDXH])
            done(("iw", 0), ins)
            turn_heads("turn_km", km_tok, M)
            wait_all("iq", range(4))
            wait_all("ik", range(1))
            for w_, (i, h) in enumerate(IDX):
                claim(("idx", w_))
                done(("idx", w_), nc.tensor.matmul(B(("idx", w_))[:, 0:P * (i + 1)], iq[:, h // 2, i * P:(i + 1) * P],
                                                   ik[h % 2][:, 0:P * (i + 1)], start=True, stop=True))
            feature_loads("hf", 2)
            feature_loads("hq", 2)
            pe.wait_ge(hq_ready, 4)

            def load_tokens(name, ld):
                weights(ld)
                for t in range(TT):
                    claim((name, t))
                    done((name, t), token_tile(B((name, t))[:, 0:COLS], ld, t, h_hi, h_lo))

            def chunk(a, h, c):
                return a[:, h * S + c * P:h * S + (c + 1) * P]

            for h in range(HG):
                claim(("self", h))
                for c in range(TT):
                    ins = nc.tensor.matmul(B(("self", h))[:, c * P:(c + 1) * P], chunk(kk, h, c), chunk(qf, h, c),
                                           start=True, stop=True)
                done(("self", h), ins)
            for lv in range(LEVELS):
                load_tokens(("sq", "sk", "sv", "mq", "hg0", "hg1", "hi0")[lv], FIRST["sq"] + lv)
                if lv in (1, 2, 4):
                    turn_heads({1: "turn_sq", 2: "turn_sk", 4: "turn_mq"}[lv], tok, S)
                pe.wait_ge(z_ready, lv + 1)
                for h in range(HG):
                    claim(("level", lv, h))
                    for c in range(TT):
                        ins = nc.tensor.matmul(B(("level", lv, h))[:, c * P:(c + 1) * P], chunk(z, h, c),
                                               chunk(z, h, c), start=True, stop=True)
                    done(("level", lv, h), ins)
            load_tokens("hi1", FIRST["hi"] + 1)
            pe.wait_ge(decayed, 1)
            turns("turn_kd", TT - 1, lambda c, h: chunk(kk, h, c), HG)
            for c in range(TT - 1):
                claim(("state", c))
                pe.wait_ge(bank_free[slot["turn_kd", c].bank], turn(("turn_kd", c)) + 1)
                for h in range(HG):
                    ins = nc.tensor.matmul(B(("state", c))[:, h * HDK:(h + 1) * HDK], kT[:, c, h, :],
                                           v_hg[:, c, h * HDK:(h + 1) * HDK], start=True, stop=True)
                done(("state", c), ins)
            for c in range(TT):
                claim(("o_hg", c))
                if c:
                    pe.wait_ge(state_ready, c)
                for h in range(HG):
                    o = B(("o_hg", c))[:, h * HDK:(h + 1) * HDK]
                    ins = nc.tensor.matmul(o, aT[:, h, c * P:(c + 1) * P], v_hg[:, c, h * HDK:(h + 1) * HDK],
                                           start=True, stop=c == 0)
                    if c:
                        ins = nc.tensor.matmul(o, chunk(qf, h, c), state[:, c - 1, h, :], start=False, stop=True)
                done(("o_hg", c), ins)
            attention("mem_2", SAH * TT,
                      lambda h, i, keys: (head64(mqT, h, i * P, (i + 1) * P), head64(kmT, h, 0, M)),
                      lambda h, c: vm[:, c, h * 64:(h + 1) * 64])
            attention("sa", SAH * TT,
                      lambda h, i, keys: (head64(sqT, h, i * P, (i + 1) * P), head64(skT, h, 0, keys)),
                      lambda h, c: sv[:, c, h * 64:(h + 1) * 64])
            all_read("sa", SAH * TT)
            turns("turn_mix", KT, lambda j, t: mix[:, t, j * P:(j + 1) * P], TT)
            feature_loads("w_out_2", 4, fresh=LOW_END["x_2"],
                          act=(lambda kt: mo_hi[:, kt, :], lambda kt: mo_lo[:, kt, :]))
            together("up_2_first", FIRST["up_2"], LOW_END["turn_mix"], "ffn_2")
            norm_spread("ffn_2")
            up("up_2")
            down_("down_2", FT + 2)


def branch(a, i, kt):
    return a[:, :, :].rearrange("p j t -> p (j t)")[:, bass.ds(4 * S * i + kt * S, S)]


def bucket_onehot():
    dist = np.arange(1024) - (S - 1)
    n = np.maximum(dist, NB_EXACT).astype(np.float32)
    large = NB_EXACT + (np.log(n / np.float32(NB_EXACT)) / np.float32(math.log(NB_DIST / NB_EXACT))
                        * np.float32(NB - NB_EXACT)).astype(np.int32)
    bucket = np.where(dist < NB_EXACT, dist, np.minimum(large, NB - 1))
    bucket = np.where(dist < 0, NB, bucket)
    return (bucket[None, :] == np.arange(NB + 1)[:, None]).astype(np.float32)


def level_masks():
    s, t = np.arange(P)[:, None], np.arange(P)[None, :]
    out = np.zeros((P, LEVELS + 1, P), np.int32)
    for lv in range(LEVELS):
        out[:, lv, :] = (s >> lv + 1 == t >> lv + 1) & (s >> lv & 1 == 0) & (t >> lv & 1 == 1)
    out[:, LEVELS, :] = s == t
    return out


def packed(w, cols=COLS, ktiles=KT):
    return w.reshape(ktiles, P, -1, cols).transpose(2, 1, 0, 3).reshape(-1, P, ktiles * cols)


def lay_out_weights(a):
    w_in, w_in2 = a["w_in"][0], a["w_in_2"][0]
    o = np.cumsum([0, 512, 512, 512, 512, 512, 512, 512, 1024, 1024, 1024])
    cb, cc, cv, q, k, v, qm, ga, gb, gc = (packed(w_in[:, o[j]:o[j + 1]]) for j in range(10))
    branches = []
    for g, w in ((ga, a["w_conv_out"]), (gb, a["w_attn_out"]), (gc, a["w_mem_out"])):
        w = packed(w[0], 512, 4)
        branches += [g[0:2], w[0:1], g[2:4], w[1:2]]

    def up(w):
        a_, g_ = packed(w[:, :DFF]), packed(w[:, DFF:])
        return np.stack([a_, g_], 1).reshape(2 * DFF // COLS, P, SLOT)

    def down(w):
        w = np.pad(w, ((0, 3 * 8 * P - DFF), (0, 0))).reshape(3, 8, P, 4, COLS)
        return w.transpose(3, 0, 2, 1, 4).reshape(12, P, SLOT)

    o = np.cumsum([0, 512, 512, 512, 512, 256, 256, 256, 512, 64, 8, 256])
    hq, hf, hi, hg, sq, sk, sv, iq, ik, iw, mq = (w_in2[:, o[j]:o[j + 1]] for j in range(11))
    idx = packed(np.pad(np.concatenate([ik, ik, iw], 1), ((0, 0), (0, COLS - 136))))
    parts = [packed(a["w_mem_kv"][0]), qm, q, k, v, cc, cv, cb, *branches, packed(a["w_out"][0]),
             up(a["w_up"][0]), down(a["w_down"][0]), packed(a["w_mem_kv_2"][0]), packed(iq), idx, packed(hf),
             packed(hq), packed(sq), packed(sk), packed(sv), packed(mq), packed(hg), packed(hi),
             packed(a["w_out_2"][0]), up(a["w_ffn_in_2"][0]), down(a["w_ffn_out_2"][0])]
    return np.ascontiguousarray(np.concatenate(parts, 0))


def columns(a):
    col = lambda x: x.reshape(-1, P).T
    names = ["g_pre_mix", "g_post_mix", "g_pre_ffn", "g_post_ffn", "g_mem", "norm_mix_2", "norm_mem_2",
             "norm_ffn_2", "b_gate", "conv_mix_w", "ffn_conv_w", "ffn_conv_b"]
    return np.ascontiguousarray(np.concatenate([col(a[x]) for x in names], 1))


def kernel(**inputs):
    import concourse.bacc as bacc
    from concourse.bass_utils import run_bass_kernel_spmd

    a = {name: np.asarray(value) for name, value in inputs.items()}
    gains = np.concatenate([a[x + "_2"].reshape(-1) for x in ROW])
    arrays = {
        "weights": lay_out_weights(a),
        "xT": np.ascontiguousarray(a["x"][0].T),
        "memT": np.ascontiguousarray(a["mem"][0].T),
        "mem2T": np.ascontiguousarray(a["mem_2"][0].T),
        "vec": columns(a),
        "rows": np.ascontiguousarray(np.broadcast_to(gains, (P, NROW))),
        "rel_bias": a["rel_bias"],
        "ident": np.eye(P, dtype=np.float32),
        "onehot": bucket_onehot(),
        "masks": level_masks(),
        "causal": np.where(np.arange(P)[None, :] <= np.arange(P)[:, None], 0, NEG).astype(np.float32),
    }
    nc = bacc.Bacc("TRN2", target_bir_lowering=False, num_devices=1)
    A = {name: nc.dram_tensor(name, value.shape, mybir.dt.from_np(value.dtype), kind="ExternalInput").ap()
         for name, value in arrays.items()}
    A["bias_scratch"] = nc.dram_tensor("bias_scratch", (HEADS, 1024), F32, kind="Internal").ap()
    out = nc.dram_tensor("outT", (D, S), F32, kind="ExternalOutput").ap()
    build(nc, A, out)
    r = run_bass_kernel_spmd(nc, [arrays], core_ids=[0])
    return np.ascontiguousarray(r.results[0]["outT"].T)[None]
```

```python
import math
from contextlib import ExitStack

import numpy as np

import concourse.bass as bass
from concourse import mybir

F32 = mybir.dt.float32
F32R = mybir.dt.float32r
U8 = mybir.dt.uint8
ACT = mybir.ActivationFunctionType
ALU = mybir.AluOpType
AX = mybir.AxisListType

P = 128
D = 1024
KT = D // P
S = 512
TT = S // P
M = 256
MT = M // P
SLOT = 2048
COLS = SLOT // KT
DFF = 2816
FT = DFF // P
HEADS, DH = 8, 64
MHEADS, MDH = 4, 128
NB, NB_EXACT, NB_DIST = 32, 16, 1024
HG, HDK = 4, 128
SAH = 4
IDXH = 8
TOPK = min(256, S // 4)
NEG = -1e30
TAKEN = -3e38
EPS = 1e-6
LEVELS = 7

VEC = {}
_at = 0
for _name, _n in [("g_pre_mix", 8), ("g_post_mix", 8), ("g_pre_ffn", 8), ("g_post_ffn", 8), ("g_mem", 8),
                  ("norm_mix_2", 8), ("norm_mem_2", 8), ("norm_ffn_2", 8), ("b_gate", 24),
                  ("conv_mix_w", 12), ("ffn_conv_w", 132), ("ffn_conv_b", 44),
                  ("sa_q_gain", 1), ("mem_q_gain", 1), ("sa_k_gain", 1), ("mem_k_gain", 1)]:
    VEC[_name] = _at
    _at += _n
NVEC = _at
ROW = {"hg_out_gain": 0}
NROW = 128

LOADS = [("mem_kv", 4), ("qm", 2), ("v", 2), ("q", 2), ("k", 2), ("cc", 2), ("cv", 2), ("cb", 2),
         ("branch", 18), ("w_out", 4), ("up", 22), ("down", 12), ("mem_kv_2", 2), ("iq", 2), ("idx", 1),
         ("hf", 2), ("hq", 2), ("sq", 1), ("sk", 1), ("sv", 1), ("mq", 1), ("hg", 2), ("hi", 2),
         ("w_out_2", 4), ("up_2", 22), ("down_2", 12)]
FIRST = {}
_at = 0
for _name, _n in LOADS:
    FIRST[_name] = _at
    _at += _n
NLOADS = _at

UNITS = ([("mem", h, i, M) for h in range(MHEADS) for i in range(TT)]
         + [("att", h, i, P * (i + 1)) for h in range(HEADS) for i in range(TT)]
         + [("mem_2", h, i, M) for h in range(SAH) for i in range(TT)]
         + [("sa", h, i, P * (i + 1)) for h in range(SAH) for i in range(TT)])
UNIT0 = {"mem": 0, "att": 16, "mem_2": 48, "sa": 64}
IDX = [(i, h) for i in range(1, TT) for h in range(IDXH)]
S_BANKS, T_BANKS, O_BANKS = ((4, 5, 0, 1), (4, 5, 2, 3)), ((6, 6), (6, 0)), ((7, 7), (7, 1))
NLP = 4
LAG = 3
CONV_TILE = [(KT * t + KT - 1) // 3 + 1 for t in range(12)]
CONV_STEPS = CONV_TILE[1:10:2]


LOWS = [("mem", KT), ("x", KT), ("turn_mem", 4), ("turn_att", 4), ("conv", 4), ("merged", KT), ("ffn", KT),
        ("mem_2", KT), ("x_2", KT), ("turn_mix", KT), ("ffn_2", KT)]
LOW_END = {}
_at = 0
for _name, _n in LOWS:
    _at += _n
    LOW_END[_name] = _at
NORM_SUMS = {"mem": 8, "x": 16, "mix": 24, "ffn": 32, "down": 48, "x_2": 56, "ffn_2": 68}
IW_SCALE = IDXH ** -0.5 * 64 ** -0.5


class Slot:

    def __init__(self, bank, before, ready, load, per=0, ready_per=0):
        self.bank, self.before, self.ready, self.load = bank, before, ready, load
        self.per, self.ready_per = per, ready_per


def plan_banks():
    used, told = [0] * 8, [0] * 8
    slot = {}

    def use(key, bank, load=None):
        if load is None:
            told[bank] += 1
        slot[key] = Slot(bank, used[bank], told[bank] if load is None else load + 1, load)
        used[bank] += 1

    def tiles(name, n, banks=(0, 1, 2, 3), first=None, per=1):
        for t in range(n):
            last = first is not None and t % per == per - 1
            use((name, t), banks[t % len(banks)], first + t // per if last else None)

    def together(name, first):
        for t in range(4):
            use((name, t), (4, 5, 2, 3)[t], {1: first, 3: first + 1}.get(t))

    def loop(name, banks, times, ends, loads):
        own = [b for c, b in enumerate(banks) if c not in ends]
        for c, b in enumerate(banks):
            if c in ends:
                slot[name, c] = Slot(b, used[b] + banks[:c].count(b), ends[c] + 1, ends[c], banks.count(b), loads)
            else:
                earlier = [x for e, x in enumerate(banks[:c]) if e not in ends].count(b)
                slot[name, c] = Slot(b, used[b] + banks[:c].count(b), told[b] + earlier + 1, None, banks.count(b),
                                     own.count(b))
        for b in banks:
            used[b] += times
        for b in own:
            told[b] += times

    def norm(k):
        use(("sum", k), 7)
        use(("spread", k), 6)

    def attention(kind, n):
        for w in range(UNIT0[kind], UNIT0[kind] + n):
            second = kind in ("mem_2", "sa")
            use(("S", w), S_BANKS[second][w % 4])
            use(("T", w), T_BANKS[second][w % 2])
            use(("O", w), O_BANKS[second][w % 2])

    tiles("mem_k", 4, first=0, per=2)
    norm("mem")
    tiles("mem_v", 4, (4, 5, 2, 3), first=2, per=2)
    tiles("qm", 4, first=FIRST["qm"], per=2)
    tiles("bias", 2, (4, 5))
    norm("x")
    attention("mem", MHEADS * TT)
    tiles("v", 8, (2, 3), first=FIRST["v"], per=4)
    tiles("turn_mem", 4)
    tiles("q", 4, first=FIRST["q"], per=2)
    tiles("k", 4, first=FIRST["k"], per=2)
    attention("att", HEADS * TT)
    tiles("cc", 4, (2, 3), first=FIRST["cc"], per=2)
    tiles("cv", 4, (2, 3), first=FIRST["cv"], per=2)
    tiles("cb", 4, (2, 3), first=FIRST["cb"], per=2)
    tiles("turn_att", 4)
    loop("branch", [0, 1, 2, 3, 4, 5, 6, 7] * 2, 3,
         {c: FIRST["branch"] + m for m, c in enumerate((1, 3, 7, 9, 11, 15))}, 6)
    tiles("w_out", KT, first=FIRST["w_out"], per=2)
    norm("mix")
    together("up_first", FIRST["up"])
    norm("ffn")
    loop("up", [0, 1, 2, 3], FT // 2 - 1, {1: FIRST["up"] + 2, 3: FIRST["up"] + 3}, 2)
    loop("down", [0, 1, 2, 3], 2, {1: FIRST["down"] + 2, 3: FIRST["down"] + 5}, 6)
    norm("down")
    tiles("mem_kv_2", 4, first=FIRST["mem_kv_2"], per=2)
    together("iq", FIRST["iq"])
    norm("x_2")
    tiles("ik", 1)
    use(("iwT", 0), 1, FIRST["idx"])
    use(("iw", 0), 2)
    tiles("turn_km", 2, (4, 5))
    for w in range(len(IDX)):
        use(("idx", w), 4 + w % 4)
    tiles("hf", 4, first=FIRST["hf"], per=2)
    tiles("hq", 4, first=FIRST["hq"], per=2)
    tiles("self", HG, (4, 5, 6, 7))
    for lv in range(LEVELS):
        if lv < 4:
            tiles(("sq", "sk", "sv", "mq")[lv], 4, first=FIRST[("sq", "sk", "sv", "mq")[lv]], per=4)
        elif lv < 6:
            tiles(f"hg{lv - 4}", 4, first=FIRST["hg"] + lv - 4, per=4)
        else:
            tiles("hi0", 4, first=FIRST["hi"], per=4)
        if 1 <= lv <= 4 and lv != 3:
            tiles({1: "turn_sq", 2: "turn_sk", 4: "turn_mq"}[lv], 2, (4, 5))
        for h in range(HG):
            use(("level", lv, h), 4 + h)
    tiles("hi1", 4, first=FIRST["hi"] + 1, per=4)
    tiles("turn_kd", TT - 1, (4, 5, 6))
    tiles("state", TT - 1, (4, 5, 6))
    tiles("o_hg", TT)
    attention("mem_2", SAH * TT)
    attention("sa", SAH * TT)
    tiles("turn_mix", KT)
    tiles("w_out_2", KT, first=FIRST["w_out_2"], per=2)
    together("up_2_first", FIRST["up_2"])
    norm("ffn_2")
    loop("up_2", [0, 1, 2, 3], FT // 2 - 1, {1: FIRST["up_2"] + 2, 3: FIRST["up_2"] + 3}, 2)
    loop("down_2", [0, 1, 2, 3], 2, {1: FIRST["down_2"] + 2, 3: FIRST["down_2"] + 5}, 6)
    return slot


class Chain:

    def __init__(self, engine, sem):
        self.engine, self.sem, self.n, self.add = engine, sem, 0, 0

    def __call__(self, ins):
        ins.then_inc(self.sem, 1)
        self.n += 1
        self.engine.wait_ge(self.sem, self.n + self.add)

    def enter(self, i, per):
        self.start, self.per, self.add = self.n, per, i * per

    def leave(self, times):
        assert self.n - self.start == self.per, (self.n - self.start, self.per)
        self.n += self.per * (times - 1)
        self.add = 0


def build(nc, A, out):
    slot = plan_banks()
    ctx = ExitStack()
    with ctx:
        base = (nc.sbuf_base + 63) // 64 * 64
        K = 1024

        def at(name, offset, shape, dt=F32):
            return nc.alloc_sbuf_tensor_at(name, [P, *shape], dt, offset=base + offset)

        x = at("x", 0, [KT, S])
        h_hi = at("h_hi", 16 * K, [KT, S], F32R)
        h_lo = at("h_lo", 32 * K, [KT, S], F32R)
        raw = [at(f"raw{s}", (48 + 8 * s) * K, [SLOT]) for s in range(2)]
        w_hi = [at(f"w_hi{s}", (64 + 8 * s) * K, [SLOT], F32R) for s in range(2)]
        w_lo = [at(f"w_lo{s}", (80 + 8 * s) * K, [SLOT], F32R) for s in range(2)]
        ssq = at("ssq", 96 * K, [S])
        square = [at(f"square{s}", (98 + 2 * s) * K, [S]) for s in range(2)]
        tap = [at(f"tap{s}", (98 + 2 * s) * K, [S]) for s in range(2)]
        diag = at("diag", 102 * K, [TT, P])
        ssq_mem = at("ssq_mem", 102 * K, [M])
        small = 104 * K
        vec = at("vec", small, [NVEC])
        rows = at("rows", small + 1280, [NROW])
        ident = at("ident", small + 2816, [P])
        ones = at("ones", small + 3328, [P])
        st = at("st", small + 3840, [6, 16])
        mx = at("mx", small + 4224, [8, 4])
        AR = small + 4352

        rms = at("rms", AR + 96 * K, [S])

        br_hi = at("br_hi", AR, [3 * 4, S], F32R)
        br_lo = at("br_lo", AR + 24 * K, [3 * 4, S], F32R)
        memT = at("memT", AR + 48 * K, [KT, M])
        mn_hi = at("mn_hi", AR + 72 * K, [KT, M], F32R)
        mn_lo = at("mn_lo", AR + 80 * K, [KT, M], F32R)
        qm = at("qm", AR + 48 * K, [4, S])
        mk = at("mk", AR + 56 * K, [4, M])
        mv = at("mv", AR + 60 * K, [MT, S])
        q = at("q", AR + 48 * K, [4, S])
        k = at("k", AR + 56 * K, [4, S])
        v = at("v", AR + 64 * K, [TT, S])
        o_tok = at("o_tok", AR + 72 * K, [TT, S])
        row = [at(f"row{s}", AR + (80 + 2 * s) * K, [S]) for s in range(NLP)]
        pT = [at(f"pT{s}", AR + (88 + 2 * s) * K, [TT, P]) for s in range(2)]
        rms_mem = at("rms_mem", AR + 92 * K, [M])
        onehot = at("onehot", AR + 8 * K, [1024])
        relb = at("relb", AR + 12 * K, [HEADS])
        bias_row = at("bias_row", AR + 16 * K, [1024])
        toep = [at(f"toep{s}", AR + 24 * K * s, [2, 896]) for s in range(2)]
        cc = at("cc", AR + 8 * K, [4, S])
        u = at("u", AR + 32 * K, [4, S])
        cy = at("cy", 96 * K, [4, S])
        gate = at("gate", AR + 48 * K, [4, S])
        merged = at("merged", AR + 56 * K, [KT, S])
        part = [at(f"part{s}", AR + (88 + 2 * s) * K, [S]) for s in range(2)]
        mixed = at("mixed", AR + 72 * K, [KT, S])
        a_hi = at("a_hi", AR, [FT * S], F32R)
        a_lo = at("a_lo", AR + 44 * K, [FT * S], F32R)
        y = [at(f"y{s}", AR + (88 + 2 * s) * K, [S]) for s in range(4)]
        down = at("down", 16 * K, [KT * S])
        mem2T = at("mem2T", 32 * K, [KT, M])
        mn2_hi = at("mn2_hi", 40 * K, [KT, M], F32R)
        mn2_lo = at("mn2_lo", AR + 88 * K, [KT, M], F32R)
        mix = at("mix", AR, [TT, D])
        g_tok = at("g_tok", AR + 16 * K, [TT, S])
        abs_z = at("abs_z", AR + 16 * K, [HG * S])
        km_tok = at("km_tok", AR + 24 * K, [MT, M])
        km_sq = at("km_sq", AR + 40 * K, [MT, M])
        kmT = at("kmT", AR + 26 * K, [2, M])
        vm = at("vm", AR + 28 * K, [MT, M])
        masks = at("masks", AR + 30 * K, [LEVELS + 1, P], U8)
        masks_in = at("masks_in", AR + 48 * K, [LEVELS + 1, P], mybir.dt.int32)
        causal = at("causal", AR + 31 * K, [P])
        iw = at("iw", AR + 31 * K + 512, [TT, IDXH])
        e_last = at("e_last", AR + 31 * K + 640, [HG, TT])
        iq = at("iq", AR + 32 * K, [4, S])
        v_hg = at("v_hg", AR + 32 * K, [TT, S])
        ik = [at(f"ik{s}", AR + (40 + 2 * s) * K, [S]) for s in range(2)]
        relu = [at(f"relu{s}", AR + (44 + 2 * s) * K, [S]) for s in range(2)]
        iwT = at("iwT", AR + 16 * K, [S])
        tok = at("tok", AR + 40 * K, [TT, M])
        tok_sq = at("tok_sq", AR + 44 * K, [TT, M])
        state = at("state", AR + 40 * K, [TT - 1, HG, HDK])
        sel = at("sel", AR + 48 * K, [TT, S])
        sqT = at("sqT", AR + 56 * K, [2, S])
        skT = at("skT", AR + 60 * K, [2, S])
        mqT = at("mqT", AR + 64 * K, [2, S])
        sv = at("sv", AR + 68 * K, [TT, M])
        lf = at("lf", AR + 72 * K, [HG * S])
        kk = at("kk", AR + 80 * K, [HG * S])
        qf = at("qf", AR + 88 * K, [HG * S])
        sfx = at("sfx", AR, [HG * S])
        ex = at("ex", AR + 8 * K, [HG * S])
        z = at("z", AR + 32 * K, [HG * S])
        kT = at("kT", AR, [TT - 1, HG, HDK])
        hg_sq = [at(f"hg_sq{s}", AR + (72 + 2 * s) * K, [S]) for s in range(2)]
        mo_hi = at("mo_hi", AR + 16 * K, [KT, S], F32R)
        mo_lo = at("mo_lo", AR + 72 * K, [KT, S], F32R)
        aT = at("aT", 96 * K, [HG, TT * P])
        row_2 = [at(f"row_2{s}", (16 + 2 * s) * K, [S]) for s in range(NLP)]
        pT_2 = [at(f"pT_2{s}", (24 + 2 * s) * K, [TT, P]) for s in range(2)]
        assert base + AR + 98 * K <= nc.sbuf_usable_end, (base, AR, nc.sbuf_usable_end)

        bank = [ctx.enter_context(nc.psum_tensor(f"bank{b}", [P, 512], F32)) for b in range(8)]

        def sem(name):
            return ctx.enter_context(nc.semaphore(name))

        raw_full = [sem(f"raw_full{s}") for s in range(2)]
        hi_ready = sem("hi_ready")
        lo_ready = sem("lo_ready")
        w_used = sem("w_used")
        bank_ready = [sem(f"bank_ready{b}") for b in range(8)]
        bank_free = [sem(f"bank_free{b}") for b in range(8)]
        mem_in, x_in, vec_in, const_in, onehot_in = (sem(x_) for x_ in ("mem_in", "x_in", "vec_in", "const_in",
                                                                        "onehot_in"))
        mem2_in, mask_in = sem("mem2_in"), sem("mask_in")
        set_up = sem("set_up")
        act_step, dve_step = sem("act_step"), sem("dve_step")
        squared = sem("squared")
        summed = sem("summed")
        root_ready = sem("root_ready")
        diag_ready = sem("diag_ready")
        gated = sem("gated")
        conv_done = sem("conv_done")
        rounded = sem("rounded")
        split = sem("split")
        neg_max = sem("neg_max")
        exp_ready = sem("exp_ready")
        bias_saved = sem("bias_saved")
        toep_in = [sem("toep_in0"), sem("toep_in1")]
        merge_add = sem("merge_add")
        x_ready = sem("x_ready")
        seed = sem("seed")
        act_gate = sem("act_gate")
        prod = sem("prod")
        a_up = sem("a_up")
        a_down = sem("a_down")
        relu_used = sem("relu_used")
        heads_sq = sem("heads_sq")
        heads_ms = sem("heads_ms")
        heads_norm = sem("heads_norm")
        log_in, log_ready, log_used = sem("log_in"), sem("log_ready"), sem("log_used")
        hq_ready = sem("hq_ready")
        rms_col = sem("rms_col")
        e_ready, e_used, z_ready, prefix_ready = sem("e_ready"), sem("e_used"), sem("z_ready"), sem("prefix_ready")
        suffix_ready = sem("suffix_ready")
        decayed, state_ready = sem("decayed"), sem("state_ready")
        stored = sem("stored")

        block = ctx.enter_context(nc.Block())

        def vcol(name, j):
            return vec[:, VEC[name] + j:VEC[name] + j + 1]

        def turn(key, i=None):
            return slot[key].before if i is None else slot[key].before + slot[key].per * i

        def completion(key, i=None):
            s_ = slot[key]
            value = s_.ready if i is None else s_.ready + s_.ready_per * i
            return (bank_ready[s_.bank] if s_.load is None else w_used), value

        def B(key):
            return bank[slot[key].bank]

        @block.sync
        def _(sp):
            def load(n):
                sp.dma_start(raw[n % 2][:, :], A["weights"][n, :, :]).then_inc(raw_full[n % 2], 16)

            def stream(first, last):
                if first % 2:
                    sp.wait_ge(lo_ready, first - 1)
                    load(first)
                    first += 1
                turns = (last - first) // 2
                with sp.Fori(0, turns) as i:
                    for c in range(2):
                        sp.wait_ge(lo_ready, first + c - 1 + 2 * i)
                        sp.dma_start(raw[c][:, :], A["weights"][bass.ds(first + c + 2 * i, 1), :, :]
                                     .rearrange("n p c -> p (n c)")).then_inc(raw_full[c], 16)
                if (last - first) % 2:
                    sp.wait_ge(lo_ready, last - 2)
                    load(last - 1)

            def toeplitz(pair):
                if pair >= 2:
                    sp.wait_ge(neg_max, UNIT0["att"] + 2 * TT * (pair - 1))
                src = A["bias_scratch"]
                for j in range(2):
                    sp.dma_start(toep[pair % 2][:, j, :],
                                 bass.AP(src.tensor, (2 * pair + j) * 1024, [[1, P], [1, 896]])
                                 ).then_inc(toep_in[pair % 2], 16)

            sp.dma_start(memT[:, :, :], A["memT"].rearrange("(k p) t -> p k t", p=P)).then_inc(mem_in, 16)
            sp.dma_start(vec[:, :], A["vec"]).then_inc(vec_in, 16)
            load(0)
            load(1)
            sp.dma_start(x[:, :, :], A["xT"].rearrange("(k p) t -> p k t", p=P)).then_inc(x_in, 16)
            sp.dma_start(rows[:, :], A["rows"]).then_inc(const_in, 16)
            sp.dma_start(ident[:, :], A["ident"]).then_inc(const_in, 16)
            sp.dma_start(onehot[0:NB + 1, :], A["onehot"]).then_inc(onehot_in, 16)
            sp.dma_start(relb[0:NB, :], A["rel_bias"]).then_inc(onehot_in, 16)
            stream(2, FIRST["v"] + 2)
            sp.wait_ge(bank_free[slot["bias", 1].bank], turn(("bias", 1)) + 1)
            sp.dma_start(A["bias_scratch"], bias_row[0:HEADS, :]).then_inc(bias_saved, 16)
            sp.wait_ge(bias_saved, 16)
            toeplitz(0)
            toeplitz(1)
            stream(FIRST["v"] + 2, FIRST["cb"])
            toeplitz(2)
            stream(FIRST["cb"], FIRST["branch"])
            toeplitz(3)
            stream(FIRST["branch"], FIRST["down"] + 2)
            sp.wait_ge(w_used, FIRST["down"])
            sp.dma_start(mem2T[:, :, :], A["mem2T"].rearrange("(k p) t -> p k t", p=P)).then_inc(mem2_in, 16)
            stream(FIRST["down"] + 2, FIRST["mem_kv_2"] + 2)
            sp.wait_ge(w_used, FIRST["mem_kv_2"])
            sp.dma_start(masks_in[:, :, :], A["masks"]).then_inc(mask_in, 16)
            sp.dma_start(causal[:, :], A["causal"]).then_inc(mask_in, 16)
            stream(FIRST["mem_kv_2"] + 2, NLOADS)
            for j in range(KT):
                sp.wait_ge(bank_free[j % 4], turn(("down_2", j % 4), j // 4) + 1)
                sp.dma_start(out.rearrange("(k p) t -> k p t", p=P)[j, :, :], x[:, j, :]).then_inc(stored, 16)
            sp.wait_ge(stored, 16 * KT)

        @block.gpsimd
        def _(pool):
            nc.gpsimd.memset(ones[:, :], 1.0).then_inc(set_up, 1)
            pool.wait_ge(set_up, 1)
            nc.gpsimd.memset(relb[NB:NB + 1, :], NEG).then_inc(set_up, 1)
            pool.wait_ge(mask_in, 32)
            nc.gpsimd.tensor_copy(masks[:, :, :], masks_in[:, :, :]).then_inc(set_up, 1)
            pool.wait_ge(set_up, 3)
            nc.gpsimd.memset(sel[:, :, :], 0.0).then_inc(set_up, 1)
            pool.wait_ge(set_up, 4)
            nc.gpsimd.memset(sfx[:, :], 0.0).then_inc(set_up, 1)
            pool.wait_ge(set_up, 5)
            pool.wait_ge(bank_free[slot["spread", "x_2"].bank], turn(("spread", "x_2")) + 1)
            nc.gpsimd.memset(aT[:, :, :], 0.0).then_inc(set_up, 1)
            for lv in range(LEVELS):
                half = 1 << lv
                pairs = lambda a: a[:, :].rearrange("p (n two l) -> p n two l", two=2, l=half)
                blocks = HG * S // (2 * half)
                pool.wait_ge(prefix_ready, lv + 1)
                pool.wait_ge(e_ready, lv + 1)
                if lv:
                    pool.wait_ge(suffix_ready, lv)
                nc.gpsimd.tensor_tensor(pairs(sfx)[:, :, 0, :], pairs(sfx)[:, :, 0, :],
                                        pairs(lf)[:, :, 1, half - 1:half].to_broadcast([P, blocks, half]),
                                        ALU.add).then_inc(suffix_ready, 1)

        @block.scalar
        def _(act):
            link = Chain(act, act_step)
            n = {"sq": 0, "heads": 0, "x": 0}

            def ready(key, i=None):
                act.wait_ge(*completion(key, i))

            def frees(key, ins):
                ins.then_inc(bank_free[slot[key].bank], 1)

            def round_w(m, i=None, per=0):
                if i is None:
                    if m >= NLOADS:
                        return
                    act.wait_ge(raw_full[m % 2], 16 * (m // 2 + 1))
                    if m >= 2:
                        act.wait_ge(w_used, m - 1)
                else:
                    act.wait_ge(raw_full[m % 2], 16 * (m // 2 + 1) + 8 * per * i)
                    act.wait_ge(w_used, m - 1 + per * i)
                nc.scalar.activation(w_hi[m % 2][:, :], raw[m % 2][:, :], ACT.Copy).then_inc(hi_ready, 1)

            def squares(src):
                if n["sq"] >= 2:
                    act.wait_ge(summed, n["sq"] - 1)
                nc.scalar.activation(square[n["sq"] % 2][:, 0:src.shape[-1]], src, ACT.Square).then_inc(squared, 1)
                n["sq"] += 1

            def root(width, sem_in, value):
                act.wait_ge(sem_in, value)
                nc.scalar.activation(st[:, 1, 0:width], st[:, 0, 0:width], ACT.Sqrt).then_inc(root_ready, 1)

            def norm_root(name, tokens):
                root(tokens // P, bank_free[7], turn(("sum", name)) + 1)

            def raised(hi, src, gain, j):
                nc.scalar.activation(hi, src, ACT.Copy, scale=vcol(gain, j)).then_inc(rounded, 1)

            def keep_rms(name, dst, tokens=S):
                ready(("spread", name))
                frees(("spread", name), nc.scalar.activation(dst[:, 0:tokens], B(("spread", name))[:, 0:tokens],
                                                             ACT.Copy))

            def tokens_out(name, dst, func=ACT.Copy, first=0, count=TT):
                for t in range(first, first + count):
                    ready((name, t))
                    frees((name, t), nc.scalar.activation(dst(t), B((name, t))[:, 0:COLS], func,
                                                          scale=st[:, 5, t % TT:t % TT + 1]))

            def turned(name, count, dst):
                for j in range(count):
                    ready((name, j))
                    nc.scalar.activation(dst(j), B((name, j))[:, :], ACT.Copy).then_inc(rounded, 1)

            def attention(kind, count, between=None):
                rb, tb = (row, pT) if kind in ("mem", "att") else (row_2, pT_2)
                for s in range(count + LAG):
                    if s < count:
                        w = UNIT0[kind] + s
                        keys = UNITS[w][3]
                        act.wait_ge(neg_max, w + 1)
                        src = rb[w % NLP][:, 0:keys]
                        if kind in ("mem", "mem_2"):
                            src = B(("S", w))[:, 0:keys]
                            if w >= NLP:
                                ready(("T", w - NLP))
                        nc.scalar.activation(rb[w % NLP][:, 0:keys], src, ACT.Exp, bias=mx[:, w % 8, 1:2],
                                             scale=MDH ** -0.5 if kind == "mem" else 1.0,
                                             accum_out=mx[:, w % 8, 2:3]).then_inc(exp_ready, 1)
                    if s >= LAG:
                        w = UNIT0[kind] + s - LAG
                        keys = UNITS[w][3]
                        ready(("T", w))
                        if w >= 2:
                            ready(("O", w - 2))
                        frees(("T", w), nc.scalar.activation(
                            tb[w % 2][:, 0:keys // P, :], B(("T", w))[:, 0:keys].rearrange("p (c t) -> p c t", t=P),
                            ACT.Copy))
                    if between is not None:
                        between(s)

            def head_squares(src, dst):
                nc.scalar.activation(dst, src, ACT.Square).then_inc(heads_sq, 1)

            def head_root(width):
                n["heads"] += 1
                root(width, heads_ms, n["heads"])

            def wait_own(key):
                act.wait_ge(bank_free[slot[key].bank], turn(key) + 1)

            act.wait_ge(mem_in, 16)
            act.wait_ge(vec_in, 16)
            for j in range(KT):
                raised(mn_hi[:, j, :], memT[:, j, :], "g_mem", j)
                squares(memT[:, j, :])
                if j == 1:
                    round_w(0)
            round_w(1)
            act.wait_ge(x_in, 16)
            for j in range(KT):
                raised(h_hi[:, j, :], x[:, j, :], "g_pre_mix", j)
                squares(x[:, j, :])
                if j == 2:
                    round_w(2)
                if j == 5:
                    round_w(3)
                if j == 6:
                    norm_root("mem", M)
            round_w(4)
            keep_rms("mem", rms_mem, M)
            act.wait_ge(rms_col, 1)
            for m in range(2):
                for t in (2 * m, 2 * m + 1):
                    ready(("mem_v", t))
                    frees(("mem_v", t), nc.scalar.activation(mv[:, t % 2, m * COLS:(m + 1) * COLS],
                                                             B(("mem_v", t))[:, 0:COLS], ACT.Copy,
                                                             scale=st[:, 5, 8 + t % 2:9 + t % 2]))
            round_w(FIRST["qm"] + 1)
            round_w(FIRST["qm"] + 2)
            norm_root("x", S)
            for t in range(2):
                ready(("bias", t))
                frees(("bias", t), nc.scalar.activation(bias_row[0:HEADS, t * 512:(t + 1) * 512],
                                                        B(("bias", t))[0:HEADS, :], ACT.Copy))
            keep_rms("x", rms)

            def value_tiles(s):
                if s % 2 == 0 and 2 <= s <= 16:
                    tokens_out("v", lambda t: v[:, t % 4, t // 4 * COLS:(t // 4 + 1) * COLS], first=s // 2 - 1, count=1)
                if s == 8:
                    round_w(FIRST["q"])

            round_w(FIRST["v"] + 1)
            attention("mem", MHEADS * TT, value_tiles)
            act.wait_ge(bias_saved, 16)
            turned("turn_mem", 4, lambda j: br_hi[:, 8 + j, :])
            for m in range(5):
                round_w(FIRST["q"] + m + 1)

            def conv_loads(s):
                if s in CONV_STEPS:
                    round_w(FIRST["cc"] + 2 + CONV_STEPS.index(s))

            attention("att", HEADS * TT, conv_loads)
            turned("turn_att", 4, lambda j: br_hi[:, 4 + j, :])
            for t in range(4):
                wait_own(("cb", t))
                nc.scalar.activation(br_hi[:, t, :], cy[:, t, :], ACT.Copy).then_inc(rounded, 1)
            with act.Fori(0, 3) as i:
                for half in range(2):
                    for m in range(3):
                        round_w(FIRST["branch"] + 3 * half + m + 1, i, 6)
                        for t in range(2 * m, 2 * m + 2) if m < 2 else ():
                            c = 8 * half + t
                            act.wait_ge(bank_free[slot["branch", c].bank], turn(("branch", c), i) + 1)
                            nc.scalar.activation(gate[:, t, :], gate[:, t, :], ACT.Sigmoid,
                                                 bias=vec[:, bass.ds(8 * i + (VEC["b_gate"] + 4 * half + t), 1)]
                                                 ).then_inc(gated, 1)
            for j in range(KT):
                act.wait_ge(merge_add, 4 + 16 + j + 1)
                nc.scalar.activation(br_hi[:, j, :], merged[:, j, :], ACT.Copy).then_inc(rounded, 1)
            for m in range(4):
                round_w(FIRST["w_out"] + m + 1)
                for j in (2 * m, 2 * m + 1):
                    ready(("w_out", j))
                    squares(B(("w_out", j))[:, :])
                    frees(("w_out", j), nc.scalar.activation(mixed[:, j, :], B(("w_out", j))[:, :], ACT.Copy))

            def next_input(gain, j):
                n["x"] += 1
                act.wait_ge(x_ready, n["x"])
                raised(h_hi[:, j, :], x[:, j, :], gain, j)
                squares(x[:, j, :])

            norm_root("mix", S)
            round_w(FIRST["up"] + 1)
            for j in range(KT):
                next_input("g_pre_ffn", j)
            round_w(FIRST["up"] + 2)
            norm_root("ffn", S)
            keep_rms("ffn", rms)

            def up_turn(name, i=None):
                it = 0 if i is None else i + 1
                for m in range(2):
                    if i is not None:
                        round_w(FIRST["up"] + m + 4, i, 2)
                    elif m:
                        round_w(FIRST["up"] + 3)
                    for c in (2 * m, 2 * m + 1):
                        key = (name, c)
                        act.wait_ge(bank_free[slot[key].bank], turn(key, i) + 1)
                        if c == 0:
                            act.wait_ge(a_down, 2 * it + 2)
                        j = 2 * it + (c % 2 + (FT if m else 0))
                        nc.scalar.activation(y[c][:, :], tap[c % 2][:, :], ACT.Identity,
                                             bias=vec[:, bass.ds(j + VEC["ffn_conv_b"], 1)],
                                             scale=vec[:, bass.ds(j + (VEC["ffn_conv_w"] + 2 * 2 * FT), 1)]
                                             ).then_inc(seed, 1)
                    if m == 0:
                        for c in range(2):
                            act.wait_ge(conv_done, 4 * it + c + 1)
                            nc.scalar.activation(y[c][:, :], y[c][:, :], ACT.Gelu_apprx_tanh).then_inc(act_gate, 1)
                for c in range(2):
                    act.wait_ge(prod, 2 * it + (c + 1))
                    nc.scalar.activation(a_hi[:, bass.ds(1024 * it + 512 * c, 512)], y[2 + c][:, :], ACT.Copy
                                         ).then_inc(a_up, 1)

            up_turn("up_first")
            with act.Fori(0, FT // 2 - 1) as i:
                up_turn("up", i)
            act.wait_ge(mem2_in, 16)
            for g in range(4):
                for m in range(3):
                    if 3 * g + m + 2 <= 12:
                        round_w(FIRST["down"] + 3 * g + m + 2)
                    if m:
                        j = 2 * g + m - 1
                        raised(mn2_hi[:, j, :], mem2T[:, j, :], "norm_mem_2", j)
                        squares(mem2T[:, j, :])
                for j in (2 * g, 2 * g + 1):
                    ready(("down", j % 4), j // 4)
                    squares(B(("down", j % 4))[:, :])
                    frees(("down", j % 4), nc.scalar.activation(down[:, j * S:(j + 1) * S], B(("down", j % 4))[:, :],
                                                                ACT.Copy))
            norm_root("down", S + M)
            round_w(FIRST["mem_kv_2"] + 1)
            round_w(FIRST["iq"])
            next_input("norm_mix_2", 0)
            round_w(FIRST["iq"] + 1)
            for j in range(1, 3):
                next_input("norm_mix_2", j)
            act.wait_ge(rms_col, 3)
            for t in range(4):
                ready(("mem_kv_2", t))
                dst = km_tok if t < 2 else vm
                frees(("mem_kv_2", t), nc.scalar.activation(dst[:, t % 2, :], B(("mem_kv_2", t))[:, 0:M], ACT.Copy,
                                                            scale=st[:, 5, 10 + t % 2:11 + t % 2]))
            for j in range(3, KT):
                next_input("norm_mix_2", j)
            wait_own(("mem_kv_2", 1))
            head_squares(km_tok[:, :, :], km_sq[:, :, :])
            round_w(FIRST["idx"])
            norm_root("x_2", S)
            keep_rms("x_2", rms)
            head_root(MT * SAH)
            ready(("iwT", 0))
            frees(("iwT", 0), nc.scalar.activation(iwT[0:IDXH, :], B(("iwT", 0))[0:IDXH, :], ACT.Copy))
            ready(("iw", 0))
            act.wait_ge(rms_col, 4)
            for t in range(TT):
                ins = nc.scalar.activation(iw[:, t, :], B(("iw", 0))[:, t * IDXH:(t + 1) * IDXH], ACT.Copy,
                                           scale=st[:, 5, 4 + t:5 + t])
            frees(("iw", 0), ins)
            round_w(FIRST["hf"])
            for f in range(2):
                ready(("turn_km", f))
                frees(("turn_km", f), nc.scalar.activation(kmT[:, f, :], B(("turn_km", f))[:, 0:M], ACT.Copy,
                                                           scale=vcol("mem_k_gain", 0)))
            for w, (i, h) in enumerate(IDX):
                ready(("idx", w))
                if w >= 2:
                    act.wait_ge(relu_used, w - 1)
                keys = P * (i + 1)
                frees(("idx", w), nc.scalar.activation(relu[w % 2][:, 0:keys], B(("idx", w))[:, 0:keys], ACT.Relu))

            def turned_heads(name, dst, gain):
                for f in range(2):
                    ready((name, f))
                    frees((name, f), nc.scalar.activation(dst[:, f, :], B((name, f))[:, :], ACT.Copy,
                                                              scale=vcol(gain, 0)))

            round_w(FIRST["hf"] + 1)
            for m in range(2):
                round_w(FIRST["hf"] + m + 2)
                for t in (2 * m, 2 * m + 1):
                    wait_own(("hf", t))
                    nc.scalar.activation(abs_z[:, t * S:(t + 1) * S], lf[:, t * S:(t + 1) * S], ACT.Abs)
                    nc.scalar.activation(kk[:, t * S:(t + 1) * S], lf[:, t * S:(t + 1) * S], ACT.Sigmoid, scale=-1.0
                                         ).then_inc(log_in, 1)
            act.wait_ge(log_in, 4)
            link(nc.scalar.activation(abs_z[:, :], abs_z[:, :], ACT.Exp, scale=-1.0))
            nc.scalar.activation(abs_z[:, :], abs_z[:, :], ACT.Ln, bias=1.0).then_inc(log_ready, 1)
            for m in range(2):
                round_w(FIRST["hq"] + m + 2)
                for t in (2 * m, 2 * m + 1):
                    wait_own(("hq", t))
                    nc.scalar.activation(qf[:, t * S:(t + 1) * S], qf[:, t * S:(t + 1) * S], ACT.Silu
                                         ).then_inc(hq_ready, 1)
            act.wait_ge(relu_used, len(IDX))
            for lv in range(LEVELS):
                half = 1 << lv
                pairs = lambda a: a[:, :].rearrange("p (n two l) -> p n two l", two=2, l=half)
                act.wait_ge(prefix_ready, lv + 1)
                if lv:
                    act.wait_ge(suffix_ready, lv)
                    act.wait_ge(e_used, lv)
                nc.scalar.activation(pairs(ex)[:, :, 0, :], pairs(sfx)[:, :, 0, :], ACT.Exp)
                nc.scalar.activation(pairs(ex)[:, :, 1, :], pairs(lf)[:, :, 1, :], ACT.Exp).then_inc(e_ready, 1)
                if lv:
                    round_w(FIRST["sq"] + lv + 1)
                if lv in (1, 2, 4):
                    head_root(TT * SAH)
                    turned_heads(*{1: ("turn_sq", sqT, "sa_q_gain"), 2: ("turn_sk", skT, "sa_k_gain"),
                                   4: ("turn_mq", mqT, "mem_q_gain")}[lv])
                if lv in (0, 1, 3):
                    name = ("sq", "sk", "", "mq")[lv]
                    tokens_out(name, lambda t: tok[:, t, :])
                    wait_own((name, 3))
                    head_squares(tok[:, :, :], tok_sq[:, :, :])
                elif lv == 2:
                    tokens_out("sv", lambda t: sv[:, t, :])
                elif lv < 6:
                    act.wait_ge(log_used, 1)
                    tokens_out(f"hg{lv - 4}", lambda t: g_tok[:, t, (lv - 4) * COLS:(lv - 3) * COLS], func=ACT.Silu)
                else:
                    ready(("level", lv, HG - 1))
                    tokens_out("hi0", lambda t: v_hg[:, t, 0:COLS])
            round_w(FIRST["w_out_2"])
            act.wait_ge(prefix_ready, LEVELS + 1)
            act.wait_ge(e_used, LEVELS)
            act.wait_ge(suffix_ready, LEVELS)
            nc.scalar.activation(ex[:, :], sfx[:, :], ACT.Exp).then_inc(e_ready, 1)
            act.wait_ge(e_used, LEVELS + 1)
            nc.scalar.activation(ex[:, :], lf[:, :], ACT.Exp).then_inc(e_ready, 1)
            tokens_out("hi1", lambda t: v_hg[:, t, COLS:2 * COLS])
            act.wait_ge(e_ready, LEVELS + 2)
            for c in range(TT - 1):
                ready(("turn_kd", c))
                frees(("turn_kd", c), nc.scalar.activation(kT[:, c, :, :], B(("turn_kd", c))[:, :]
                                                           .rearrange("p (h d) -> p h d", d=HDK), ACT.Copy))
            for c in range(TT):
                ready(("o_hg", c))
                if c >= 2:
                    act.wait_ge(summed, n["sq"] - 1)
                nc.scalar.activation(hg_sq[c % 2][:, :], B(("o_hg", c))[:, :], ACT.Square).then_inc(squared, 1)
                n["sq"] += 1
            head_root(HG * TT)
            attention("mem_2", SAH * TT)
            attention("sa", SAH * TT)
            turned("turn_mix", KT, lambda j: mo_hi[:, j, :])
            for m in range(4):
                round_w(FIRST["w_out_2"] + m + 1)
                for j in (2 * m, 2 * m + 1):
                    wait_own(("w_out_2", j))
                    raised(h_hi[:, j, :], x[:, j, :], "norm_ffn_2", j)
                    squares(x[:, j, :])
            round_w(FIRST["up_2"] + 1)
            round_w(FIRST["up_2"] + 2)
            norm_root("ffn_2", S)
            keep_rms("ffn_2", rms)

            def up_2_turn(name, i=None):
                it = 0 if i is None else i + 1
                if i is not None:
                    round_w(FIRST["up_2"] + 4, i, 2)
                for c in range(2):
                    act.wait_ge(bank_free[slot[name, c].bank], turn((name, c), i) + 1)
                    nc.scalar.activation(y[c][:, :], y[c][:, :], ACT.Silu).then_inc(act_gate, 1)
                if i is not None:
                    round_w(FIRST["up_2"] + 5, i, 2)
                else:
                    round_w(FIRST["up_2"] + 3)
                for c in range(2):
                    act.wait_ge(prod, FT + 2 * it + (c + 1))
                    nc.scalar.activation(a_hi[:, bass.ds(1024 * it + 512 * c, 512)], y[2 + c][:, :], ACT.Copy
                                         ).then_inc(a_up, 1)

            up_2_turn("up_2_first")
            with act.Fori(0, FT // 2 - 1) as i:
                up_2_turn("up_2", i)
            for m in range(2, 12):
                round_w(FIRST["down_2"] + m)

        @block.vector
        def _(dve):
            link = Chain(dve, dve_step)
            n = {"sum": 0, "root": 0, "low": 0, "heads": 0}

            def ready(key, i=None):
                dve.wait_ge(*completion(key, i))

            def frees(key, ins):
                ins.then_inc(bank_free[slot[key].bank], 1)

            def wait_free(key, i=None):
                dve.wait_ge(bank_free[slot[key].bank], turn(key, i) + 1)

            def split_w(m, i=None, per=0):
                if i is None and m >= NLOADS:
                    return
                dve.wait_ge(hi_ready, m + 1 if i is None else m + 1 + per * i)
                nc.vector.tensor_tensor(w_lo[m % 2][:, :], raw[m % 2][:, :], w_hi[m % 2][:, :].bitcast(F32),
                                        ALU.subtract).then_inc(lo_ready, 1)

            def split_part(m, part):
                if part == 0:
                    dve.wait_ge(hi_ready, m + 1)
                cut = slice(part * SLOT // 2, (part + 1) * SLOT // 2)
                ins = nc.vector.tensor_tensor(w_lo[m % 2][:, cut], raw[m % 2][:, cut],
                                              w_hi[m % 2][:, cut].bitcast(F32), ALU.subtract)
                if part == 1:
                    ins.then_inc(lo_ready, 1)

            def add_squares(first, tokens=S, into=None):
                into = ssq if into is None else into
                src = square[n["sum"] % 2][:, 0:tokens]
                dve.wait_ge(squared, n["sum"] + 1)
                if first:
                    nc.vector.tensor_copy(into[:, 0:tokens], src).then_inc(summed, 1)
                else:
                    dve.wait_ge(summed, n["sum"])
                    nc.vector.tensor_tensor(into[:, 0:tokens], into[:, 0:tokens], src, ALU.add).then_inc(summed, 1)
                n["sum"] += 1

            def inverse_root(width):
                n["root"] += 1
                ms, r, t = st[:, 0, 0:width], st[:, 2, 0:width], st[:, 3, 0:width]
                dve.wait_ge(root_ready, n["root"])
                link(nc.vector.reciprocal(r, st[:, 1, 0:width]))
                link(nc.vector.tensor_tensor(t, r, r, ALU.mult))
                link(nc.vector.tensor_tensor(t, t, ms, ALU.mult))
                link(nc.vector.tensor_scalar(t, t, -0.5, 1.5, ALU.mult, ALU.add))
                link(nc.vector.tensor_tensor(r, r, t, ALU.mult))

            def norm_scale(name, tokens, keep=None, extra=0):
                width = (tokens + extra) // P
                ready(("sum", name))
                frees(("sum", name), nc.vector.tensor_scalar(st[:, 0, 0:width], B(("sum", name))[:, 0:width],
                                                             1.0 / D, EPS, ALU.mult, ALU.add))
                wait_free(("sum", name))
                inverse_root(width)
                if extra:
                    nc.vector.tensor_copy(st[:, 5, 10:12], st[:, 2, tokens // P:width]).then_inc(rms_col, 1)
                if keep is not None:
                    ins = nc.vector.tensor_copy(st[:, 5, keep:keep + tokens // P], st[:, 2, 0:tokens // P])
                    if name == "x_2":
                        link(ins)
                        ins = nc.vector.tensor_scalar(st[:, 5, 4:8], st[:, 5, 0:4], IW_SCALE, None, ALU.mult)
                    ins.then_inc(rms_col, 1)
                for c in range(tokens // P):
                    ins = nc.vector.tensor_scalar(diag[:, c, :], ident[:, :], st[:, 2, c:c + 1], None, ALU.mult)
                ins.then_inc(diag_ready, 1)

            def low_part(lo, src, hi, key=None):
                n["low"] += 1
                dve.wait_ge(rounded, n["low"])
                nc.vector.tensor_tensor(lo, src, hi.bitcast(F32), ALU.subtract).then_inc(split, 1)
                if key is not None:
                    dve.wait_ge(split, n["low"])
                    dve.sem_inc(bank_free[slot[key].bank], 1)

            def low_gained(lo, src, gain, hi, j):
                n["low"] += 1
                dve.wait_ge(rounded, n["low"])
                nc.vector.scalar_tensor_tensor(out=lo, in0=src, scalar=vcol(gain, j), in1=hi.bitcast(F32),
                                               op0=ALU.mult, op1=ALU.subtract).then_inc(split, 1)

            def residual(name, src, gain, next_gain, tiles, between=None):
                spread = B(("spread", name))[:, :]
                ready(("spread", name))
                for j in tiles:
                    ins = nc.vector.scalar_tensor_tensor(out=src(j), in0=src(j), scalar=vcol(gain, j), in1=spread,
                                                         op0=ALU.mult, op1=ALU.mult)
                    if j == KT - 1:
                        frees(("spread", name), ins)
                        wait_free(("spread", name))
                    else:
                        link(ins)
                    nc.vector.tensor_tensor(x[:, j, :], x[:, j, :], src(j), ALU.add).then_inc(x_ready, 1)
                    if j > 1:
                        low_gained(h_lo[:, j - 1, :], x[:, j - 1, :], next_gain, h_hi[:, j - 1, :], j - 1)
                        add_squares(False)
                    if j == 0:
                        low_gained(h_lo[:, j, :], x[:, j, :], next_gain, h_hi[:, j, :], j)
                        add_squares(True)
                    if between is not None:
                        between(j)
                if j == KT - 1:
                    low_gained(h_lo[:, j, :], x[:, j, :], next_gain, h_hi[:, j, :], j)
                    add_squares(False)

            def times_rms(name, loads, dst, scale=None):
                for m in range(loads):
                    split_w(FIRST[name] + m + 1)
                    for t in (2 * m, 2 * m + 1):
                        ready((name, t))
                        normal(name, t, dst(t), scale)

            def normal(name, t, dst, scale=None, i=None):
                src = B((name, t))[:, :]
                if scale is None:
                    ins = nc.vector.tensor_tensor(dst, src, rms[:, :], ALU.mult)
                else:
                    ins = nc.vector.scalar_tensor_tensor(out=dst, in0=src, scalar=scale, in1=rms[:, :],
                                                         op0=ALU.mult, op1=ALU.mult)
                frees((name, t), ins)

            def attention(kind, count, bias_of, dst, between=None):
                rb = row if kind in ("mem", "att") else row_2
                for s in range(count + LAG + 1):
                    if s < count:
                        w = UNIT0[kind] + s
                        _, h, i, keys = UNITS[w]
                        ready(("S", w))
                        S_ = B(("S", w))[:, 0:keys]
                        scale = 1.0
                        if bias_of is None:
                            link(nc.vector.reduce_max(mx[:, w % 8, 0:1], S_, AX.X))
                            scale = MDH ** -0.5 if kind == "mem" else 1.0
                        else:
                            if w >= NLP:
                                ready(("T", w - NLP))
                            frees(("S", w), nc.vector.tensor_tensor_reduce(
                                out=rb[w % NLP][:, 0:keys], in0=S_, in1=bias_of(h, i), scale=1.0, scalar=-3e38,
                                op0=ALU.add, op1=ALU.max, accum_out=mx[:, w % 8, 0:1]))
                            wait_free(("S", w))
                        nc.vector.tensor_scalar(mx[:, w % 8, 1:2], mx[:, w % 8, 0:1], -scale, None, ALU.mult
                                                ).then_inc(neg_max, 1)
                    if s >= LAG + 1:
                        w = UNIT0[kind] + s - LAG - 1
                        _, h, i, keys = UNITS[w]
                        dve.wait_ge(exp_ready, w + 1)
                        link(nc.vector.reciprocal(mx[:, w % 8, 3:4], mx[:, w % 8, 2:3]))
                        ready(("O", w))
                        d = dst(h, i)
                        frees(("O", w), nc.vector.tensor_scalar(d, B(("O", w))[:, 0:d.shape[-1]], mx[:, w % 8, 3:4],
                                                                None, ALU.mult))
                    if between is not None:
                        between(s)

            def turned(name, count, hi, lo):
                for j in range(count):
                    low_part(lo(j), B((name, j))[:, :], hi(j), (name, j))

            dve.wait_ge(vec_in, 16)
            for j in range(KT):
                low_gained(mn_lo[:, j, :], memT[:, j, :], "g_mem", mn_hi[:, j, :], j)
                add_squares(j == 0, M, ssq_mem)
                if j == 1:
                    split_w(0)
            split_w(1)
            dve.wait_ge(const_in, 32)
            for j in range(KT):
                low_gained(h_lo[:, j, :], x[:, j, :], "g_pre_mix", h_hi[:, j, :], j)
                add_squares(j == 0)
                if j == 2:
                    split_w(2)
                if j == 5:
                    norm_scale("mem", M, keep=8)
                    split_w(3)
                    dve.wait_ge(bank_free[6], turn(("spread", "mem")) + 1)
                    for t in range(4):
                        ready(("mem_k", t))
                        frees(("mem_k", t), nc.vector.tensor_tensor(mk[:, t, :], B(("mem_k", t))[:, 0:M], rms_mem[:, :],
                                                                    ALU.mult))
            split_w(4)
            split_w(5)
            split_w(6)
            norm_scale("x", S, keep=0)
            wait_free(("spread", "x"))
            for t in range(4):
                ready(("qm", t))
                normal("qm", t, qm[:, t, :])
            split_w(FIRST["v"] + 1)
            attention("mem", MHEADS * TT, None, lambda h, i: o_tok[:, i, h * MDH:(h + 1) * MDH],
                      between=lambda s: s in (8, 9) and split_part(FIRST["q"], s - 8))
            turned("turn_mem", 4, lambda j: br_hi[:, 8 + j, :], lambda j: br_lo[:, 8 + j, :])
            times_rms("q", 2, lambda t: q[:, t, :], DH ** -0.5)
            times_rms("k", 2, lambda t: k[:, t, :])
            split_w(FIRST["cc"] + 1)

            def toeplitz(h, i):
                if i == 0 and h % 2 == 0:
                    dve.wait_ge(toep_in[h // 2 % 2], 32 * (h // 4 + 1))
                return toep[h // 2 % 2][:, h % 2, P * i + 511:383:-1]

            def conv_branch(s):
                for part_ in range(2):
                    if s - part_ in CONV_STEPS:
                        split_part(FIRST["cc"] + 2 + CONV_STEPS.index(s - part_), part_)
                if s - 1 in CONV_TILE[4:8]:
                    t = CONV_TILE.index(s - 1) - 4
                    link(nc.vector.tensor_scalar(cy[:, t, :], u[:, t, :], vcol("conv_mix_w", 8 + t), None, ALU.mult))
                    for back in (1, 2):
                        link(nc.vector.scalar_tensor_tensor(
                            out=cy[:, t, back:], in0=u[:, t, 0:S - back], scalar=vcol("conv_mix_w", 4 * (2 - back) + t),
                            in1=cy[:, t, back:], op0=ALU.mult, op1=ALU.add))
                if s not in CONV_TILE:
                    return
                part_, t = divmod(CONV_TILE.index(s), 4)
                if part_ == 0:
                    ready(("cc", t))
                    normal("cc", t, cc[:, t, :])
                elif part_ == 1:
                    wait_free(("cc", t))
                    link(nc.vector.tensor_tensor(cc[:, t, :], cc[:, t, :], rms[:, :], ALU.mult))
                    ready(("cv", t))
                    frees(("cv", t), nc.vector.tensor_tensor(u[:, t, :], B(("cv", t))[:, :], cc[:, t, :], ALU.mult))
                    wait_free(("cv", t))
                else:
                    link(nc.vector.tensor_tensor(cy[:, t, :], cy[:, t, :], rms[:, :], ALU.mult))
                    ready(("cb", t))
                    frees(("cb", t), nc.vector.tensor_tensor(cy[:, t, :], B(("cb", t))[:, :], cy[:, t, :], ALU.mult))

            attention("att", HEADS * TT, toeplitz, lambda h, i: o_tok[:, i, h * DH:(h + 1) * DH], between=conv_branch)
            turned("turn_att", 4, lambda j: br_hi[:, 4 + j, :], lambda j: br_lo[:, 4 + j, :])
            for t in range(4):
                low_part(br_lo[:, t, :], cy[:, t, :], br_hi[:, t, :])
            dve.wait_ge(split, n["low"])
            for t in range(4):
                nc.vector.memset(merged[:, 2 * t:2 * t + 2, :], 0.0).then_inc(merge_add, 1)
            with dve.Fori(0, 3) as i:
                link.enter(i, 8)
                for half in range(2):
                    for m in range(3):
                        split_w(FIRST["branch"] + 3 * half + m + 1, i, 6)
                        for t in range(2 * m, 2 * m + 2) if m < 2 else ():
                            dve.wait_ge(merge_add, 1 + 4 * half + t + 8 * i)
                            ready(("branch", 8 * half + t), i)
                            normal("branch", 8 * half + t, gate[:, t, :])
                    for t in range(4):
                        c = 8 * half + 4 + t
                        dve.wait_ge(gated, 4 * half + t + 1 + 8 * i)
                        ready(("branch", c), i)
                        link(nc.vector.tensor_tensor(part[t % 2][:, :], B(("branch", c))[:, :], gate[:, t, :],
                                                     ALU.mult))
                        dve.sem_inc(bank_free[4 + t], 1)
                        dve.wait_ge(merge_add, 4 + 4 * half + t + 8 * i)
                        nc.vector.tensor_tensor(merged[:, 4 * half + t, :], merged[:, 4 * half + t, :],
                                                part[t % 2][:, :], ALU.add).then_inc(merge_add, 1)
            link.leave(3)
            for j in range(KT):
                low_part(br_lo[:, j, :], merged[:, j, :], br_hi[:, j, :])
            for m in range(4):
                split_w(FIRST["w_out"] + m + 1)
                for j in (2 * m, 2 * m + 1):
                    add_squares(j == 0)
            norm_scale("mix", S)
            split_w(FIRST["up"] + 1)
            wait_free(("w_out", KT - 1))
            residual("mix", lambda j: mixed[:, j, :], "g_post_mix", "g_pre_ffn", range(KT))
            split_w(FIRST["up"] + 2)
            norm_scale("ffn", S)
            for c in range(2):
                nc.vector.memset(y[2 + c][:, :], 0.0).then_inc(a_down, 1)
            wait_free(("spread", "ffn"))

            def up_turn(name, i=None):
                it = 0 if i is None else i + 1
                for m in range(2):
                    if i is not None:
                        split_w(FIRST["up"] + m + 4, i, 2)
                    elif m:
                        split_w(FIRST["up"] + 3)
                    for c in (2 * m, 2 * m + 1):
                        ready((name, c), i)
                        normal(name, c, tap[c % 2][:, :])
                    for c in (2 * m, 2 * m + 1):
                        wait_free((name, c), i)
                        dve.wait_ge(seed, 4 * it + (c + 1))
                        col = VEC["ffn_conv_w"] + c % 2 + (FT if m else 0)
                        link(nc.vector.scalar_tensor_tensor(
                            out=y[c][:, 1:], in0=tap[c % 2][:, 0:S - 1],
                            scalar=vec[:, bass.ds(2 * it + (col + 2 * FT), 1)], in1=y[c][:, 1:], op0=ALU.mult,
                            op1=ALU.add))
                        nc.vector.scalar_tensor_tensor(
                            out=y[c][:, 2:], in0=tap[c % 2][:, 0:S - 2], scalar=vec[:, bass.ds(2 * it + col, 1)],
                            in1=y[c][:, 2:], op0=ALU.mult, op1=ALU.add).then_inc(conv_done, 1)
                    dve.wait_ge(conv_done, 4 * it + (2 * m + 2))
                for c in range(2):
                    dve.wait_ge(act_gate, 2 * it + (c + 1))
                    nc.vector.tensor_tensor(y[2 + c][:, :], y[2 + c][:, :], y[c][:, :], ALU.mult).then_inc(prod, 1)
                for c in range(2):
                    dve.wait_ge(a_up, 2 * it + (c + 1))
                    nc.vector.tensor_tensor(a_lo[:, bass.ds(1024 * it + 512 * c, 512)], y[2 + c][:, :],
                                            a_hi[:, bass.ds(1024 * it + 512 * c, 512)].bitcast(F32), ALU.subtract
                                            ).then_inc(a_down, 1)

            up_turn("up_first")
            with dve.Fori(0, FT // 2 - 1) as i:
                link.enter(i, 4)
                up_turn("up", i)
            link.leave(FT // 2 - 1)
            dve.wait_ge(a_down, FT + 2)
            for g in range(4):
                for m in range(3):
                    if 3 * g + m + 2 <= 12:
                        split_w(FIRST["down"] + 3 * g + m + 2)
                    if m:
                        j = 2 * g + m - 1
                        low_gained(mn2_lo[:, j, :], mem2T[:, j, :], "norm_mem_2", mn2_hi[:, j, :], j)
                        add_squares(j == 0, M, ssq_mem)
                for j in (2 * g, 2 * g + 1):
                    add_squares(j == 0)
            norm_scale("down", S, extra=M)
            split_w(FIRST["mem_kv_2"] + 1)
            dve.wait_ge(bank_free[3], turn(("down", 3), 1) + 1)

            def between(j):
                if j == 0:
                    split_w(FIRST["iq"])
                if j == 2:
                    split_w(FIRST["iq"] + 1)

            out_tile = lambda j: down[:, j * S:(j + 1) * S]
            residual("down", out_tile, "g_post_ffn", "norm_mix_2", range(4), between)
            dve.wait_ge(w_used, FIRST["mem_kv_2"] + 2)
            residual("down", out_tile, "g_post_ffn", "norm_mix_2", range(4, KT))
            split_w(FIRST["idx"])
            norm_scale("x_2", S, keep=0)

            def head_norm(src, sq, tokens):
                width = tokens // P * SAH
                n["heads"] += 1
                dve.wait_ge(heads_sq, n["heads"])
                heads = lambda a: a[:, :, :].rearrange("p t (h d) -> p (t h) d", d=64)
                link(nc.vector.tensor_reduce(st[:, 0, 0:width], heads(sq), AX.X, ALU.add))
                link(nc.vector.tensor_scalar(st[:, 0, 0:width], st[:, 0, 0:width], 1.0 / 64, EPS, ALU.mult, ALU.add))
                dve.sem_inc(heads_ms, 1)
                inverse_root(width)
                nc.vector.tensor_tensor(heads(src), heads(src), st[:, 2, 0:width].unsqueeze(2)
                                        .to_broadcast([P, width, 64]), ALU.mult).then_inc(heads_norm, 1)

            wait_free(("spread", "x_2"))
            for t in range(4):
                ready(("iq", t))
                normal("iq", t, iq[:, t, :])
            head_norm(km_tok, km_sq, M)
            link(nc.vector.memset(ik[0][64:P, :], 0.0))
            link(nc.vector.memset(ik[1][0:64, :], 0.0))
            ready(("ik", 0))
            link(nc.vector.tensor_tensor(ik[0][0:64, :], B(("ik", 0))[0:64, :], rms[0:64, :], ALU.mult))
            frees(("ik", 0), nc.vector.tensor_tensor(ik[1][64:P, :], B(("ik", 0))[64:P, :], rms[64:P, :], ALU.mult))
            link(nc.vector.tensor_scalar(vec[:, VEC["sa_q_gain"]:VEC["sa_q_gain"] + 2],
                                         vec[:, VEC["sa_q_gain"]:VEC["sa_q_gain"] + 2], 64 ** -0.5, None, ALU.mult))
            split_w(FIRST["hf"])
            dve.wait_ge(set_up, 4)
            wait_free(("iw", 0))
            for w, (i, h) in enumerate(IDX):
                keys = P * (i + 1)
                wait_free(("idx", w))
                if w:
                    dve.wait_ge(relu_used, w)
                nc.vector.scalar_tensor_tensor(out=sel[:, i, 0:keys], in0=relu[w % 2][:, 0:keys],
                                               scalar=iw[:, i, h:h + 1], in1=sel[:, i, 0:keys], op0=ALU.mult,
                                               op1=ALU.add).then_inc(relu_used, 1)
            dve.wait_ge(relu_used, len(IDX))
            for i in range(1, TT):
                link(nc.vector.tensor_tensor(sel[:, i, P * i:P * (i + 1)], sel[:, i, P * i:P * (i + 1)], causal[:, :],
                                             ALU.add))

            def top_keys(first, last):
                for r in range(first, last):
                    i, step = 1 + r // (TOPK // 8), r % (TOPK // 8)
                    scores = sel[:, i, 0:P * (i + 1)]
                    link(nc.vector.max(st[:, 4, 0:8], scores))
                    link(nc.vector.match_replace(scores, in_to_replace=st[:, 4, 0:8], in_values=scores,
                                                 imm_value=TAKEN))
                    if step == TOPK // 8 - 1:
                        link(nc.vector.tensor_scalar(scores, scores, TAKEN, NEG, ALU.not_equal, ALU.mult))

            for m in range(2):
                if m == 0:
                    split_w(FIRST["hf"] + 1)
                for t in (2 * m, 2 * m + 1):
                    ready(("hf", t))
                    normal("hf", t, lf[:, t * S:(t + 1) * S])
                split_w(FIRST["hf"] + m + 2)
                top_keys(5 * m, 5 * m + 5)
            for m in range(2):
                if m == 0:
                    dve.wait_ge(log_in, 4)
                    link(nc.vector.tensor_scalar(lf[:, :], lf[:, :], 0.0, None, ALU.min))
                    dve.wait_ge(log_ready, 1)
                    nc.vector.tensor_tensor(lf[:, :], lf[:, :], abs_z[:, :], ALU.subtract).then_inc(log_used, 1)
                for t in (2 * m, 2 * m + 1):
                    ready(("hq", t))
                    normal("hq", t, qf[:, t * S:(t + 1) * S])
                split_w(FIRST["hq"] + m + 2)
                top_keys(10 + 5 * m, 15 + 5 * m)
            dve.wait_ge(set_up, 6)
            dve.wait_ge(log_used, 1)
            dve.sem_inc(prefix_ready, 1)
            dve.wait_ge(hq_ready, 4)

            def keep(h, lv, key):
                ready(key)
                frees(key, nc.vector.copy_predicated(
                    aT[:, h, :].rearrange("p (c t) -> p c t", t=P),
                    masks[:, lv, :].unsqueeze(1).to_broadcast([P, TT, P]),
                    B(key)[:, :].rearrange("p (c t) -> p c t", t=P)))

            for lv in range(LEVELS + 1):
                for h in range(HG):
                    if lv == 0:
                        keep(h, LEVELS, ("self", h))
                    else:
                        if lv == 1:
                            wait_free(("self", h))
                        else:
                            wait_free(("level", lv - 2, h))
                        keep(h, lv - 1, ("level", lv - 1, h))
                if lv == LEVELS:
                    split_w(FIRST["sq"] + lv + 1)
                    break
                half = 1 << lv
                pairs = lambda a: a[:, :].rearrange("p (n two l) -> p n two l", two=2, l=half)
                blocks = HG * S // (2 * half)
                dve.wait_ge(e_ready, lv + 1)
                nc.vector.tensor_tensor(pairs(z)[:, :, 0, :], pairs(kk)[:, :, 0, :], pairs(ex)[:, :, 0, :], ALU.mult)
                link(nc.vector.tensor_tensor(pairs(z)[:, :, 1, :], pairs(qf)[:, :, 1, :], pairs(ex)[:, :, 1, :],
                                             ALU.mult))
                dve.sem_inc(z_ready, 1)
                dve.sem_inc(e_used, 1)
                dve.wait_ge(suffix_ready, lv + 1)
                nc.vector.tensor_tensor(pairs(lf)[:, :, 1, :], pairs(lf)[:, :, 1, :],
                                        pairs(lf)[:, :, 0, half - 1:half].to_broadcast([P, blocks, half]),
                                        ALU.add).then_inc(prefix_ready, 1)
                dve.wait_ge(prefix_ready, lv + 2)
                if lv in (1, 2, 4):
                    head_norm(tok, tok_sq, S)
                if lv:
                    split_w(FIRST["sq"] + lv + 1)
                top_keys((20, 24, 24, 24, 28, 28, 31)[lv], (24, 24, 24, 28, 28, 31, 34)[lv])
            dve.wait_ge(e_ready, LEVELS + 1)
            link(nc.vector.tensor_tensor(kk[:, :], kk[:, :], ex[:, :], ALU.mult))
            dve.sem_inc(decayed, 1)
            dve.sem_inc(e_used, 1)
            dve.wait_ge(e_ready, LEVELS + 2)
            nc.vector.tensor_copy(e_last[:, :, :], ex[:, :].rearrange("p (h c t) -> p h c t", h=HG, t=P)[:, :, :, P - 1])
            link(nc.vector.tensor_tensor(qf[:, :], qf[:, :], ex[:, :], ALU.mult))
            wait_free(("hg1", TT - 1))
            link(nc.vector.tensor_tensor(g_tok[:, :, :].rearrange("p t (h d) -> p (t h) d", d=HDK),
                                         g_tok[:, :, :].rearrange("p t (h d) -> p (t h) d", d=HDK),
                                         rows[:, ROW["hg_out_gain"]:ROW["hg_out_gain"] + HDK].unsqueeze(1)
                                         .to_broadcast([P, TT * HG, HDK]), ALU.mult))
            for c in range(TT - 1):
                ready(("state", c))
                if c == 0:
                    link(nc.vector.tensor_copy(state[:, 0, :, :], B(("state", 0))[:, :]
                                               .rearrange("p (h d) -> p h d", d=HDK)))
                else:
                    for h in range(HG):
                        ins = nc.vector.scalar_tensor_tensor(
                            out=state[:, c, h, :], in0=state[:, c - 1, h, :], scalar=e_last[:, h, c:c + 1],
                            in1=B(("state", c))[:, h * HDK:(h + 1) * HDK], op0=ALU.mult, op1=ALU.add)
                    link(ins)
                dve.sem_inc(bank_free[slot["state", c].bank], 1)
                dve.sem_inc(state_ready, 1)
            for c in range(TT):
                dve.wait_ge(squared, n["sum"] + 1)
                nc.vector.tensor_reduce(st[:, 0, HG * c:HG * (c + 1)], hg_sq[c % 2][:, :]
                                        .rearrange("p (h d) -> p h d", d=HDK), AX.X, ALU.add).then_inc(summed, 1)
                n["sum"] += 1
            dve.wait_ge(summed, n["sum"])
            link(nc.vector.tensor_scalar(st[:, 0, :], st[:, 0, :], 1.0 / HDK, EPS, ALU.mult, ALU.add))
            dve.sem_inc(heads_ms, 1)
            n["heads"] += 1
            inverse_root(HG * TT)

            def scale_hg(c):
                for h in range(HG):
                    ins = nc.vector.scalar_tensor_tensor(
                        out=mix[:, c, h * HDK:(h + 1) * HDK], in0=B(("o_hg", c))[:, h * HDK:(h + 1) * HDK],
                        scalar=st[:, 2, HG * c + h:HG * c + h + 1], in1=g_tok[:, c, h * HDK:(h + 1) * HDK],
                        op0=ALU.mult, op1=ALU.mult)
                frees(("o_hg", c), ins)

            def between_mem(s):
                if s < TT:
                    scale_hg((2, 3, 0, 1)[s])
                else:
                    top_keys(min(30 + s, 48), min(31 + s, 48))

            attention("mem_2", SAH * TT, None, lambda h, i: mix[:, i, 768 + h * 64:768 + (h + 1) * 64],
                      between=between_mem)
            attention("sa", SAH * TT, lambda h, i: sel[:, i, 0:P * (i + 1)] if i else causal[:, :],
                      lambda h, i: mix[:, i, 512 + h * 64:512 + (h + 1) * 64])
            turned("turn_mix", KT, lambda j: mo_hi[:, j, :], lambda j: mo_lo[:, j, :])
            for m in range(4):
                split_w(FIRST["w_out_2"] + m + 1)
                for j in (2 * m, 2 * m + 1):
                    ready(("w_out_2", j))
                    frees(("w_out_2", j), nc.vector.tensor_tensor(x[:, j, :], B(("w_out_2", j))[:, :], x[:, j, :],
                                                                  ALU.add))
                for j in (2 * m, 2 * m + 1):
                    low_gained(h_lo[:, j, :], x[:, j, :], "norm_ffn_2", h_hi[:, j, :], j)
                    add_squares(j == 0)
            split_w(FIRST["up_2"] + 1)
            split_w(FIRST["up_2"] + 2)
            norm_scale("ffn_2", S)
            wait_free(("spread", "ffn_2"))

            def up_2_turn(name, i=None):
                it = 0 if i is None else i + 1
                if i is not None:
                    split_w(FIRST["up_2"] + 4, i, 2)
                dve.wait_ge(prod, FT + 2 * it)
                for c in range(2):
                    ready((name, c), i)
                    normal(name, c, y[c][:, :])
                if i is not None:
                    split_w(FIRST["up_2"] + 5, i, 2)
                else:
                    split_w(FIRST["up_2"] + 3)
                dve.wait_ge(a_down, FT + 2 + 2 * it)
                for c in range(2):
                    ready((name, 2 + c), i)
                    normal(name, 2 + c, y[2 + c][:, :])
                for c in range(2):
                    wait_free((name, 2 + c), i)
                    dve.wait_ge(act_gate, FT + 2 * it + (c + 1))
                    nc.vector.tensor_tensor(y[2 + c][:, :], y[2 + c][:, :], y[c][:, :], ALU.mult).then_inc(prod, 1)
                for c in range(2):
                    dve.wait_ge(a_up, FT + 2 * it + (c + 1))
                    nc.vector.tensor_tensor(a_lo[:, bass.ds(1024 * it + 512 * c, 512)], y[2 + c][:, :],
                                            a_hi[:, bass.ds(1024 * it + 512 * c, 512)].bitcast(F32), ALU.subtract
                                            ).then_inc(a_down, 1)

            up_2_turn("up_2_first")
            with dve.Fori(0, FT // 2 - 1) as i:
                up_2_turn("up_2", i)
            for g in range(4):
                for m in range(3):
                    split_w(FIRST["down_2"] + 3 * g + m + 2)
                for j in (2 * g, 2 * g + 1):
                    ready(("down_2", j % 4), j // 4)
                    frees(("down_2", j % 4), nc.vector.tensor_tensor(x[:, j, :], B(("down_2", j % 4))[:, :],
                                                                     x[:, j, :], ALU.add))

        @block.tensor
        def _(pe):
            n = {"diag": 0, "heads": 0}

            def claim(key, i=None):
                if slot[key].before or i is not None:
                    pe.wait_ge(bank_free[slot[key].bank], turn(key, i))

            def done(key, ins):
                ins.then_inc(completion(key)[0], 1)

            def weights(m, i=None, per=0):
                pe.wait_ge(lo_ready, m + 1 if i is None else m + 1 + per * i)

            def product(o, lh, ll, rh, rl, first, last):
                nc.tensor.matmul(o, lh, rh, start=first, stop=False)
                nc.tensor.matmul(o, lh, rl, start=False, stop=False)
                return nc.tensor.matmul(o, ll, rh, start=False, stop=last)

            def w(m, hi, ktiles=KT):
                return (w_hi if hi else w_lo)[m % 2][:, :].rearrange("p (k c) -> p k c", k=ktiles)

            def feature_tile(o, m, c, ah, al, tokens=S, ktiles=KT, fresh=None, first=True, last=True, kk_=None):
                for kt in range(kk_ or ktiles):
                    if fresh is not None:
                        pe.wait_ge(split, fresh + kt + 1)
                    cs = slice(c * P, (c + 1) * P)
                    ins = product(o[:, 0:tokens], w(m, 1, ktiles)[:, kt, cs], w(m, 0, ktiles)[:, kt, cs], ah(kt),
                                  al(kt), first and kt == 0, last and kt == (kk_ or ktiles) - 1)
                return ins

            def token_tile(o, m, t, ah, al, lo=0, hi=COLS, fresh=None):
                ts = slice(t * P, (t + 1) * P)
                for kt in range(KT):
                    if fresh is not None:
                        pe.wait_ge(split, fresh + kt + 1)
                    ins = product(o, ah[:, kt, ts], al[:, kt, ts], w(m, 1)[:, kt, lo:hi], w(m, 0)[:, kt, lo:hi],
                                  kt == 0, kt == KT - 1)
                return ins

            H = (lambda kt: h_hi[:, kt, :], lambda kt: h_lo[:, kt, :])

            def feature_loads(name, loads, fresh=None, act=H):
                for m in range(loads):
                    weights(FIRST[name] + m)
                    for c in range(2):
                        t = 2 * m + c
                        claim((name, t))
                        ins = feature_tile(B((name, t)), FIRST[name] + m, c, *act, fresh=fresh if t == 0 else None)
                        done((name, t), ins)

            def norm_sum(name, tokens, *sources):
                claim(("sum", name))
                pe.wait_ge(summed, NORM_SUMS[name])
                columns_ = [src[:, c * P:(c + 1) * P] for src, count in sources or ((ssq, tokens),)
                            for c in range(count // P)]
                for c, col in enumerate(columns_):
                    ins = nc.tensor.matmul(B(("sum", name))[:, c:c + 1], col, ones[:, 0:1], start=True, stop=True)
                done(("sum", name), ins)

            def norm_spread(name, tokens=S):
                n["diag"] += 1
                claim(("spread", name))
                pe.wait_ge(diag_ready, n["diag"])
                done(("spread", name), nc.tensor.matmul(B(("spread", name))[:, 0:tokens], ones[:, :],
                                                        diag[:, 0:tokens // P, :].rearrange("p c t -> p (c t)"),
                                                        start=True, stop=True))

            def together(name, first, fresh, norm_name):
                lag = 3
                for step in range(KT + lag):
                    for load in range(2):
                        kt = step - lag * load
                        if not 0 <= kt < KT:
                            continue
                        if kt == 0:
                            weights(first + load)
                            claim((name, 2 * load))
                            claim((name, 2 * load + 1))
                        pe.wait_ge(split, fresh + kt + 1)
                        for c in range(2):
                            cs = slice(c * P, (c + 1) * P)
                            t = 2 * load + c
                            ins = product(B((name, t))[:, :], w(first + load, 1)[:, kt, cs],
                                          w(first + load, 0)[:, kt, cs], h_hi[:, kt, :], h_lo[:, kt, :], kt == 0,
                                          kt == KT - 1)
                            if kt == KT - 1:
                                done((name, t), ins)
                    if step == KT - 1:
                        norm_sum(norm_name, S)

            def attention(kind, count, qk, vv, between=None):
                rb, tb = (row, pT) if kind in ("mem", "att") else (row_2, pT_2)
                for s in range(count + LAG + 1):
                    if kind in ("mem", "mem_2") and LAG <= s < count + LAG:
                        u_ = UNIT0[kind] + s - LAG
                        pe.wait_ge(exp_ready, u_ + 1)
                        pe.sem_inc(bank_free[slot["S", u_].bank], 1)
                    if s < count:
                        u_ = UNIT0[kind] + s
                        _, h, i, keys = UNITS[u_]
                        claim(("S", u_))
                        q_, k_ = qk(h, i, keys)
                        done(("S", u_), nc.tensor.matmul(B(("S", u_))[:, 0:keys], q_, k_, start=True, stop=True))
                    if LAG <= s < count + LAG:
                        u_ = UNIT0[kind] + s - LAG
                        keys = UNITS[u_][3]
                        claim(("T", u_))
                        pe.wait_ge(exp_ready, u_ + 1)
                        for c in range(keys // P):
                            ins = nc.tensor.transpose(B(("T", u_))[:, c * P:(c + 1) * P],
                                                      rb[u_ % NLP][:, c * P:(c + 1) * P], ident[:, :])
                        done(("T", u_), ins)
                    if s >= LAG + 1:
                        u_ = UNIT0[kind] + s - LAG - 1
                        _, h, i, keys = UNITS[u_]
                        claim(("O", u_))
                        pe.wait_ge(bank_free[slot["T", u_].bank], turn(("T", u_)) + 1)
                        for c in range(keys // P):
                            v_ = vv(h, c)
                            ins = nc.tensor.matmul(B(("O", u_))[:, 0:v_.shape[-1]], tb[u_ % 2][:, c, :], v_,
                                                   start=c == 0, stop=c == keys // P - 1)
                        done(("O", u_), ins)
                    if between is not None:
                        between(s)

            def turns(name, count, src, blocks):
                for j in range(count):
                    claim((name, j))
                    for t in range(blocks):
                        ins = nc.tensor.transpose(B((name, j))[:, t * P:(t + 1) * P], src(j, t), ident[:, :])
                    done((name, j), ins)

            def wait_all(name, keys):
                for key in keys:
                    pe.wait_ge(bank_free[slot[name, key].bank], turn((name, key)) + 1)

            for m in range(2):
                weights(m)
                for c in range(2):
                    key = ("mem_k", 2 * m + c)
                    claim(key)
                    done(key, feature_tile(B(key), m, c, lambda kt: mn_hi[:, kt, :], lambda kt: mn_lo[:, kt, :],
                                           tokens=M, fresh=0 if m + c == 0 else None))
            pe.wait_ge(set_up, 2)
            norm_sum("mem", M, (ssq_mem, M))
            for m in range(2):
                if m == 1:
                    norm_spread("mem", M)
                weights(2 + m)
                for t in range(MT):
                    key = ("mem_v", 2 * m + t)
                    claim(key)
                    done(key, token_tile(B(key)[:, 0:COLS], 2 + m, t, mn_hi, mn_lo))
            feature_loads("qm", 2, fresh=LOW_END["mem"])
            norm_sum("x", S)
            pe.wait_ge(onehot_in, 32)
            for t in range(2):
                claim(("bias", t))
                done(("bias", t), nc.tensor.matmul(B(("bias", t))[0:HEADS, :], relb[0:NB + 1, :],
                                                   onehot[0:NB + 1, t * 512:(t + 1) * 512], start=True, stop=True))
            norm_spread("x")
            pe.wait_ge(const_in, 32)
            wait_all("mem_v", range(4))
            wait_all("qm", range(4))

            def value_steps(s):
                for p_ in range(4 * s, 4 * s + 4) if s < MHEADS * TT else ():
                    t, kt = divmod(p_, KT)
                    ld, key, ts = FIRST["v"] + t // TT, ("v", t), slice(t % TT * P, (t % TT + 1) * P)
                    if kt == 0:
                        weights(ld)
                        claim(key)
                    ins = product(B(key)[:, 0:COLS], h_hi[:, kt, ts], h_lo[:, kt, ts], w(ld, 1)[:, kt, :],
                                  w(ld, 0)[:, kt, :], kt == 0, kt == KT - 1)
                    if kt == KT - 1:
                        done(key, ins)

            attention("mem", MHEADS * TT, lambda h, i, keys: (qm[:, h, i * P:(i + 1) * P], mk[:, h, :]),
                      lambda h, c: mv[:, c, h * MDH:(h + 1) * MDH], value_steps)

            def all_read(kind, count):
                for w_ in range(UNIT0[kind] + count - 2, UNIT0[kind] + count):
                    pe.wait_ge(bank_free[slot["O", w_].bank], turn(("O", w_)) + 1)

            all_read("mem", MHEADS * TT)
            turns("turn_mem", 4, lambda j, t: o_tok[:, t, j * P:(j + 1) * P], TT)
            feature_loads("q", 2)
            feature_loads("k", 2)
            wait_all("k", range(4))
            wait_all("v", range(4, 8))

            def head64(a, h, lo, hi):
                return a[64 * (h % 2):64 * (h % 2) + 64, h // 2, lo:hi]

            def conv_steps(s):
                for p_ in range(3 * s, 3 * s + 3) if s < HEADS * TT else ():
                    tile, kt = divmod(p_, KT)
                    ld, key = FIRST["cc"] + tile // 2, (("cc", "cv", "cb")[tile // 4], tile % 4)
                    cs = slice(tile % 2 * P, (tile % 2 + 1) * P)
                    if kt == 0:
                        weights(ld)
                        claim(key)
                    ins = product(B(key)[:, :], w(ld, 1)[:, kt, cs], w(ld, 0)[:, kt, cs], h_hi[:, kt, :],
                                  h_lo[:, kt, :], kt == 0, kt == KT - 1)
                    if kt == KT - 1:
                        done(key, ins)

            attention("att", HEADS * TT,
                      lambda h, i, keys: (head64(q, h, i * P, (i + 1) * P), head64(k, h, 0, keys)),
                      lambda h, c: v[:, c, h * DH:(h + 1) * DH], conv_steps)
            all_read("att", HEADS * TT)
            turns("turn_att", 4, lambda j, t: o_tok[:, t, j * P:(j + 1) * P], TT)
            with pe.Fori(0, 3) as i:
                for half in range(2):
                    for m in range(3):
                        ld = FIRST["branch"] + 3 * half + m
                        weights(ld, i, 6)
                        if m == 2:
                            pe.wait_ge(split, LOW_END["conv"])
                        for c in range(2 if m < 2 else 4):
                            key = ("branch", 8 * half + 2 * m + c)
                            claim(key, i)
                            if m < 2:
                                ins = feature_tile(B(key), ld, c, *H)
                            else:
                                ins = feature_tile(
                                    B(key), ld, c, lambda kt: branch(br_hi, i, kt), lambda kt: branch(br_lo, i, kt),
                                    ktiles=4)
                            done(key, ins)
            for m in range(4):
                weights(FIRST["w_out"] + m)
                for c in range(2):
                    key = ("w_out", 2 * m + c)
                    claim(key)
                    done(key, feature_tile(B(key), FIRST["w_out"] + m, c, lambda kt: br_hi[:, kt, :],
                                           lambda kt: br_lo[:, kt, :],
                                           fresh=LOW_END["conv"] if m + c == 0 else None))
            norm_sum("mix", S)
            norm_spread("mix")
            together("up_first", FIRST["up"], LOW_END["merged"], "ffn")
            norm_spread("ffn")

            def up(name):
                with pe.Fori(0, FT // 2 - 1) as i:
                    for m in range(2):
                        weights(FIRST[name] + 2 + m, i, 2)
                        for c in range(2):
                            claim((name, 2 * m + c), i)
                            done((name, 2 * m + c), feature_tile(B((name, 2 * m + c)), FIRST[name] + m, c, *H))

            def down_(name, hidden):
                with pe.Fori(0, 2) as i:
                    for g in range(2):
                        for c in range(2):
                            claim((name, 2 * g + c), i)
                        for m in range(3):
                            ld = FIRST[name] + 3 * g + m
                            weights(ld, i, 6)
                            pe.wait_ge(a_down, hidden + min(8 * m + 8, FT))
                            for c in range(2):
                                ins = feature_tile(
                                    B((name, 2 * g + c)), ld, c,
                                    lambda kt: a_hi[:, (8 * m + kt) * S:(8 * m + kt + 1) * S],
                                    lambda kt: a_lo[:, (8 * m + kt) * S:(8 * m + kt + 1) * S],
                                    first=m == 0, last=m == 2, kk_=min(8, FT - 8 * m))
                                if m == 2:
                                    done((name, 2 * g + c), ins)
                            if m < 2:
                                ins.then_inc(w_used, 1)

            up("up")
            down_("down", 2)
            pe.wait_ge(split, LOW_END["mem_2"])
            for m in range(2):
                weights(FIRST["mem_kv_2"] + m)
                for t in range(MT):
                    key = ("mem_kv_2", 2 * m + t)
                    claim(key)
                    done(key, token_tile(B(key)[:, 0:COLS], FIRST["mem_kv_2"] + m, t, mn2_hi, mn2_lo))
                    if m + t == 0:
                        norm_sum("down", S, (ssq, S), (ssq_mem, M))
                    if m == 0 and t == 1:
                        norm_spread("down")
            together("iq", FIRST["iq"], LOW_END["mem_2"], "x_2")
            norm_spread("x_2")

            def turn_heads(name, src, tokens):
                n["heads"] += 1
                pe.wait_ge(heads_norm, n["heads"])
                turns(name, 2, lambda f, t: src[:, t, f * P:(f + 1) * P], tokens // P)

            ld = FIRST["idx"]
            weights(ld)
            claim(("ik", 0))
            done(("ik", 0), feature_tile(B(("ik", 0)), ld, 0, *H))
            claim(("iwT", 0))
            for kt in range(KT):
                ins = product(B(("iwT", 0))[0:IDXH, :], w(ld, 1)[:, kt, P:P + IDXH], w(ld, 0)[:, kt, P:P + IDXH],
                              h_hi[:, kt, :], h_lo[:, kt, :], kt == 0, kt == KT - 1)
            done(("iwT", 0), ins)
            claim(("iw", 0))
            pe.wait_ge(bank_free[slot["iwT", 0].bank], turn(("iwT", 0)) + 1)
            for t in range(TT):
                ins = nc.tensor.transpose(B(("iw", 0))[:, t * IDXH:(t + 1) * IDXH],
                                          iwT[0:IDXH, t * P:(t + 1) * P], ident[0:IDXH, 0:IDXH])
            done(("iw", 0), ins)
            turn_heads("turn_km", km_tok, M)
            wait_all("iq", range(4))
            wait_all("ik", range(1))
            for w_, (i, h) in enumerate(IDX):
                claim(("idx", w_))
                done(("idx", w_), nc.tensor.matmul(B(("idx", w_))[:, 0:P * (i + 1)], iq[:, h // 2, i * P:(i + 1) * P],
                                                   ik[h % 2][:, 0:P * (i + 1)], start=True, stop=True))
            feature_loads("hf", 2)
            feature_loads("hq", 2)
            def load_tokens(name, ld):
                weights(ld)
                for t in range(TT):
                    claim((name, t))
                    done((name, t), token_tile(B((name, t))[:, 0:COLS], ld, t, h_hi, h_lo))

            def chunk(a, h, c):
                return a[:, h * S + c * P:h * S + (c + 1) * P]

            for lv in range(LEVELS):
                load_tokens(("sq", "sk", "sv", "mq", "hg0", "hg1", "hi0")[lv], FIRST["sq"] + lv)
                if lv == 0:
                    pe.wait_ge(hq_ready, 4)
                    for h in range(HG):
                        claim(("self", h))
                        for c in range(TT):
                            ins = nc.tensor.matmul(B(("self", h))[:, c * P:(c + 1) * P], chunk(kk, h, c),
                                                   chunk(qf, h, c), start=True, stop=True)
                        done(("self", h), ins)
                if lv in (1, 2, 4):
                    turn_heads({1: "turn_sq", 2: "turn_sk", 4: "turn_mq"}[lv], tok, S)
                pe.wait_ge(z_ready, lv + 1)
                for h in range(HG):
                    claim(("level", lv, h))
                    for c in range(TT):
                        ins = nc.tensor.matmul(B(("level", lv, h))[:, c * P:(c + 1) * P], chunk(z, h, c),
                                               chunk(z, h, c), start=True, stop=True)
                    done(("level", lv, h), ins)
            load_tokens("hi1", FIRST["hi"] + 1)
            pe.wait_ge(decayed, 1)
            turns("turn_kd", TT - 1, lambda c, h: chunk(kk, h, c), HG)
            for c in range(TT - 1):
                claim(("state", c))
                pe.wait_ge(bank_free[slot["turn_kd", c].bank], turn(("turn_kd", c)) + 1)
                for h in range(HG):
                    ins = nc.tensor.matmul(B(("state", c))[:, h * HDK:(h + 1) * HDK], kT[:, c, h, :],
                                           v_hg[:, c, h * HDK:(h + 1) * HDK], start=True, stop=True)
                done(("state", c), ins)
            for c in range(TT):
                claim(("o_hg", c))
                if c:
                    pe.wait_ge(state_ready, c)
                for h in range(HG):
                    o = B(("o_hg", c))[:, h * HDK:(h + 1) * HDK]
                    ins = nc.tensor.matmul(o, aT[:, h, c * P:(c + 1) * P], v_hg[:, c, h * HDK:(h + 1) * HDK],
                                           start=True, stop=c == 0)
                    if c:
                        ins = nc.tensor.matmul(o, chunk(qf, h, c), state[:, c - 1, h, :], start=False, stop=True)
                done(("o_hg", c), ins)
            attention("mem_2", SAH * TT,
                      lambda h, i, keys: (head64(mqT, h, i * P, (i + 1) * P), head64(kmT, h, 0, M)),
                      lambda h, c: vm[:, c, h * 64:(h + 1) * 64])
            attention("sa", SAH * TT,
                      lambda h, i, keys: (head64(sqT, h, i * P, (i + 1) * P), head64(skT, h, 0, keys)),
                      lambda h, c: sv[:, c, h * 64:(h + 1) * 64])
            all_read("sa", SAH * TT)
            turns("turn_mix", KT, lambda j, t: mix[:, t, j * P:(j + 1) * P], TT)
            feature_loads("w_out_2", 4, fresh=LOW_END["x_2"],
                          act=(lambda kt: mo_hi[:, kt, :], lambda kt: mo_lo[:, kt, :]))
            together("up_2_first", FIRST["up_2"], LOW_END["turn_mix"], "ffn_2")
            norm_spread("ffn_2")
            up("up_2")
            down_("down_2", FT + 2)


def branch(a, i, kt):
    return a[:, :, :].rearrange("p j t -> p (j t)")[:, bass.ds(4 * S * i + kt * S, S)]


def bucket_onehot():
    dist = np.arange(1024) - (S - 1)
    n = np.maximum(dist, NB_EXACT).astype(np.float32)
    large = NB_EXACT + (np.log(n / np.float32(NB_EXACT)) / np.float32(math.log(NB_DIST / NB_EXACT))
                        * np.float32(NB - NB_EXACT)).astype(np.int32)
    bucket = np.where(dist < NB_EXACT, dist, np.minimum(large, NB - 1))
    bucket = np.where(dist < 0, NB, bucket)
    return (bucket[None, :] == np.arange(NB + 1)[:, None]).astype(np.float32)


def level_masks():
    s, t = np.arange(P)[:, None], np.arange(P)[None, :]
    out = np.zeros((P, LEVELS + 1, P), np.int32)
    for lv in range(LEVELS):
        out[:, lv, :] = (s >> lv + 1 == t >> lv + 1) & (s >> lv & 1 == 0) & (t >> lv & 1 == 1)
    out[:, LEVELS, :] = s == t
    return out


def packed(w, cols=COLS, ktiles=KT):
    return w.reshape(ktiles, P, -1, cols).transpose(2, 1, 0, 3).reshape(-1, P, ktiles * cols)


def lay_out_weights(a):
    w_in, w_in2 = a["w_in"][0], a["w_in_2"][0]
    o = np.cumsum([0, 512, 512, 512, 512, 512, 512, 512, 1024, 1024, 1024])
    cb, cc, cv, q, k, v, qm, ga, gb, gc = (packed(w_in[:, o[j]:o[j + 1]]) for j in range(10))
    branches = []
    for g, w in ((ga, a["w_conv_out"]), (gb, a["w_attn_out"]), (gc, a["w_mem_out"])):
        w = packed(w[0], 512, 4)
        branches += [g[0:2], w[0:1], g[2:4], w[1:2]]

    def up(w):
        a_, g_ = packed(w[:, :DFF]), packed(w[:, DFF:])
        return np.stack([a_, g_], 1).reshape(2 * DFF // COLS, P, SLOT)

    def down(w):
        w = np.pad(w, ((0, 3 * 8 * P - DFF), (0, 0))).reshape(3, 8, P, 4, COLS)
        return w.transpose(3, 0, 2, 1, 4).reshape(12, P, SLOT)

    o = np.cumsum([0, 512, 512, 512, 512, 256, 256, 256, 512, 64, 8, 256])
    hq, hf, hi, hg, sq, sk, sv, iq, ik, iw, mq = (w_in2[:, o[j]:o[j + 1]] for j in range(11))
    idx = packed(np.pad(np.concatenate([ik, ik, iw], 1), ((0, 0), (0, COLS - 136))))
    parts = [packed(a["w_mem_kv"][0]), qm, v, q, k, cc, cv, cb, *branches, packed(a["w_out"][0]),
             up(a["w_up"][0]), down(a["w_down"][0]), packed(a["w_mem_kv_2"][0]), packed(iq), idx, packed(hf),
             packed(hq), packed(sq), packed(sk), packed(sv), packed(mq), packed(hg), packed(hi),
             packed(a["w_out_2"][0]), up(a["w_ffn_in_2"][0]), down(a["w_ffn_out_2"][0])]
    return np.ascontiguousarray(np.concatenate(parts, 0))


def columns(a):
    col = lambda x: x.reshape(-1, P).T
    names = ["g_pre_mix", "g_post_mix", "g_pre_ffn", "g_post_ffn", "g_mem", "norm_mix_2", "norm_mem_2",
             "norm_ffn_2", "b_gate", "conv_mix_w", "ffn_conv_w", "ffn_conv_b"]
    heads = [np.tile(a[x + "_2"].reshape(-1), 2)[:, None] for x in ("sa_q_gain", "mem_q_gain", "sa_k_gain",
                                                                    "mem_k_gain")]
    return np.ascontiguousarray(np.concatenate([col(a[x]) for x in names] + heads, 1))


def kernel(**inputs):
    import concourse.bacc as bacc
    from concourse.bass_utils import run_bass_kernel_spmd

    a = {name: np.asarray(value) for name, value in inputs.items()}
    gains = np.concatenate([a[x + "_2"].reshape(-1) for x in ROW])
    arrays = {
        "weights": lay_out_weights(a),
        "xT": np.ascontiguousarray(a["x"][0].T),
        "memT": np.ascontiguousarray(a["mem"][0].T),
        "mem2T": np.ascontiguousarray(a["mem_2"][0].T),
        "vec": columns(a),
        "rows": np.ascontiguousarray(np.broadcast_to(gains, (P, NROW))),
        "rel_bias": a["rel_bias"],
        "ident": np.eye(P, dtype=np.float32),
        "onehot": bucket_onehot(),
        "masks": level_masks(),
        "causal": np.where(np.arange(P)[None, :] <= np.arange(P)[:, None], 0, NEG).astype(np.float32),
    }
    nc = bacc.Bacc("TRN2", target_bir_lowering=False, num_devices=1)
    A = {name: nc.dram_tensor(name, value.shape, mybir.dt.from_np(value.dtype), kind="ExternalInput").ap()
         for name, value in arrays.items()}
    A["bias_scratch"] = nc.dram_tensor("bias_scratch", (HEADS, 1024), F32, kind="Internal").ap()
    out = nc.dram_tensor("outT", (D, S), F32, kind="ExternalOutput").ap()
    build(nc, A, out)
    r = run_bass_kernel_spmd(nc, [arrays], core_ids=[0])
    return np.ascontiguousarray(r.results[0]["outT"].T)[None]
```
